# Optimizing a Trainium2 kernel written in Bass

```python
import jax, jax.numpy as jnp
from jax import lax
import numpy as np

D_MODEL = 1024
BATCH = 1
SEQ = 256
DEPTH = 1
DEC_BATCH = 8
DEC_SEQ = 1
PAST_LEN = 2048
PAGE_SIZE = 128

HG_HEADS = 4
HG_DK = 128
HG_DV = 128
HG_WIDTH = HG_HEADS * HG_DK
HG_OUT = HG_HEADS * HG_DV
HG_CHUNK = 64
FOX_HEADS = 8
FOX_DH = 64
FOX_WIDTH = FOX_HEADS * FOX_DH
FOX_QBLOCK = 128
FOX_F_BIAS_INIT = 8.0
N_EXPERTS = 32
TOP_K = 4
D_FF = D_MODEL
SWIGLU_ALPHA = 1.702
SWIGLU_LIMIT = 7.0
MOE_BLOCK = 128
PLE_DIM = 256
NORM_EPS = 1e-6
IN_SPLITS = (HG_WIDTH, HG_WIDTH, HG_OUT, HG_OUT, FOX_WIDTH, FOX_WIDTH, FOX_WIDTH, FOX_HEADS)
IN_WIDTH = 2 * HG_WIDTH + 2 * HG_OUT + 3 * FOX_WIDTH + FOX_HEADS

kernel_name = 'hymba_hgrn2_fox_moe_decode_step'

def rmsnorm(x, g):
    xf = x.astype(jnp.float32)
    xf = xf * lax.rsqrt(jnp.mean(xf * xf, axis=-1, keepdims=True) + NORM_EPS)
    return (xf * g.astype(jnp.float32)).astype(x.dtype)

def head_rmsnorm(o, g):
    of = o.astype(jnp.float32)
    of = of * lax.rsqrt(jnp.mean(of * of, axis=-1, keepdims=True) + NORM_EPS)
    return of.reshape(*o.shape[:-2], o.shape[-2] * o.shape[-1]) * g.astype(jnp.float32)

def hgrn2_chunked(q, k, v, log_f, s0):
    B, T, H, Dk = q.shape
    Dv = v.shape[-1]
    C = HG_CHUNK if T % HG_CHUNK == 0 else T
    n = T // C

    def to_chunks(a):
        return a.reshape(B, n, C, H, a.shape[-1]).transpose(1, 0, 3, 2, 4)

    causal = jnp.tril(jnp.ones((C, C), bool))

    def step(S, inp):
        qc, kc, vc, gc = inp
        b = jnp.cumsum(gc, axis=2)
        o_inter = jnp.einsum('bhtk,bhkv->bhtv', qc * jnp.exp(b), S)
        diff = b[:, :, :, None, :] - b[:, :, None, :, :]
        decay = jnp.exp(jnp.where(causal[:, :, None], diff, -jnp.inf))
        A = jnp.einsum('bhtk,bhsk,bhtsk->bhts', qc, kc, decay)
        o_intra = jnp.einsum('bhts,bhsv->bhtv', A, vc)
        b_last = b[:, :, -1:, :]
        S_new = jnp.exp(b_last[:, :, 0, :, None]) * S + jnp.einsum('bhsk,bhsv->bhkv', kc * jnp.exp(b_last - b), vc)
        return S_new, o_inter + o_intra

    S_fin, o = lax.scan(step, s0, (to_chunks(q), to_chunks(k), to_chunks(v), to_chunks(log_f)))
    o = o.transpose(1, 0, 3, 2, 4).reshape(B, T, H, Dv)
    return o, S_fin

def fox_prompt_attn(q, k, v, logf):
    B, T, H, Dh = q.shape
    QB = FOX_QBLOCK if T % FOX_QBLOCK == 0 else T
    nq = T // QB
    scale = FOX_DH ** -0.5
    c = jnp.cumsum(logf, axis=1)
    c_keys = c.transpose(0, 2, 1)
    key_pos = jnp.arange(T)
    qb = q.reshape(B, nq, QB, H, Dh).transpose(1, 0, 2, 3, 4)
    cb = c.reshape(B, nq, QB, H).transpose(1, 0, 3, 2)

    def block(args):
        qi, ci, i = args
        s = jnp.einsum('bqhd,bkhd->bhqk', qi, k, preferred_element_type=jnp.float32) * scale
        s = s + ci[..., None] - c_keys[:, :, None, :]
        q_pos = i * QB + jnp.arange(QB)
        s = jnp.where(key_pos[None, :] <= q_pos[:, None], s, -jnp.inf)
        p = jax.nn.softmax(s, axis=-1)
        return jnp.einsum('bhqk,bkhd->bqhd', p.astype(v.dtype), v)

    o = lax.map(block, (qb, cb, jnp.arange(nq)))
    return o.transpose(1, 0, 2, 3, 4).reshape(B, T, H, Dh)

def fox_decode_attn(q, k, v, logf, k_past, v_past, lf_past):
    P = k_past.shape[1]
    T = q.shape[1]
    scale = FOX_DH ** -0.5
    c_new = jnp.cumsum(logf, axis=1).transpose(0, 2, 1)
    lf_p = lf_past.astype(jnp.float32)
    suffix = (lax.cumsum(lf_p, axis=1, reverse=True) - lf_p).transpose(0, 2, 1)
    s_past = jnp.einsum('bqhd,bkhd->bhqk', q, k_past, preferred_element_type=jnp.float32) * scale
    s_past = s_past + c_new[..., None] + suffix[:, :, None, :]
    s_new = jnp.einsum('bqhd,bkhd->bhqk', q, k, preferred_element_type=jnp.float32) * scale
    s_new = s_new + c_new[..., None] - c_new[:, :, None, :]
    causal = jnp.tril(jnp.ones((T, T), bool))
    s_new = jnp.where(causal, s_new, -jnp.inf)
    p = jax.nn.softmax(jnp.concatenate([s_past, s_new], axis=-1), axis=-1)
    o = jnp.einsum('bhqk,bkhd->bqhd', p[..., :P].astype(v_past.dtype), v_past)
    return o + jnp.einsum('bhqk,bkhd->bqhd', p[..., P:].astype(v.dtype), v)

def moe_ffn(u, w_router, b_router, w_up, b_up, w_down, b_down):
    shape = u.shape
    xt = u.reshape(-1, shape[-1])
    n_tok = xt.shape[0]
    logits = jnp.einsum('nd,de->ne', xt, w_router, preferred_element_type=jnp.float32) + b_router.astype(jnp.float32)
    top_val, top_idx = lax.top_k(logits, TOP_K)
    gates = jax.nn.softmax(top_val, axis=-1)
    n_assign = n_tok * TOP_K
    exp_flat = top_idx.reshape(-1).astype(jnp.int32)
    tok_flat = jnp.repeat(jnp.arange(n_tok, dtype=jnp.int32), TOP_K)
    gate_flat = gates.reshape(-1)
    order = jnp.argsort(exp_flat)
    e_s = exp_flat[order]
    t_s = tok_flat[order]
    g_s = gate_flat[order]
    counts = jnp.zeros((N_EXPERTS,), jnp.int32).at[exp_flat].add(1)
    padded = (counts + MOE_BLOCK - 1) // MOE_BLOCK * MOE_BLOCK
    start = jnp.cumsum(counts) - counts
    pend = jnp.cumsum(padded)
    pstart = pend - padded
    dest = pstart[e_s] + jnp.arange(n_assign, dtype=jnp.int32) - start[e_s]
    n_blocks = -(-n_assign // MOE_BLOCK) + N_EXPERTS
    cap = n_blocks * MOE_BLOCK
    buf_tok = jnp.full((cap,), n_tok, jnp.int32).at[dest].set(t_s)
    buf_gate = jnp.zeros((cap,), jnp.float32).at[dest].set(g_s)
    block_exp = jnp.minimum(jnp.searchsorted(pend, jnp.arange(n_blocks, dtype=jnp.int32) * MOE_BLOCK, side='right'), N_EXPERTS - 1).astype(jnp.int32)
    x_pad = jnp.concatenate([xt, jnp.zeros((1, xt.shape[1]), xt.dtype)], axis=0)
    xb = x_pad[buf_tok].reshape(n_blocks, MOE_BLOCK, xt.shape[1])

    def expert_block(args):
        xblk, e = args
        hdn = xblk @ w_up[e] + b_up[e]
        glu = jnp.minimum(hdn[:, :D_FF], SWIGLU_LIMIT)
        lin = jnp.clip(hdn[:, D_FF:], -SWIGLU_LIMIT, SWIGLU_LIMIT)
        act = glu * jax.nn.sigmoid(SWIGLU_ALPHA * glu) * (lin + 1.0)
        return act @ w_down[e] + b_down[e]

    yb = lax.map(expert_block, (xb, block_exp)).reshape(cap, xt.shape[1])
    y = jax.ops.segment_sum(yb * buf_gate[:, None].astype(yb.dtype), buf_tok, num_segments=n_tok + 1)[:n_tok]
    return y.reshape(shape)

def hybrid_layer(h, p_emb, s0, fox_past, lw):
    B, T, _ = h.shape
    u = rmsnorm(h, lw['g_mix'])
    proj = u @ lw['w_in']
    split_pts = np.cumsum(IN_SPLITS)[:-1].tolist()
    hq, hf, hi, hg, fq, fk, fv, ff = jnp.split(proj, split_pts, axis=-1)
    lb = lw['lb'].reshape(HG_HEADS, HG_DK)
    q_h = jax.nn.silu(hq.astype(jnp.float32)).reshape(B, T, HG_HEADS, HG_DK)
    f_h = lb + (1.0 - lb) * jax.nn.sigmoid(hf.astype(jnp.float32).reshape(B, T, HG_HEADS, HG_DK))
    k_h = 1.0 - f_h
    v_h = hi.astype(jnp.float32).reshape(B, T, HG_HEADS, HG_DV)
    o_h, s_new = hgrn2_chunked(q_h, k_h, v_h, jnp.log(f_h), s0.astype(jnp.float32))
    o_h = head_rmsnorm(o_h, lw['g_hg_out']) * jax.nn.silu(hg.astype(jnp.float32))
    q_f = fq.reshape(B, T, FOX_HEADS, FOX_DH)
    k_f = fk.reshape(B, T, FOX_HEADS, FOX_DH)
    v_f = fv.reshape(B, T, FOX_HEADS, FOX_DH)
    logf = jax.nn.log_sigmoid(ff.astype(jnp.float32) + lw['fox_f_bias'].astype(jnp.float32))
    if fox_past is None:
        o_f = fox_prompt_attn(q_f, k_f, v_f, logf)
    else:
        k_past, v_past, lf_past = fox_past
        o_f = fox_decode_attn(q_f, k_f, v_f, logf, k_past, v_past, lf_past)
    o_f = head_rmsnorm(o_f, lw['g_fox_out'])
    mix = jnp.concatenate([o_h, o_f], axis=-1).astype(h.dtype) @ lw['w_out']
    h = h + mix
    h = h + moe_ffn(rmsnorm(h, lw['g_mlp']), lw['w_router'], lw['b_router'], lw['w_up'], lw['b_up'], lw['w_down'], lw['b_down'])
    h = h + jax.nn.sigmoid(h @ lw['w_ple_gate']) * (p_emb.astype(h.dtype) @ lw['w_ple'])
    return h, s_new.astype(s0.dtype), k_f, v_f, logf

def setup_inputs(seed: int = 0) -> dict:
    key = jax.random.key(seed)
    ks = jax.random.split(key, 26)
    n_pages = PAST_LEN // PAGE_SIZE
    n_used = DEC_BATCH * n_pages
    n_phys = n_used + n_used // 4
    f32 = jnp.float32
    nrm = lambda k, s: jax.random.normal(k, s, f32)
    return {
        'x_prompt': nrm(ks[0], (BATCH, SEQ, D_MODEL)),
        'x_sample': nrm(ks[1], (DEC_BATCH, DEC_SEQ, D_MODEL)),
        'state_hgrn': 0.5 * nrm(ks[2], (DEPTH, DEC_BATCH, HG_HEADS, HG_DK, HG_DV)),
        'cache_k': nrm(ks[3], (DEPTH, n_phys, PAGE_SIZE, FOX_HEADS, FOX_DH)),
        'cache_v': nrm(ks[4], (DEPTH, n_phys, PAGE_SIZE, FOX_HEADS, FOX_DH)),
        'cache_logf': jax.nn.log_sigmoid(FOX_F_BIAS_INIT + nrm(ks[5], (DEPTH, n_phys, PAGE_SIZE, FOX_HEADS))),
        'page_table': jax.random.permutation(ks[6], n_phys)[:n_used].reshape(DEC_BATCH, n_pages).astype(jnp.int32),
        'p_prompt': nrm(ks[7], (DEPTH, BATCH, SEQ, PLE_DIM)),
        'p_sample': nrm(ks[8], (DEPTH, DEC_BATCH, DEC_SEQ, PLE_DIM)),
        'g_mix': 1.0 + 0.05 * nrm(ks[9], (DEPTH, D_MODEL)),
        'w_in': nrm(ks[10], (DEPTH, D_MODEL, IN_WIDTH)) * D_MODEL ** -0.5,
        'hg_lb_logits': 0.1 * nrm(ks[11], (DEPTH + 1, HG_WIDTH)),
        'g_hg_out': 1.0 + 0.05 * nrm(ks[12], (DEPTH, HG_OUT)),
        'fox_f_bias': FOX_F_BIAS_INIT + 0.1 * nrm(ks[13], (DEPTH, FOX_HEADS)),
        'g_fox_out': 1.0 + 0.05 * nrm(ks[14], (DEPTH, FOX_WIDTH)),
        'w_out': nrm(ks[15], (DEPTH, D_MODEL, D_MODEL)) * D_MODEL ** -0.5,
        'g_mlp': 1.0 + 0.05 * nrm(ks[16], (DEPTH, D_MODEL)),
        'w_router': nrm(ks[17], (DEPTH, D_MODEL, N_EXPERTS)) * D_MODEL ** -0.5,
        'b_router': 0.01 * nrm(ks[18], (DEPTH, N_EXPERTS)),
        'w_up': nrm(ks[19], (DEPTH, N_EXPERTS, D_MODEL, 2 * D_FF)) * D_MODEL ** -0.5,
        'b_up': 0.01 * nrm(ks[20], (DEPTH, N_EXPERTS, 2 * D_FF)),
        'w_down': nrm(ks[21], (DEPTH, N_EXPERTS, D_FF, D_MODEL)) * D_FF ** -0.5,
        'b_down': 0.01 * nrm(ks[22], (DEPTH, N_EXPERTS, D_MODEL)),
        'w_ple': nrm(ks[23], (DEPTH, PLE_DIM, D_MODEL)) * PLE_DIM ** -0.5,
        'w_ple_gate': nrm(ks[24], (DEPTH, D_MODEL, D_MODEL)) * D_MODEL ** -0.5,
        'g_final': 1.0 + 0.05 * nrm(ks[25], (D_MODEL,)),
    }

def reference(x_prompt, x_sample, state_hgrn, cache_k, cache_v, cache_logf, page_table, p_prompt, p_sample,
              g_mix, w_in, hg_lb_logits, g_hg_out, fox_f_bias, g_fox_out, w_out, g_mlp, w_router, b_router,
              w_up, b_up, w_down, b_down, w_ple, w_ple_gate, g_final):
    dec_b, n_pages = page_table.shape
    past = n_pages * PAGE_SIZE
    lb_all = jnp.cumsum(jax.nn.softmax(hg_lb_logits.astype(jnp.float32), axis=0), axis=0)
    hp, hs = x_prompt, x_sample
    sp_l, kp_l, vp_l, lp_l, ss_l, ks_l, vs_l, ls_l = [], [], [], [], [], [], [], []
    for i in range(DEPTH):
        lw = dict(g_mix=g_mix[i], w_in=w_in[i], lb=lb_all[i], g_hg_out=g_hg_out[i], fox_f_bias=fox_f_bias[i],
                  g_fox_out=g_fox_out[i], w_out=w_out[i], g_mlp=g_mlp[i], w_router=w_router[i],
                  b_router=b_router[i], w_up=w_up[i], b_up=b_up[i], w_down=w_down[i], b_down=b_down[i],
                  w_ple=w_ple[i], w_ple_gate=w_ple_gate[i])
        s0p = jnp.zeros((x_prompt.shape[0], HG_HEADS, HG_DK, HG_DV), state_hgrn.dtype)
        hp, sp, kp, vp, lp = hybrid_layer(hp, p_prompt[i], s0p, None, lw)
        k_past = cache_k[i, page_table].reshape(dec_b, past, FOX_HEADS, FOX_DH)
        v_past = cache_v[i, page_table].reshape(dec_b, past, FOX_HEADS, FOX_DH)
        lf_past = cache_logf[i, page_table].reshape(dec_b, past, FOX_HEADS)
        hs, ss, ks_, vs, ls = hybrid_layer(hs, p_sample[i], state_hgrn[i], (k_past, v_past, lf_past), lw)
        sp_l.append(sp); kp_l.append(kp); vp_l.append(vp); lp_l.append(lp)
        ss_l.append(ss); ks_l.append(ks_); vs_l.append(vs); ls_l.append(ls)
    y_prompt = rmsnorm(hp, g_final)
    y_sample = rmsnorm(hs, g_final)
    return (y_prompt, y_sample, jnp.stack(sp_l), jnp.stack(kp_l), jnp.stack(vp_l), jnp.stack(lp_l),
            jnp.stack(ss_l), jnp.stack(ks_l), jnp.stack(vs_l), jnp.stack(ls_l))


_drawn_inputs = setup_inputs


def setup_inputs(seed=0):
    import zlib

    import numpy as np

    out = dict(_drawn_inputs(seed))
    spreads = {}
    factors = {'cache_logf': 8.0, 'b_up': 8.0, 'b_down': 8.0}
    for name, (base, spread) in spreads.items():
        noise = np.random.default_rng([zlib.crc32(name.encode()), seed]).standard_normal(out[name].shape)
        drawn = base * np.exp(spread * noise) if base else spread * noise
        out[name] = __import__('jax').numpy.asarray(drawn.astype(out[name].dtype))
    for name, factor in factors.items():
        out[name] = (out[name] * factor).astype(out[name].dtype)
    return out
```

```python
from contextlib import ExitStack, contextmanager

import concourse.bass as bass
from concourse import mybir

F32 = mybir.dt.float32
BF16 = mybir.dt.bfloat16
I32 = mybir.dt.int32
U32 = mybir.dt.uint32
ALU = mybir.AluOpType
ACT = mybir.ActivationFunctionType
AX = mybir.AxisListType
ds = bass.ds

P = 128
EPS = 1e-6
NEG = -1.0e30
TOPK = 4
LIMIT = 7.0


class Chain:

    def __init__(self, eng, sem):
        self.eng, self.sem, self.n, self.off = eng, sem, 0, 0

    def __call__(self, ins):
        self.n += 1
        ins.then_inc(self.sem, 1)
        self.eng.wait_ge(self.sem, self.off + self.n)


def hybrid_layer_kernel(nc, x_prompt, x_sample, state_hgrn, cache_k, cache_v, cache_logf, page_table,
                        p_prompt, p_sample, g_mix, w_in, hg_lb_logits, g_hg_out, fox_f_bias, g_fox_out,
                        w_out, g_mlp, w_router, b_router, w_up, b_up, w_down, b_down, w_ple, w_ple_gate,
                        g_final, y_p, y_s, st_p, k_p, v_p, lf_p, st_s, k_s, v_s, lf_s, SLOTS=64):
    D = x_prompt.shape[2]
    T = x_prompt.shape[1]
    B = x_sample.shape[0]
    NT = T + B
    KC = D // P
    NTILE = T // P
    TILES = [(i * P, P) for i in range(NTILE)] + [(T, B)]
    HH, DK = state_hgrn.shape[2], state_hgrn.shape[3]
    FH, DH = cache_k.shape[3], cache_k.shape[4]
    FW = FH * DH
    NPG = page_table.shape[1]
    NPAGE = B * NPG
    E = w_up.shape[1]
    PLE = w_ple.shape[1]
    SCALE = float(DH) ** -0.5
    CH = 32
    NCH = T // CH
    NB = w_in.shape[2] // 512
    FC = FW // P
    HQ, HF, HI, HG, FQ, FK, FV = (4 * j for j in range(7))
    ORDER = [4, 5, 6, 1, 2, 0, 3]
    RING = 12
    CK = 4
    CPG = NPG // CK
    assert D == 1024 and T == 256 and B == 8 and FW == 512 and DK == P and NB == 7 and NPAGE == P

    with ExitStack() as ctx:
        def sb(name, shape, dt=F32):
            return ctx.enter_context(nc.sbuf_tensor(name, shape, dt))

        def sem(name):
            return ctx.enter_context(nc.semaphore(name))

        PS = [ctx.enter_context(nc.psum_tensor(f"bank{i}", [P, 512], F32)) for i in range(8)]

        ring = sb("ring", [P, RING, 2048])
        xT = sb("xT", [P, KC, NT])
        uT = sb("uT", [P, KC, NT])
        PT = sb("PT", [P, 28, NT])
        XN = sb("XN", [P, 3, D])
        hin = sb("hin", [P, 3, 512])
        arena = sb("arena", [P, 6400])

        ident = sb("ident", [P, P])
        ones = sb("ones", [P, P])
        pair_ones = sb("pair_ones", [P, P])
        hmask = sb("hmask", [P, P])
        cmask = sb("cmask", [P, P])
        tri_after = sb("tri_after", [P, P])
        tri_before = sb("tri_before", [P, P])
        later = sb("later", [P, P])
        slot_no = sb("slot_no", [P, P])
        reset = sb("reset", [P, T])
        ofmask = arena[:, 5888:6400].rearrange("p (h d) -> p h d", h=FH)
        hsel = arena[:, 4864:5376].rearrange("p (c r h) -> p c r h", c=FC, h=FH)
        negsel = sb("negsel", [B, FH, P])
        gcols = sb("gcols", [P, 40])
        small = sb("small", [P, 256])
        sq = sb("sq", [P, 2, NT])
        rt = sb("rt", [P, 2, NT])
        rstd = sb("rstd", [P, NT])
        snew = sb("snew", [P, B])
        page_i = sb("page_i", [1, NPAGE], I32)
        page_c = sb("page_c", [P, 1], I32)
        cnat = sb("cnat", [P, 2, FH])

        GMIX, GMLP, GFIN, GHG, GFOX, LB0, LB1 = 0, 8, 16, 24, 28, 32, 36
        eps = small[:, 0:1]
        lb = small[:, 4:8]
        oml = small[:, 8:12]
        lbt = small[:, 12:24].rearrange("p (a b) -> p a b", b=4)
        ffb = small[0:FH, 24:25]
        rb = small[0:E, 25:26]
        lfn = small[:, 32:56].rearrange("p (i h) -> p i h", i=3)

        sems = {}

        def S(name):
            if name not in sems:
                sems[name] = sem(name)
            return sems[name]

        STAGES = {
            "pe_stage": ["g_ready", "ff_mm", "qnat_mm", "lfn_mm", "st_o", "snew_mm", "lgT_mm", "lg_mm", "rk_mm", "tot_mm"],
            "act_stage": ["lb_exp", "ff_exp", "ff_ln", "hf_sig", "st_o_ev", "snew_ok", "lgT_ok", "gT_ok"],
            "dve_stage": ["lb_in", "ff_na", "ff_w", "lf_one", "lfT_ok", "fkv_nat", "q_nat", "lf_nat", "qk_new", "f_ok", "lnew_cp", "tot_ok", "list_ok", "stz_zero", "moe_done"],
        }
        AT = {name: k + 1 for names in STAGES.values() for k, name in enumerate(names)}
        told = {stage: 0 for stage in STAGES}

        def once(stage, name):
            told[stage] += 1
            assert STAGES[stage][told[stage] - 1] == name, name
            return 1

        dchain, achain, gchain = S("dve_chain"), S("act_chain"), S("pool_chain")

        def av(a, n):
            return arena[:, a:a + n]
        lnf, bb, bc, b2, e1, e2, e3, e4, qe, kd, qi, ko, ats, kn = (av(256 * i, 256) for i in range(14))
        St = av(3584, 1152).rearrange("p (c v) -> p c v", v=P)
        kT = av(4736, 1056).rearrange("p (h t) -> p h t", h=HH)
        sfin = av(5800, 512).rearrange("p (h v) -> p h v", h=HH)
        tmp4 = av(0, 1056).rearrange("p (h t) -> p h t", h=HH)
        zz, pp, ptr = av(0, 512), av(512, 384), av(1024, 384)
        prod = av(0, 2048)
        Lrow = av(0, 2048).rearrange("p (h two g) -> p h two g", h=FH, two=2)
        LF = av(2048, 1024)
        SF = av(3072, 1024).rearrange("p (h g) -> p h g", h=FH)
        sc, z = av(4096, 128), av(4224, 128)
        P32 = av(4352, 512).rearrange("p (g r h) -> p g r h", g=NPG, r=4)
        of = av(5376, 512)
        of2 = prod[:, 0:512]
        stt = ring[:, 10:12, :].rearrange("p a (b h v) -> p (a b) h v", h=HH, v=P)
        fkn, fvn = XN[:, :, 0:512], XN[:, :, 512:1024]
        qnat = sb("qnat", [B, 512])
        PTf = PT[:, :, :].rearrange("p a b -> p (a b)")
        qm, vm = PTf[0:B, 0:512], PTf[0:B, 512:1024]
        dec = sb("dec", [P, 304])
        mrep, lrep = dec[:, 0:128], dec[:, 128:256]
        mx, dmx, lsum = dec[:, 256:264], dec[:, 264:272], dec[:, 272:280]
        mcol, pnew, ltot, rl, pnr = (dec[:, 280 + i:281 + i] for i in range(5))
        qkn = small[:, 64:96].rearrange("p (c b) -> p c b", c=4)
        mcol_neg = dec[:, 286:287]
        lfT = sb("lfT", [FH, NT])
        cT8 = sb("cT8", [FH, T])
        fft = arena[0:FH, 0:4 * NT].rearrange("p (i t) -> p i t", i=4)
        lnewv = PTf[0:B, 4 * NT:4 * NT + FH * NPAGE].rearrange("p (h g) -> p h g", h=FH)

        def zrep(z):
            return z.rearrange("p (g h) -> p g h", h=FH).unsqueeze(2).broadcast_to([P, NPG, 4, FH])

        def mixc(c):
            return HI + c if c < HH else FQ + c - HH

        def wslot(n):
            return (n % 6) * 2

        def wview(n):
            return ring[:, wslot(n):wslot(n) + 2, :].rearrange("p a (c n) -> p (a c) n", n=512)

        wff = hin[:, 2, 0:KC * FH].rearrange("p (c n) -> p c n", n=FH)
        wout = ring[:, 8:12, :].rearrange("p a (c n) -> p (a c) n", n=D)

        PTf = PT[:, :, :].rearrange("p a b -> p (a b)")
        UB = PTf[:, 0:4608].bitcast(BF16).rearrange("p (s i d) -> p s i d", s=3, i=3)
        XTe = PTf[:, 4608:5632].rearrange("p (u n) -> p u n", u=2)
        RG = PTf[:, 5632:5824].rearrange("p (e r) -> p e r", r=6)
        lg = PTf[:, 5824:5920].rearrange("p (i e) -> p i e", i=3)
        gate = PTf[:, 5920:6016].rearrange("p (i e) -> p i e", i=3)
        selm = PTf[:, 6016:6112].rearrange("p (i e) -> p i e", i=3)
        rk = PTf[:, 6112:6208].rearrange("p (i e) -> p i e", i=3)
        m8neg = PTf[:, 6232:6235]
        m8 = PTf[:, 6208:6232].rearrange("p (i e) -> p i e", i=3)
        rt4 = PTf[:, 6240:6368].rearrange("p (i e) -> p i e", i=4)
        cnt = PTf[:, 6368:6384]
        lgT = PTf[:, 6400:6664]
        gT = PTf[:, 6664:6928]
        cur = PTf[:, 6928:6940].rearrange("p (u r) -> p u r", u=2)
        first_rank = PTf[:, 6940:6941]
        sel32 = PTf[:, 6944:7072].rearrange("p (u r) -> p u r", u=2)
        XMAX = NT * TOPK // SLOTS
        NBLK = (NT - 1) // SLOTS
        flag, pos, hit = (hin[0:XMAX, k, 0:E * NBLK] for k in range(3))
        codes = sq[0:XMAX, :, :].rearrange("p a b -> p (a b)")[:, 0:2 * E * NBLK]
        found = dec[0:XMAX, 0:3]
        dgl = dec[0:XMAX, 8:8 + 2 * XMAX + 1]
        xlist = dec[:, 128:128 + 2 * XMAX + 1]
        xint = small[0:1, 128:128 + XMAX + 1].bitcast(I32)
        order_no = small[:, 112:113]
        a1, a2, a3, AT2, YG = (av(512 * i, 512) for i in range(5))
        STz = av(2560, 4 * NT).rearrange("p (u d t) -> p u d t", u=2, d=2)
        SG = av(4672, 768).rearrange("p (u i s) -> p u i s", u=2, i=3)
        SB = av(5440, 192).bitcast(BF16).rearrange("p (u i s) -> p u i s", u=2, i=3)
        bup = uT[:, :, :].rearrange("p a b -> p (a b)")[0:E, 0:2048]
        pwT = XN[:, :, :].rearrange("p a b -> p (a b)")[:, 0:KC * NT].rearrange("p (c t) -> p c t", c=KC)
        unat = ring[:, 0:2, :].rearrange("p a b -> p (a b)")[:, 0:3 * D].rearrange("p (i d) -> p i d", i=3)
        wrt = ring[:, 2, 0:KC * E].rearrange("p (c e) -> p c e", e=E)
        bdn = ring[0:E, 2, 1024:2048]
        ures = ring[:, 3:5, :].rearrange("p a b -> p (a b)")[:, 0:3 * D].rearrange("p (i d) -> p i d", i=3)
        wple = ring[:, 5, :].rearrange("p (c n) -> p c n", n=D)
        pnat = ring[:, 6, 0:3 * PLE].rearrange("p (i d) -> p i d", i=3)
        pT = ring[:, 6, 1024:1024 + 2 * NT].rearrange("p (c t) -> p c t", c=2)
        wgate = ring[:, 0:4, :].rearrange("p a (c n) -> p (a c) n", n=D)
        sgT = PTf[:, 0:KC * NT].rearrange("p (c t) -> p c t", c=KC)
        yout = PTf[:, 2112:2112 + 3 * D].rearrange("p (i d) -> p i d", i=3)

        w_in_c = w_in[0].rearrange("(c p) n -> p c n", p=P)
        wo_c = w_out[0].rearrange("(c p) n -> p c n", p=P)
        wg_c = w_ple_gate[0].rearrange("(c p) n -> p c n", p=P)
        PAIRS = E // 2

        @contextmanager
        def further(eng):
            eng.wait_ge(S("dve_stage"), AT["list_ok"])
            count = eng.value_load(xint[0:1, 0:1], min_val=0, max_val=XMAX)
            with eng.If(count > 0):
                with eng.Fori(0, count) as x:
                    yield x

        block = ctx.enter_context(nc.Block())

        @block.sync
        def _(sp):
            def load(dst, src, s, k=16):
                sp.dma_start(dst, src).then_inc(S(s), k)

            load(XN[:, 0:2, :], x_prompt[0].rearrange("(i p) d -> p i d", p=P), "x_in")
            load(XN[0:B, 2, :], x_sample[:, 0, :], "x_in")
            for r, v in ((GMIX, g_mix[0]), (GMLP, g_mlp[0]), (GFIN, g_final), (GHG, g_hg_out[0]), (GFOX, g_fox_out[0]),
                         (LB0, hg_lb_logits[0]), (LB1, hg_lb_logits[1])):
                n = v.shape[0] // P
                load(hin[r:r + n, 0, 0:P], v.rearrange("(c p) -> c p", p=P), "rows_in")
            load(ffb, fox_f_bias.rearrange("a h -> h a"), "rows_in")
            load(rb, b_router.rearrange("a h -> h a"), "rows_in")
            load(page_i[:, :], page_table.rearrange("b g -> (b g)").rearrange("(a n) -> a n", a=1), "page_in")
            load(page_c[:, :], page_table.rearrange("b g -> (b g)").rearrange("(n a) -> n a", a=1), "page_in")
            for n in range(6):
                load(wview(n), w_in_c[:, :, 512 * ORDER[n]:512 * ORDER[n] + 512], f"w_in{n}")
            load(wff, w_in_c[:, :, NB * 512:NB * 512 + FH], "wff_in")
            sp.wait_ge(S("pt_mm"), 4)
            load(wview(6), w_in_c[:, :, 512 * ORDER[6]:512 * ORDER[6] + 512], "w_in6")
            sp.wait_ge(S("pt_mm"), 24)
            load(stt, state_hgrn[0].rearrange("b h k v -> k b h v"), "st_in")
            sp.wait_ge(S("dve_stage"), AT["fkv_nat"])
            load(k_p[0, 0].rearrange("(i p) h d -> p i (h d)", p=P), fkn[:, 0:2, :], "out")
            load(k_s[0, :, 0].rearrange("b h d -> b (h d)"), fkn[0:B, 2, :], "out")
            load(v_p[0, 0].rearrange("(i p) h d -> p i (h d)", p=P), fvn[:, 0:2, :], "out")
            load(v_s[0, :, 0].rearrange("b h d -> b (h d)"), fvn[0:B, 2, :], "out")
            sp.wait_ge(S("dve_stage"), AT["lf_nat"])
            load(lf_p[0, 0].rearrange("(i p) h -> p i h", p=P), lfn[:, 0:2, :], "out")
            load(lf_s[0, :, 0], lfn[0:B, 2, :], "out")
            sp.wait_ge(S("pt_mm"), 28)
            sp.wait_ge(S("page_in"), 32)

            def pages(cache, slot0, b, land):
                for c in range(CK):
                    for g in range(CPG):
                        r = sp.value_load(page_i[0:1, ds(b * NPG + c * CPG + g, 1)], min_val=0,
                                          max_val=cache_k.shape[1] - 1)
                        if g == 0 and not (isinstance(b, int) and b == 0):
                            sp.wait_ge(S(land + "_used"), CK * b + c - CK + 1)
                        sp.dma_start(ring[:, slot0 + c, 512 * g:512 * g + 512],
                                     cache[0][ds(r, 1)].rearrange("a r h d -> r (a h d)")).then_inc(S(f"{land}{c}"), 16)

            def seq(b):
                pages(cache_k, 0, b, "k_land")
                pages(cache_v, CK, b, "v_land")

            seq(0)
            with sp.Fori(1, B) as b:
                seq(b)
            sp.wait_ge(S("k_land_used"), CK * B)
            sp.wait_ge(S("v_land_used"), CK * B)
            load(wrt, w_router[0].rearrange("(c p) e -> p c e", p=P), "wr_in")
            load(bdn, b_down[0], "wr_in")
            load(wple, w_ple[0].rearrange("(c p) n -> p c n", p=P), "wple_in")
            load(pnat[:, 0:2, :], p_prompt[0, 0].rearrange("(i p) d -> p i d", p=P), "wple_in")
            load(pnat[0:B, 2, :], p_sample[0, :, 0, :], "wple_in")
            sp.wait_ge(S("un_mm"), 6)
            sp.wait_ge(S("pe_stage"), AT["lgT_mm"])
            load(bup, b_up[0], "bup_in")

            def expert(src_e, n, first, s):
                if not first:
                    sp.wait_ge(S("w_used"), 12 * n + s - 11)
                if s < 8:
                    src = w_up[0][ds(src_e, 1)].rearrange("a (c p) n -> p (a c) n", p=P)[:, s, :]
                    sp.dma_start(ring[:, s, :], src).then_inc(S(f"w_land{s}"), 16)
                else:
                    j = s - 8
                    src = w_down[0][ds(src_e, 1)].rearrange("a (c p) n -> p (a c) n", p=P)[:, 2 * j:2 * j + 2, :]
                    sp.dma_start(ring[:, s, :].rearrange("p (c n) -> p c n", c=2), src)\
                      .then_inc(S(f"w_land{s}"), 16)

            sp.wait_ge(S("h_mm"), KC)
            for s in (7, 8, 9, 10, 11):
                expert(0, 0, True, s)
            sp.wait_ge(S("bd_mm"), KC)
            sp.wait_ge(S("pw_mm"), KC)
            for s in range(7):
                expert(0, 0, True, s)
            with sp.Fori(1, E) as e:
                for s in range(RING):
                    expert(e, e, False, s)
            with further(sp) as x:
                e = sp.value_load(xint[0:1, ds(x + 1, 1)], min_val=0, max_val=E - 1)
                for s in range(RING):
                    expert(e, E + x, False, s)
            sp.wait_ge(S("dve_stage"), AT["moe_done"])
            load(wgate, wg_c, "wg_in")
            sp.wait_ge(S("yo_lo"), 3)
            sp.wait_ge(S("yo_hi"), 3)
            load(y_p[0].rearrange("(i p) d -> p i d", p=P), yout[:, 0:2, :], "out")
            load(y_s[:, 0, :], yout[0:B, 2, :], "out")
            sp.wait_ge(S("out"), 16 * 8)

        @block.gpsimd
        def _(gp):
            g = Chain(gp, gchain)

            def fill(t, v):
                g(gp.memset(t, v))

            def keep(t, base, cm, pattern, op=ALU.is_ge, fillv=0.0):
                g(gp.affine_select(out=t, in_=t, compare_op=op, fill=fillv, base=base, pattern=pattern,
                                   channel_multiplier=cm))

            fill(eps, EPS)
            fill(ident[:, :], 0.0)
            keep(ident[:, :], 0, 1, [[-1, P]], ALU.not_equal, 1.0)
            fill(ones[:, :], 1.0)
            gp.nop().then_inc(S("const_a"), 1)
            po = pair_ones[:, :].rearrange("p (a b) -> p a b", a=2)
            fill(po, 1.0)
            keep(po, 0, 1, [[-DH, 2], [0, DH]])
            keep(po, DH - 1, -1, [[DH, 2], [0, DH]])
            fill(hmask[:, :], 1.0)
            hm = hmask[:, :].rearrange("p (a b) -> p a b", b=CH)
            keep(hm, 0, 1, [[-CH, P // CH], [0, CH]])
            keep(hm, 0, -1, [[CH, P // CH], [1, CH]])
            fill(cmask[:, :], 0.0)
            keep(cmask[:, :], 0, 1, [[-1, P]], ALU.is_ge, NEG)
            fill(tri_after[:, :], 1.0)
            keep(tri_after[:, :], -1, 1, [[-1, P]])
            fill(tri_before[:, :], 1.0)
            keep(tri_before[:, :], -1, -1, [[1, P]])
            fill(later[:, :], 1.0)
            lt = later[:, :].rearrange("p (a b) -> p a b", b=NPG)
            keep(lt, -1, 1, [[-NPG, B], [-1, NPG]])
            keep(lt, NPG - 1, -1, [[NPG, B], [0, NPG]])
            fill(negsel[:, :, :], 0.0)
            keep(negsel[:, :, :], 0, 1, [[-1, FH], [0, P]], ALU.not_equal, -1.0)
            fill(reset[:, :], 1.0)
            fill(reset[:, :].rearrange("p (c r) -> p c r", r=CH)[:, :, 0:1], 0.0)
            g(gp.iota(slot_no[:, :], [[0, P // 64], [1, 64]], base=0, channel_multiplier=0,
                      allow_small_or_imprecise_dtypes=True))
            if SLOTS < 64:
                fill(slot_no[:, :].rearrange("p (a b) -> p a b", a=2)[:, :, SLOTS:64], -1.0e4)
            g(gp.iota(order_no, [[0, 1]], base=1, channel_multiplier=1, allow_small_or_imprecise_dtypes=True))
            gp.nop().then_inc(S("const_b"), 1)
            gp.wait_ge(S("sfin_ok"), HH)
            gp.dma_start(st_p[0, 0].rearrange("h k v -> k h v"), sfin).then_inc(S("sfin_out"), 16)
            gp.wait_ge(S("st_new"), B)
            gp.dma_start(st_s[0].rearrange("b h k v -> k b h v"), stt).then_inc(S("st_out"), 16)
            gp.wait_ge(S("pe_stage"), AT["st_o"])
            gp.wait_ge(S("st_out"), 16)
            gp.wait_ge(S("pt_mm"), 28)
            gp.dma_start(wout, wo_c).then_inc(S("w_out"), 16)
            gp.wait_ge(S("dve_stage"), AT["lnew_cp"])
            lv = lnewv.rearrange("p h (b g) -> p h b g", b=B)
            keep(lv, 0, 1, [[0, FH], [-1, B], [0, NPG]], ALU.is_equal, 0.0)
            gp.nop().then_inc(S("lnew_ok"), 1)
            gp.wait_ge(S("sfin_out"), 16)
            gp.wait_ge(S("vb_used"), B)
            fill(ofmask, 0.0)
            for q in range(4):
                keep(ofmask, -CH * q, 1, [[-1, FH], [0, DH]], ALU.not_equal, 1.0)
            fill(hsel, 1.0)
            keep(hsel, 0, 1, [[P, FC], [0, 16], [-DH, FH]])
            keep(hsel, DH - 1, -1, [[-P, FC], [0, 16], [DH, FH]])
            gp.nop().then_inc(S("const_c"), 1)
            gp.wait_ge(S("page_in"), 32)
            gp.indirect_dma_start(
                LF, None, cache_logf[0].rearrange("n r h -> n (r h)"),
                bass.IndirectOffsetOnAxis(ap=page_c[:, :].bitcast(U32), axis=0)).then_inc(S("lf_past"), 16)
            gp.wait_ge(S("u_ready"), 2 * KC)
            c4 = codes.rearrange("p (w b e) -> p w b e", w=2, e=E)
            g(gp.iota(c4[:, 0], [[0, NBLK], [1, E]], base=0, channel_multiplier=0,
                      allow_small_or_imprecise_dtypes=True))
            g(gp.iota(c4[:, 1], [[SLOTS, NBLK], [0, E]], base=SLOTS, channel_multiplier=0,
                      allow_small_or_imprecise_dtypes=True))
            gp.nop().then_inc(S("codes_ok"), 1)

        @block.tensor
        def _(pe):
            mm, tr = pe.matmul, pe.transpose

            def rms_sum(k, n=KC, lhs=None, per=1):
                for c in range(n):
                    pe.wait_ge(S("sq_ready"), k + c + 1)
                    mm(PS[4][:, 0:NT], ones[:, :], sq[:, (k + c) % 2, :], start=c == 0, stop=c == n - 1)\
                        .then_inc(S("sq_used"), 1)

            pe.wait_ge(S("const_a"), 1)
            pe.wait_ge(S("rows_in"), 16 * 9)
            tr(PS[7][:, 0:40], hin[0:40, 0, 0:P], ident[0:40, 0:40]).then_inc(S("pe_stage"), once("pe_stage", "g_ready"))
            pe.wait_ge(S("x_in"), 32)
            for c in range(KC):
                if c >= 4:
                    pe.wait_ge(S("xt_ev"), c - 3)
                for i, (t0, n) in enumerate(TILES):
                    m = tr(PS[c % 4][:, t0:t0 + n], XN[0:n, i, c * P:(c + 1) * P], ident[0:n, 0:n])
                m.then_inc(S("xt_mm"), 1)
            rms_sum(0)
            pe.wait_ge(S("u_ready"), KC)
            pe.wait_ge(S("xt_ev"), KC)
            for n, j in enumerate(ORDER):
                pe.wait_ge(S(f"w_in{n}"), 16)
                for m in range(4):
                    q = 4 * n + m
                    if q >= 4:
                        pe.wait_ge(S("pt_ev"), q - 3)
                    for c in range(KC):
                        last = mm(PS[q % 4][:, 0:NT], wview(n)[:, c, m * P:(m + 1) * P], uT[:, c, :],
                                  start=c == 0, stop=c == KC - 1)
                    last.then_inc(S("pt_mm"), 1)
                if n == 1:
                    pe.wait_ge(S("wff_in"), 16)
                    for c in range(KC):
                        last = mm(PS[5][0:FH, 0:NT], wff[:, c, :], uT[:, c, :], start=c == 0, stop=c == KC - 1)
                    last.then_inc(S("pe_stage"), once("pe_stage", "ff_mm"))
            pe.wait_ge(S("pt_ev"), 28)
            q = 0
            for base in (FK, FV, HI):
                for i, (t0, n) in enumerate(TILES):
                    if q >= 2:
                        pe.wait_ge(S("nat_ev"), q - 1)
                    for c in range(4):
                        m = tr(PS[q % 2][0:n, c * P:(c + 1) * P], PT[:, base + c, t0:t0 + n], ident[:, :])
                    m.then_inc(S("nat_mm"), 1)
                    q += 1
            for c in range(4):
                m = tr(PS[2][0:B, c * P:(c + 1) * P], PT[:, FQ + c, T:NT], ident[:, :])
            m.then_inc(S("pe_stage"), once("pe_stage", "qnat_mm"))
            pe.wait_ge(S("dve_stage"), AT["lfT_ok"])
            for i, (t0, n) in enumerate(TILES):
                m = tr(PS[3][0:n, i * FH:(i + 1) * FH], lfT[:, t0:t0 + n], ident[0:FH, 0:FH])
            for i in range(2):
                m = tr(PS[3][:, 32 + i * FH:32 + (i + 1) * FH], cT8[:, i * P:(i + 1) * P], ident[0:FH, 0:FH])
            m.then_inc(S("pe_stage"), once("pe_stage", "lfn_mm"))
            pe.wait_ge(S("nat_ev"), 9)
            pe.wait_ge(S("dve_stage"), AT["lf_nat"])
            pe.wait_ge(S("const_b"), 1)

            for h in range(HH):
                pe.wait_ge(S("hg_qk"), h + 1)
                if h:
                    pe.wait_ge(S("hg_ats"), h)
                for i in range(NTILE):
                    m = mm(PS[0][:, i * P:(i + 1) * P], kd[:, i * P:(i + 1) * P], qe[:, i * P:(i + 1) * P],
                           start=True, stop=True)
                m.then_inc(S("hg_A"), 1)
                if h:
                    pe.wait_ge(S("hg_kn"), h)
                for i in range(NTILE):
                    m = tr(PS[1][:, i * P:(i + 1) * P], ko[:, i * P:(i + 1) * P], ident[:, :])
                m.then_inc(S("hg_koT"), 1)
                pe.wait_ge(S("hg_kn"), h + 1)
                if h:
                    pe.wait_ge(S("hg_S"), h)
                for c in range(NCH):
                    i, j = c // 4, c % 4
                    m = mm(PS[(2, 3, 6, 7)[j]][:, i * P:(i + 1) * P], kn[CH * j:CH * j + CH, i * P:(i + 1) * P],
                           hin[CH * j:CH * j + CH, i, h * P:(h + 1) * P], start=True, stop=True,
                           tile_position=(CH * j, 0))
                m.then_inc(S("hg_U"), 1)
                pe.wait_ge(S("hg_ats"), h + 1)
                pe.wait_ge(S("hg_S"), h + 1)
                if h >= 2:
                    pe.wait_ge(S("hg_o_ev"), h - 1)
                for i in range(NTILE):
                    O = PS[4 + h % 2]
                    mm(O[:, i * P:(i + 1) * P], hin[:, i, h * P:(h + 1) * P], ats[:, i * P:(i + 1) * P],
                       start=True, stop=False, skip_group_check=True)
                    for j in range(4):
                        c = 4 * i + j
                        if c:
                            m = mm(O[:, c * CH:(c + 1) * CH], St[:, c, :], qi[:, c * CH:(c + 1) * CH],
                                   start=False, stop=j == 3, skip_group_check=True)
                m.then_inc(S("hg_o"), 1)
            for b in range(B):
                if b >= 2:
                    pe.wait_ge(S("vb_used"), b - 1)
                mm(PS[6 + b % 2][:, :], negsel[:, b, :], hin[0:B, 2, :], start=True, stop=True).then_inc(S("vb_mm"), 1)
            pe.wait_ge(S("st_new"), B)
            for b in range(B):
                for h in range(HH):
                    m = mm(PS[0][:, h * B + b:h * B + b + 1], stt[:, b, h, :], PT[:, HQ + h, T + b:T + b + 1],
                           start=True, stop=True)
            m.then_inc(S("pe_stage"), once("pe_stage", "st_o"))

            pe.wait_ge(S("hg_o_ev"), HH)
            pe.wait_ge(S("act_stage"), AT["st_o_ev"])
            for h in range(FH):
                c, o = h // 2, DH * (h % 2)
                if h:
                    pe.wait_ge(S("fx_z"), h)
                qh, kh = PT[o:o + DH, FQ + c, :], PT[o:o + DH, FK + c, :]
                for i, (a, n) in enumerate(((0, P), (P, 2 * P))):
                    mm(PS[0][:, a:a + n], qh[:, i * P:(i + 1) * P], kh[:, 0:n], start=True, stop=False,
                       tile_position=(o, 0))
                    m = mm(PS[0][:, a:a + n], negsel[:, h, :], cT8[:, 0:n], start=False, stop=True)
                m.then_inc(S("fx_s"), 1)
                pe.wait_ge(S("fx_p"), h + 1)
                if h:
                    pe.wait_ge(S("fx_pt"), h)
                for k in range(3):
                    m = tr(PS[1][:, k * P:(k + 1) * P], pp[:, k * P:(k + 1) * P], ident[:, :])
                m.then_inc(S("fx_tr"), 1)
                pe.wait_ge(S("fx_pt"), h + 1)
                if h >= 4 and h % 2 == 0:
                    pe.wait_ge(S("fx_o_ev"), c - 1)
                O = PS[2 + c % 2]
                v = fvn[:, :, h * DH:(h + 1) * DH]
                mm(O[o:o + DH, 0:P], v[:, 0, :], ptr[:, 0:P], start=True, stop=True, tile_position=(0, o))
                mm(O[o:o + DH, P:2 * P], v[:, 0, :], ptr[:, P:2 * P], start=True, stop=False, tile_position=(0, o))
                mm(O[o:o + DH, P:2 * P], v[:, 1, :], ptr[:, 2 * P:3 * P], start=False, stop=True,
                   tile_position=(0, o)).then_inc(S("fx_o"), 1)

            pe.wait_ge(S("fx_o_ev"), FC)
            pe.wait_ge(S("lf_past"), 16)
            for h in range(FH):
                if h >= 2:
                    pe.wait_ge(S("lr_ev"), h - 1)
                lfh = LF.rearrange("p (r h) -> p h r", h=FH)[:, h, :]
                tr(PS[h % 2][:, 0:P], lfh, ident[:, :])
                mm(PS[h % 2][:, P:2 * P], lfh, later[:, :], start=True, stop=True).then_inc(S("lr_mm"), 1)
            pe.wait_ge(S("lr_ev"), FH)
            pe.wait_ge(S("lnew_ok"), 1)
            for q in range(2):
                hs = slice(4 * q, 4 * q + 4)
                O = PS[2 + q][:, :].rearrange("p (h g) -> p h g", h=4)
                mm(O, tri_after[:, :], Lrow[:, hs, 0, :], start=True, stop=False)
                mm(O, ones[:, :], Lrow[:, hs, 1, :], start=False, stop=False)
                mm(O, ones[0:B, :], lnewv[:, hs, :], start=False, stop=True).then_inc(S("sf_mm"), 1)
            pe.wait_ge(S("dve_stage"), AT["qk_new"])
            pe.wait_ge(S("const_c"), 1)
            for c in range(FC):
                m = mm(PS[4][:, 0:B], hsel[:, c, :, :].rearrange("p r h -> p (r h)"), qkn[:, c, :],
                       start=c == 0, stop=c == FC - 1)
            m.then_inc(S("pe_stage"), once("pe_stage", "snew_mm"))
            pe.wait_ge(S("sf_ok"), 2)
            pe.wait_ge(S("act_stage"), AT["snew_ok"])

            def fox_seq(b):
                first = isinstance(b, int)
                pe.wait_ge(S("qm_ok"), b + 1)
                if not first:
                    pe.wait_ge(S("k_land_used"), CK * b)
                mm(PS[0][:, :], ones[0:B, :], qm[:, :], start=True, stop=True).then_inc(S("qb_mm"), 1)
                if not first:
                    pe.wait_ge(S("of_ok"), b)
                mm(PS[1][:, :], ones[0:B, :], vm[:, :], start=True, stop=True).then_inc(S("vb2_mm"), 1)
                pe.wait_ge(S("mx_ok"), b + 1)
                tr(PS[2][:, 0:P], mrep, ident[:, :]).then_inc(S("mx_tr"), 1)
                pe.wait_ge(S("dm_ok"), b + 1)
                mm(PS[3][:, 0:FH], ones[0:FH, :], dmx[0:FH, :], start=True, stop=True).then_inc(S("mb_mm"), 1)
                pe.wait_ge(S("lp_ok"), b + 1)
                mm(PS[4][:, 0:1], lrep, ones[:, 0:1], start=True, stop=True).then_inc(S("l_mm"), 1)
                for c in range(CK):
                    pe.wait_ge(S(f"v_land{c}"), 16 * CPG * (b + 1))
                    for g in range(CPG):
                        m = mm(PS[5][CH * g:CH * g + CH, :],
                               P32[:, c * CPG + g, :, :].rearrange("p r h -> p (r h)"),
                               ring[:, CK + c, 512 * g:512 * g + 512], start=c == 0, stop=c == CK - 1,
                               tile_position=(0, CH * g))
                    m.then_inc(S("v_land_used"), 1)
                pe.wait_ge(S("of_ok"), b + 1)
                for c in range(FC):
                    m = mm(PS[6][:, c:c + 1], of[:, c * P:(c + 1) * P], ones[:, 0:1], start=True, stop=True)
                m.then_inc(S("fo_mm"), 1)

            fox_seq(0)
            with pe.Fori(1, B) as b:
                fox_seq(b)

            for c in range(KC):
                pe.wait_ge(S("hs_ready"), c + 1)
                if c >= 2:
                    pe.wait_ge(S("hs_ev"), c - 1)
                mm(PS[c % 2][:, 0:NT], ones[:, :] if c < HH else pair_ones[:, :], sq[:, c % 2, :],
                   start=True, stop=True).then_inc(S("hs_mm"), 1)
            pe.wait_ge(S("mix_ok"), KC)
            pe.wait_ge(S("w_out"), 16)
            pe.wait_ge(S("hs_ev"), KC)
            for m_ in range(KC):
                if m_ >= 2:
                    pe.wait_ge(S("h_ev"), m_ - 1)
                for c in range(KC):
                    last = mm(PS[m_ % 2][:, 0:NT], wout[:, c, m_ * P:(m_ + 1) * P], PT[:, mixc(c), :],
                              start=c == 0, stop=c == KC - 1)
                last.then_inc(S("h_mm"), 1)
            rms_sum(KC)
            pe.wait_ge(S("u_ready"), 2 * KC)
            pe.wait_ge(S("wr_in"), 32)
            for c in range(KC):
                last = mm(PS[2][0:E, 0:NT], wrt[:, c, :], uT[:, c, :], start=c == 0, stop=c == KC - 1)
            last.then_inc(S("pe_stage"), once("pe_stage", "lgT_mm"))
            pe.wait_ge(S("act_stage"), AT["lgT_ok"])
            for i, (t0, n) in enumerate(TILES):
                last = tr(PS[3][0:n, i * E:(i + 1) * E], lgT[0:E, t0:t0 + n], ident[0:E, 0:E])
            last.then_inc(S("pe_stage"), once("pe_stage", "lg_mm"))
            q = 0
            for i, (t0, n) in enumerate(TILES):
                for half in range(2):
                    if q >= 2:
                        pe.wait_ge(S("un_ev"), q - 1)
                    for c in range(4):
                        last = tr(PS[q % 2][0:n, c * P:(c + 1) * P], uT[:, 4 * half + c, t0:t0 + n], ident[:, :])
                    last.then_inc(S("un_mm"), 1)
                    q += 1
            pe.wait_ge(S("un_ev"), 6)
            pe.wait_ge(S("wple_in"), 48)
            for c in range(2):
                for i, (t0, n) in enumerate(TILES):
                    last = tr(PS[5 + c][:, t0:t0 + n], pnat[0:n, i, c * P:(c + 1) * P], ident[0:n, 0:n])
                last.then_inc(S("pT_mm"), 1)
            pe.wait_ge(S("pT_ok"), 2)
            for m_ in range(KC):
                if m_ >= 2:
                    pe.wait_ge(S("pw_ev"), m_ - 1)
                for c in range(2):
                    last = mm(PS[m_ % 2][:, 0:NT], wple[:, c, m_ * P:(m_ + 1) * P], pT[:, c, :],
                              start=c == 0, stop=c == 1)
                last.then_inc(S("pw_mm"), 1)
            pe.wait_ge(S("sel_ok"), 3)
            for i, (t0, n) in enumerate(TILES):
                for j in range(i):
                    mm(PS[4][0:n, i * E:(i + 1) * E], ones[:, 0:n], selm[:, j, :], start=j == 0, stop=False)
                last = mm(PS[4][0:n, i * E:(i + 1) * E], tri_before[0:n, 0:n], selm[0:n, i, :],
                          start=i == 0, stop=True)
            for j, (t0, n) in enumerate(TILES):
                last = mm(PS[4][0:XMAX, 128:128 + E], ones[0:n, 0:XMAX], selm[0:n, j, :], start=j == 0, stop=j == 2)
            for i, (t0, n) in enumerate(TILES):
                last = tr(PS[5][0:E, t0:t0 + n], gate[0:n, i, :], ident[0:n, 0:n])
            last.then_inc(S("pe_stage"), once("pe_stage", "rk_mm"))
            pe.wait_ge(S("dve_stage"), AT["tot_ok"])
            mm(PS[7][:, 0:2 * XMAX + 1], ones[0:XMAX, :], dgl, start=True, stop=True).then_inc(S("pe_stage"), once("pe_stage", "tot_mm"))
            pe.wait_ge(S("act_stage"), AT["gT_ok"])
            pe.wait_ge(S("pw_ev"), KC)
            for c in range(KC):
                if c >= 2:
                    pe.wait_ge(S("bd_ev"), c - 1)
                mm(PS[c % 2][:, 0:NT], bdn[:, c * P:(c + 1) * P], gT[0:E, :], start=True, stop=True)\
                    .then_inc(S("bd_mm"), 1)
            pe.wait_ge(S("bd_ev"), KC)
            pe.wait_ge(S("bup_in"), 16)

            def gather(n, u):
                pe.wait_ge(S("sel_e"), n + 1)
                if not (isinstance(n, int) and n == 0):
                    pe.wait_ge(S("xg_ev"), n)
                    pe.wait_ge(S("stz_ok"), n)
                for k in range(KC):
                    for i, (t0, nn) in enumerate(TILES):
                        for s in range(3):
                            last = mm(PS[2][:, k * 64:(k + 1) * 64], UB[0:nn, s, i, k * P:(k + 1) * P],
                                      SB[0:nn, u, i, :], start=(i == 0 and s == 0), stop=(i == 2 and s == 2))
                last.then_inc(S("xg_mm"), 1)
                for i, (t0, nn) in enumerate(TILES):
                    last = tr(PS[5][:, t0:t0 + nn], SG[0:nn, u, i, :], ident[0:nn, 0:nn])
                last.then_inc(S("st_mm"), 1)

            def up(n, u, first):
                pe.wait_ge(S("xg_ev"), n + 1)
                if not first:
                    pe.wait_ge(S("h_read"), n)
                for k in range(KC):
                    pe.wait_ge(S(f"w_land{k}"), 16 * n + 16)
                    for q in range(2):
                        for hf in range(2):
                            last = mm(PS[q][64 * hf:64 * hf + 64, :], XTe[:, u, k * 64:(k + 1) * 64],
                                      ring[:, k, q * 1024 + hf * 512:q * 1024 + hf * 512 + 512],
                                      start=k == 0, stop=False, tile_position=(0, 64 * hf))
                    last.then_inc(S("w_used"), 1)
                for q in range(2):
                    for hf in range(2):
                        last = mm(PS[q][64 * hf:64 * hf + 64, :], sel32[0:E, u, :],
                                  bup[:, q * 1024 + hf * 512:q * 1024 + hf * 512 + 512],
                                  start=False, stop=True)
                last.then_inc(S("up_mm"), 1)

            def down(n, u, first):
                pe.wait_ge(S("act_ok"), n + 1)
                for j in range(4):
                    last = tr(PS[3][:, j * P:(j + 1) * P], a3[:, j * P:(j + 1) * P], ident[:, :])
                last.then_inc(S("at_mm"), 1)
                pe.wait_ge(S("at_ev"), n + 1)
                if not first:
                    pe.wait_ge(S("yg_ev"), n)
                for kk in range(KC):
                    if kk % 2 == 0:
                        pe.wait_ge(S(f"w_land{8 + kk // 2}"), 16 * n + 16)
                    for dh in range(2):
                        last = mm(PS[4][64 * dh:64 * dh + 64, :],
                                  AT2[:, (kk % 4) * P + (kk // 4) * 64:(kk % 4) * P + (kk // 4) * 64 + 64],
                                  ring[:, 8 + kk // 2, (kk % 2) * 1024 + dh * 512:(kk % 2) * 1024 + dh * 512 + 512],
                                  start=kk == 0, stop=kk == KC - 1, tile_position=(0, 64 * dh))
                    if kk % 2:
                        last.then_inc(S("w_used"), 1)

            def scatter(n, u, first):
                pe.wait_ge(S("yg_ev"), n + 1)
                pe.wait_ge(S("stz_ok"), n + 1)
                for c in range(KC):
                    if not (first and c < 2):
                        pe.wait_ge(S("y_add"), KC * n + c - 1)
                    last = mm(PS[6 + c % 2][:, 0:NT], YG[:, (c % 4) * P:(c % 4) * P + P], STz[:, u, c // 4, :],
                              start=True, stop=True)
                    last.then_inc(S("y_mm"), 1)

            def experts(base, i, first, last):
                for u in range(2):
                    n = base + 2 * i + u
                    z0 = isinstance(n, int) and n == 0
                    up(n, u, z0)
                    if not (last and u == 1):
                        gather(n + 1, 1 - u)
                    if not (first and u == 0):
                        scatter(n - 1, 1 - u, isinstance(n, int) and n == 1)
                    down(n, u, z0)

            def moe_pass(base):
                gather(base, 0)
                experts(base, 0, True, False)
                with pe.Fori(1, PAIRS - 1) as i:
                    experts(base, i, False, False)
                experts(base, PAIRS - 1, False, True)
                scatter(base + E - 1, 1, False)

            moe_pass(0)
            with further(pe) as x:
                gather(E + x, 0)
                up(E + x, 0, False)
                down(E + x, 0, False)
                scatter(E + x, 0, False)

            pe.wait_ge(S("dve_stage"), AT["moe_done"])
            pe.wait_ge(S("wg_in"), 16)
            for m_ in range(KC):
                if m_ >= 2:
                    pe.wait_ge(S("sg_ev"), m_ - 1)
                for c in range(KC):
                    last = mm(PS[m_ % 2][:, 0:NT], wgate[:, c, m_ * P:(m_ + 1) * P], xT[:, c, :],
                              start=c == 0, stop=c == KC - 1)
                last.then_inc(S("sg_mm"), 1)
            rms_sum(2 * KC)
            pe.wait_ge(S("u_ready"), 3 * KC)
            pe.wait_ge(S("sg_ev"), KC)
            q = 0
            for i, (t0, n) in enumerate(TILES):
                for half in range(2):
                    if q >= 2:
                        pe.wait_ge(S("yo_lo" if q % 2 == 0 else "yo_hi"), q // 2)
                    for c in range(4):
                        last = tr(PS[q % 2][0:n, c * P:(c + 1) * P], uT[:, 4 * half + c, t0:t0 + n], ident[:, :])
                    last.then_inc(S("yo_mm"), 1)
                    q += 1

        @block.scalar
        def _(act):
            a = Chain(act, achain)
            A = act.activation

            def root(out, in_, width):
                return A(out, in_, ACT.Sqrt, bias=eps[0:out.shape[0]], scale=1.0 / width)

            act.wait_ge(S("const_a"), 1)
            act.wait_ge(S("dve_stage"), AT["lb_in"])
            A(lbt[:, 0:2, :], lbt[:, 0:2, :], ACT.Exp).then_inc(S("act_stage"), once("act_stage", "lb_exp"))
            for c in range(KC):
                act.wait_ge(S("xt_mm"), c + 1)
                A(xT[:, c, :], PS[c % 4][:, 0:NT], ACT.Copy).then_inc(S("xt_ev"), 1)
            act.wait_ge(S("sq_used"), KC)
            root(rt[:, 0, :], PS[4][:, 0:NT], D).then_inc(S("rt_ok"), 1)
            for q in range(28):
                act.wait_ge(S("pt_mm"), q + 1)
                j, m = ORDER[q // 4], q % 4
                A(PT[:, 4 * j + m, :], PS[q % 4][:, 0:NT], ACT.Copy).then_inc(S("pt_ev"), 1)
                if q == 8:
                    act.wait_ge(S("dve_stage"), AT["ff_na"])
                    A(fft[:, 1, :], fft[:, 1, :], ACT.Exp).then_inc(S("act_stage"), once("act_stage", "ff_exp"))
                    act.wait_ge(S("dve_stage"), AT["ff_w"])
                    A(fft[:, 3, :], fft[:, 2, :], ACT.Ln).then_inc(S("act_stage"), once("act_stage", "ff_ln"))
            act.wait_ge(S("pt_ev"), 28)
            A(PT[:, HF:HF + 4, :], PT[:, HF:HF + 4, :], ACT.Sigmoid).then_inc(S("act_stage"), once("act_stage", "hf_sig"))
            act.wait_ge(S("dve_stage"), AT["lfT_ok"])
            for k, base in enumerate((HQ, HG)):
                if k:
                    act.wait_ge(S("silu"), k)
                A(tmp4, PT[:, base:base + 4, :], ACT.Sigmoid).then_inc(S("silu_sig"), 1)
            for h in range(HH):
                act.wait_ge(S("dve_stage"), AT["f_ok"])
                act.wait_ge(S("silu"), 2)
                if h:
                    act.wait_ge(S("hg_b"), h)
                A(lnf, PT[:, HF + h, 0:T], ACT.Ln).then_inc(S("hg_ln"), 1)
                act.wait_ge(S("hg_d"), h + 1)
                A(e1, bc, ACT.Exp)
                A(e2, bc, ACT.Exp, scale=-1.0)
                A(e3, bb, ACT.Exp)
                A(e4, b2, ACT.Exp).then_inc(S("hg_exp"), 1)
                act.wait_ge(S("hg_koT"), h + 1)
                A(kn, PS[1][:, 0:T], ACT.Copy).then_inc(S("hg_kn"), 1)
                act.wait_ge(S("hg_o"), h + 1)
                A(PT[:, HI + h, 0:T], PS[4 + h % 2][:, 0:T], ACT.Copy).then_inc(S("hg_o_ev"), 1)
            act.wait_ge(S("pe_stage"), AT["st_o"])
            A(PT[:, HI:HI + HH, T:NT], PS[0][:, 0:HH * B].rearrange("p (h b) -> p h b", h=HH), ACT.Copy)\
                .then_inc(S("act_stage"), once("act_stage", "st_o_ev"))
            for h in range(FH):
                act.wait_ge(S("fx_max"), h + 1)
                A(pp[:, 0:P], zz[:, 0:P], ACT.Exp, bias=small[:, 100:101], accum_out=small[:, 102:103])
                A(pp[:, P:3 * P], zz[:, P:3 * P], ACT.Exp, bias=small[:, 101:102], accum_out=small[:, 103:104])\
                    .then_inc(S("fx_exp"), 1)
                act.wait_ge(S("fx_tr"), h + 1)
                if h:
                    act.wait_ge(S("fx_o"), h)
                A(ptr, PS[1][:, 0:3 * P], ACT.Copy).then_inc(S("fx_pt"), 1)
                if h % 2:
                    c = h // 2
                    act.wait_ge(S("fx_o"), h + 1)
                    A(PT[:, FQ + c, 0:T], PS[2 + c % 2][:, 0:T], ACT.Copy).then_inc(S("fx_o_ev"), 1)
            for h in range(FH):
                act.wait_ge(S("lr_mm"), h + 1)
                A(Lrow[:, h, :, :], PS[h % 2][:, 0:2 * P].rearrange("p (a b) -> p a b", a=2), ACT.Copy)\
                    .then_inc(S("lr_ev"), 1)
            for q in range(2):
                act.wait_ge(S("sf_mm"), q + 1)
                A(SF[:, 4 * q:4 * q + 4, :], PS[2 + q][:, :].rearrange("p (h g) -> p h g", h=4), ACT.Copy)\
                    .then_inc(S("sf_ok"), 1)
            act.wait_ge(S("pe_stage"), AT["snew_mm"])
            A(snew[:, :], PS[4][:, 0:B], ACT.Copy, scale=SCALE).then_inc(S("act_stage"), once("act_stage", "snew_ok"))
            act.wait_ge(S("act_stage"), AT["snew_ok"])
            act.wait_ge(S("dve_stage"), AT["q_nat"])

            def fox_seq(b):
                first = isinstance(b, int)
                if not first:
                    act.wait_ge(S("qb_mm"), b)
                    act.wait_ge(S("vb2_mm"), b)
                A(qm[:, :], qnat[:, :], ACT.Copy, scale=ident[0:B, ds(b, 1)])
                A(vm[:, :], fvn[0:B, 2, :], ACT.Copy, scale=ident[0:B, ds(b, 1)]).then_inc(S("qm_ok"), 1)
                act.wait_ge(S("z_ok"), b + 1)
                A(P32[:, :, :, :], zrep(z), ACT.Exp).then_inc(S("p_ok"), 1)
                A(pnew, snew[:, ds(b, 1)], ACT.Exp, bias=mcol_neg).then_inc(S("pn_ok"), 1)
                act.wait_ge(S("fo_mm"), b + 1)
                A(PT[:, FQ:FQ + FC, ds(b + T, 1)], PS[6][:, 0:FC].rearrange("p (c a) -> p c a", a=1), ACT.Copy)\
                    .then_inc(S("fo_ev"), 1)

            fox_seq(0)
            with act.Fori(1, B) as b:
                fox_seq(b)
            for c in range(KC):
                act.wait_ge(S("hs_mm"), c + 1)
                if c >= 2:
                    act.wait_ge(S("hs_rstd"), c - 1)
                root(rt[:, c % 2, :], PS[c % 2][:, 0:NT], DK if c < HH else DH).then_inc(S("hs_ev"), 1)
            act.wait_ge(S("sq_used"), 2 * KC)
            act.wait_ge(S("hs_rstd"), KC)
            root(rt[:, 0, :], PS[4][:, 0:NT], D).then_inc(S("rt_ok"), 1)
            act.wait_ge(S("pe_stage"), AT["lgT_mm"])
            A(lgT[0:E, :], PS[2][0:E, 0:NT], ACT.Identity, bias=rb).then_inc(S("act_stage"), once("act_stage", "lgT_ok"))
            for i in range(3):
                n = TILES[i][1]
                act.wait_ge(S("top_ok"), i + 1)
                A(gate[0:n, i, :], lg[0:n, i, :], ACT.Exp, bias=m8neg[0:n, i:i + 1]).then_inc(S("g_exp"), 1)
            for q in range(6):
                i, half = q // 2, q % 2
                n = TILES[i][1]
                act.wait_ge(S("un_mm"), q + 1)
                A(UB[0:n, 0, i, 512 * half:512 * half + 512], PS[q % 2][0:n, :], ACT.Copy).then_inc(S("u_hi"), 1)
            for c in range(2):
                act.wait_ge(S("pT_mm"), c + 1)
                A(pT[:, c, :], PS[5 + c][:, 0:NT], ACT.Copy).then_inc(S("pT_ok"), 1)
            for m_ in range(KC):
                act.wait_ge(S("pw_mm"), m_ + 1)
                A(pwT[:, m_, :], PS[m_ % 2][:, 0:NT], ACT.Copy).then_inc(S("pw_ev"), 1)
            act.wait_ge(S("pe_stage"), AT["rk_mm"])
            A(gT[0:E, :], PS[5][0:E, 0:NT], ACT.Copy).then_inc(S("act_stage"), once("act_stage", "gT_ok"))
            act.wait_ge(S("dve_stage"), AT["stz_zero"])

            def gathered(n, u):
                act.wait_ge(S("xg_mm"), n + 1)
                A(XTe[:, u, :], PS[2][:, :], ACT.Copy).then_inc(S("xg_ev"), 1)

            def turned(n, u, first, after=None):
                act.wait_ge(S("st_mm"), n + 1)
                if not first:
                    act.wait_ge(S("y_mm"), KC * (n - 1 if after is None else after))
                A(STz[0:64, u, 0, :], PS[5][0:64, 0:NT], ACT.Copy)
                A(STz[64:128, u, 1, :], PS[5][64:128, 0:NT], ACT.Copy).then_inc(S("stz_ok"), 1)

            def experts(base, i, first, last):
                for u in range(2):
                    n = base + 2 * i + u
                    z0 = isinstance(n, int) and n == 0
                    act.wait_ge(S("glu_ok"), n + 1)
                    A(a3, a1, ACT.Sigmoid, scale=1.702).then_inc(S("sig_ok"), 1)
                    if not (last and u == 1):
                        gathered(n + 1, 1 - u)
                        turned(n + 1, 1 - u, z0)
                    act.wait_ge(S("at_mm"), n + 1)
                    A(AT2, PS[3][:, :], ACT.Copy).then_inc(S("at_ev"), 1)
                    act.wait_ge(S("w_used"), 12 * n + 12)
                    if not z0:
                        act.wait_ge(S("y_mm"), KC * n)
                    A(YG, PS[4][:, :], ACT.Copy).then_inc(S("yg_ev"), 1)

            def moe_pass(base):
                gathered(base, 0)
                turned(base, 0, isinstance(base, int))
                experts(base, 0, True, False)
                with act.Fori(1, PAIRS - 1) as i:
                    experts(base, i, False, False)
                experts(base, PAIRS - 1, False, True)

            moe_pass(0)
            with further(act) as x:
                n = E + x
                gathered(n, 0)
                turned(n, 0, False, after=n)
                act.wait_ge(S("glu_ok"), n + 1)
                A(a3, a1, ACT.Sigmoid, scale=1.702).then_inc(S("sig_ok"), 1)
                act.wait_ge(S("at_mm"), n + 1)
                A(AT2, PS[3][:, :], ACT.Copy).then_inc(S("at_ev"), 1)
                act.wait_ge(S("w_used"), 12 * n + 12)
                act.wait_ge(S("y_mm"), KC * n)
                A(YG, PS[4][:, :], ACT.Copy).then_inc(S("yg_ev"), 1)
            act.wait_ge(S("dve_stage"), AT["moe_done"])
            for m_ in range(KC):
                act.wait_ge(S("sg_mm"), m_ + 1)
                A(sgT[:, m_, :], PS[m_ % 2][:, 0:NT], ACT.Sigmoid).then_inc(S("sg_ev"), 1)
            act.wait_ge(S("sq_used"), 3 * KC)
            root(rt[:, 0, :], PS[4][:, 0:NT], D).then_inc(S("rt_ok"), 1)
            for q in range(1, 6, 2):
                i, half = q // 2, q % 2
                n = TILES[i][1]
                act.wait_ge(S("yo_mm"), q + 1)
                A(yout[0:n, i, 512:1024], PS[1][0:n, :], ACT.Copy).then_inc(S("yo_hi"), 1)

        @block.vector
        def _(dve):
            d = Chain(dve, dchain)

            def head_scale(c):
                dve.wait_ge(S("hs_ev"), c + 1)
                d(dve.reciprocal(rstd[:, :], rt[:, c % 2, :]))
                mc = PT[:, mixc(c), :]
                g = (GHG + c) if c < HH else (GFOX + c - HH)
                out = STT(mc, mc, gcols[:, g:g + 1], rstd[:, :], ALU.mult, ALU.mult)
                out.then_inc(S("hs_rstd"), 1)
                dve.wait_ge(S("hs_rstd"), c + 1)
                if c < HH:
                    dve.tensor_tensor(mc, mc, PT[:, HG + c, :], ALU.mult).then_inc(S("mix_ok"), 1)
                else:
                    dve.nop().then_inc(S("mix_ok"), 1)
            TT, TS, STT, CP = dve.tensor_tensor, dve.tensor_scalar, dve.scalar_tensor_tensor, dve.tensor_copy
            M, AD, SU = ALU.mult, ALU.add, ALU.subtract

            def bcast(ap, n):
                return ap.unsqueeze(len(ap.shape)).broadcast_to(list(ap.shape) + [n])

            def squares(k, src, c):
                if k + c >= 2:
                    dve.wait_ge(S("sq_used"), k + c - 1)
                TT(sq[:, (k + c) % 2, :], src, src, M).then_inc(S("sq_ready"), 1)

            def rms(k, g):
                for c in range(KC):
                    squares(k, xT[:, c, :], c)
                dve.wait_ge(S("rt_ok"), k // KC + 1)
                d(dve.reciprocal(rstd[:, :], rt[:, 0, :]))
                for c in range(KC):
                    STT(uT[:, c, :], xT[:, c, :], gcols[:, g + c:g + c + 1], rstd[:, :], M, M)\
                        .then_inc(S("u_ready"), 1)

            dve.wait_ge(S("pe_stage"), AT["g_ready"])
            d(CP(gcols[:, :], PS[7][:, 0:40]))
            l0, l1 = gcols[:, LB0:LB0 + 4], gcols[:, LB1:LB1 + 4]
            d(TT(lbt[:, 2, :], l0, l1, ALU.max))
            TT(lbt[:, 0, :], l0, lbt[:, 2, :], SU)
            TT(lbt[:, 1, :], l1, lbt[:, 2, :], SU).then_inc(S("dve_stage"), once("dve_stage", "lb_in"))
            dve.wait_ge(S("act_stage"), AT["lb_exp"])
            d(TT(lbt[:, 2, :], lbt[:, 0, :], lbt[:, 1, :], AD))
            d(dve.reciprocal(oml, lbt[:, 2, :]))
            d(TT(lb, lbt[:, 0, :], oml, M))
            d(TS(oml, lb, -1.0, 1.0, M, AD))
            dve.wait_ge(S("xt_ev"), KC)
            rms(0, GMIX)

            dve.wait_ge(S("pe_stage"), AT["ff_mm"])
            x, e, w, l = (fft[:, i, :] for i in range(4))
            d(TS(x, PS[5][0:FH, 0:NT], ffb, None, AD))
            d(TS(w, x, -1.0, None, M))
            TT(e, x, w, ALU.min).then_inc(S("dve_stage"), once("dve_stage", "ff_na"))
            dve.wait_ge(S("act_stage"), AT["ff_exp"])
            TS(w, e, 1.0, None, AD).then_inc(S("dve_stage"), once("dve_stage", "ff_w"))
            dve.wait_ge(S("dve_stage"), AT["ff_w"])
            t1, t2 = lfT[:, :], sq[0:FH, 0, :]
            d(TS(t1, w, -1.0, None, AD))
            d(TS(t2, t1, 0.0, None, ALU.is_equal))
            d(TT(t1, t1, t2, AD))
            dve.wait_ge(S("act_stage"), AT["ff_ln"])
            d(dve.reciprocal(w, t1))
            d(TT(l, l, w, M))
            d(TT(l, l, t2, AD))
            d(TT(l, l, e, M))
            d(TS(x, x, 0.0, None, ALU.min))
            d(TT(lfT[:, :], x, l, SU))
            dve.memset(fft[:, 1, 0:T], 1.0).then_inc(S("dve_stage"), once("dve_stage", "lf_one"))
            dve.wait_ge(S("dve_stage"), AT["lf_one"])
            dve.tensor_tensor_scan(cT8[:, :], fft[:, 1, 0:T], lfT[:, 0:T], 0.0, M, AD).then_inc(S("dve_stage"), once("dve_stage", "lfT_ok"))
            q = 0
            for dst in (fkn, fvn, hin):
                for i, (t0, n) in enumerate(TILES):
                    dve.wait_ge(S("nat_mm"), q + 1)
                    CP(dst[0:n, i, :], PS[q % 2][0:n, :]).then_inc(S("nat_ev"), 1)
                    if q == 5:
                        dve.wait_ge(S("nat_ev"), 6)
                        dve.nop().then_inc(S("dve_stage"), once("dve_stage", "fkv_nat"))
                    q += 1
            dve.wait_ge(S("pe_stage"), AT["qnat_mm"])
            CP(qnat[:, :], PS[2][0:B, :]).then_inc(S("dve_stage"), once("dve_stage", "q_nat"))
            dve.wait_ge(S("pe_stage"), AT["lfn_mm"])
            for i, (t0, n) in enumerate(TILES):
                CP(lfn[0:n, i, :], PS[3][0:n, i * FH:(i + 1) * FH])
            d(CP(cnat[:, :, :], PS[3][:, 32:32 + 2 * FH].rearrange("p (i h) -> p i h", i=2)))
            dve.nop().then_inc(S("dve_stage"), once("dve_stage", "lf_nat"))
            d(TS(cT8[:, :], cT8[:, :], 1.0 / SCALE, None, M))
            TT(qkn, PT[:, FQ:FQ + 4, T:NT], PT[:, FK:FK + 4, T:NT], M).then_inc(S("dve_stage"), once("dve_stage", "qk_new"))

            dve.wait_ge(S("act_stage"), AT["hf_sig"])
            for h in range(HH):
                last = TS(PT[:, HF + h, :], PT[:, HF + h, :], oml[:, h:h + 1], lb[:, h:h + 1], M, AD)
            last.then_inc(S("dve_stage"), once("dve_stage", "f_ok"))
            dve.wait_ge(S("dve_stage"), AT["f_ok"])
            d(TS(kT, PT[:, HF:HF + 4, :], -1.0, 1.0, M, AD))
            for k, base in enumerate((HQ, HG)):
                dve.wait_ge(S("silu_sig"), k + 1)
                TT(PT[:, base:base + 4, :], PT[:, base:base + 4, :], tmp4, M).then_inc(S("silu"), 1)
            dve.wait_ge(S("silu"), 2)
            dve.wait_ge(S("const_b"), 1)
            dve.memset(St[:, 0, :], 0.0)
            for h in range(HH):
                def chunks(t):
                    return t.rearrange("p (c r) -> p c r", r=CH)
                dve.wait_ge(S("hg_ln"), h + 1)
                dve.tensor_tensor_scan(bb, reset[:, :], lnf, 0.0, M, AD).then_inc(S("hg_b"), 1)
                dve.wait_ge(S("hg_b"), h + 1)
                mid = chunks(bb)[:, :, CH // 2 - 1:CH // 2].broadcast_to([P, NCH, CH])
                end = chunks(bb)[:, :, CH - 1:CH].broadcast_to([P, NCH, CH])
                d(TT(chunks(bc), chunks(bb), mid, SU))
                TT(chunks(b2), end, chunks(bb), SU)
                TS(bc, bc, 80.0, -80.0, ALU.min, ALU.max).then_inc(S("hg_d"), 1)
                dve.wait_ge(S("hg_exp"), h + 1)
                if h:
                    dve.wait_ge(S("hg_o"), h)
                qh, kh = PT[:, HQ + h, 0:T], kT[:, h, 0:T]
                TT(qe, qh, e1, M)
                TT(kd, kh, e2, M)
                TT(qi, qh, e3, M)
                TT(ko, kh, e4, M).then_inc(S("hg_qk"), 1)
                dve.wait_ge(S("hg_A"), h + 1)
                for i in range(NTILE):
                    last = TT(ats[:, i * P:(i + 1) * P], PS[0][:, i * P:(i + 1) * P], hmask[:, :], M)
                last.then_inc(S("hg_ats"), 1)
                dve.wait_ge(S("hg_U"), h + 1)
                for c in range(NCH):
                    U = PS[(2, 3, 6, 7)[c % 4]][:, (c // 4) * P:(c // 4 + 1) * P]
                    dst = St[:, c + 1, :] if c < NCH - 1 else sfin[:, h, :]
                    last = STT(dst, St[:, c, :], e3[:, c * CH + CH - 1:c * CH + CH], U, M, AD)
                    if c < NCH - 1:
                        d(last)
                last.then_inc(S("hg_S"), 1)
                dve.wait_ge(S("hg_S"), h + 1)
                dve.nop().then_inc(S("sfin_ok"), 1)
            dve.wait_ge(S("st_in"), 16)
            for b in range(B):
                dve.wait_ge(S("vb_mm"), b + 1)
                kb = kT[:, :, T + b:T + b + 1].broadcast_to([P, HH, DK])
                fb = PT[:, HF:HF + HH, T + b:T + b + 1].broadcast_to([P, HH, DK])
                t = av(1280 + 512 * (b % 2), 512).rearrange("p (h v) -> p h v", h=HH)
                TT(t, PS[6 + b % 2][:, :].rearrange("p (h v) -> p h v", h=HH), kb, M).then_inc(S("vb_used"), 1)
                d(TT(stt[:, b, :, :], stt[:, b, :, :], fb, M))
                dve.wait_ge(S("vb_used"), b + 1)
                TT(stt[:, b, :, :], stt[:, b, :, :], t, SU).then_inc(S("st_new"), 1)

            dve.wait_ge(S("st_new"), B)
            CP(lnewv, bcast(lfn[0:B, 2, :], NPAGE)).then_inc(S("dve_stage"), once("dve_stage", "lnew_cp"))
            dve.wait_ge(S("hg_o_ev"), HH)
            nm, ls, rs = small[:, 100:102], small[:, 102:104], small[:, 104:106]
            mxs = small[:, 106:108]
            z2 = zz.rearrange("p (a b) -> p a b", b=2 * P)[:, :, 0:P]
            for h in range(FH):
                dve.wait_ge(S("fx_s"), h + 1)
                if h:
                    dve.wait_ge(S("fx_exp"), h)
                TS(zz[:, 0:P], PS[0][:, 0:P], SCALE, cnat[:, 0, h:h + 1], M, AD)
                TS(zz[:, P:3 * P], PS[0][:, P:3 * P], SCALE, cnat[:, 1, h:h + 1], M, AD).then_inc(S("fx_z"), 1)
                dve.wait_ge(S("fx_z"), h + 1)
                for z_ in (zz[:, 0:P], zz[:, 2 * P:3 * P]):
                    d(TT(z_, z_, cmask[:, :], AD))
                dve.tensor_reduce(mxs[:, 0:1], zz[:, 0:P], AX.X, ALU.max)
                d(dve.tensor_reduce(mxs[:, 1:2], zz[:, P:3 * P], AX.X, ALU.max))
                TS(nm, mxs, -1.0, None, M).then_inc(S("fx_max"), 1)
                dve.wait_ge(S("fx_exp"), h + 1)
                d(dve.reciprocal(rs, ls))
                TS(pp[:, 0:P], pp[:, 0:P], rs[:, 0:1], None, M)
                TS(pp[:, P:3 * P], pp[:, P:3 * P], rs[:, 1:2], None, M).then_inc(S("fx_p"), 1)

            dve.wait_ge(S("sf_ok"), 2)
            dve.wait_ge(S("act_stage"), AT["snew_ok"])
            dve.wait_ge(S("const_c"), 1)
            dve.wait_ge(S("lr_ev"), FH)
            SEQ_STEPS = 14

            def fox_seq(b):
                d0 = d.n
                first = isinstance(b, int)
                dve.wait_ge(S("qb_mm"), b + 1)
                qb = PS[0][:, :].unsqueeze(1).broadcast_to([P, CPG, 512])
                for c in range(CK):
                    dve.wait_ge(S(f"k_land{c}"), 16 * CPG * (b + 1))
                    TT(prod.rearrange("p (g n) -> p g n", n=512),
                       ring[:, c, :].rearrange("p (g n) -> p g n", n=512), qb, M).then_inc(S("k_land_used"), 1)
                    dve.wait_ge(S("k_land_used"), CK * b + c + 1)
                    d(dve.tensor_reduce(sc[:, 32 * c:32 * c + 32], prod.rearrange("p (a b) -> p a b", b=DH),
                                        AX.X, AD))
                zv = z.rearrange("p (g h) -> p g h", h=FH)
                d(STT(zv, sc.rearrange("p (g h) -> p g h", h=FH), SCALE,
                      SF[:, :, ds(b * NPG, NPG)].rearrange("p h g -> p g h"), M, AD))
                d(dve.tensor_reduce(mx, z.rearrange("p (g h) -> p h g", h=FH), AX.X, ALU.max))
                CP(mrep.rearrange("p (r h) -> p r h", h=FH), mx.unsqueeze(1).broadcast_to([P, 16, FH]))\
                    .then_inc(S("mx_ok"), 1)
                dve.wait_ge(S("mx_tr"), b + 1)
                d(dve.tensor_reduce(mcol, PS[2][:, 0:P], AX.X, ALU.max))
                d(TT(mcol, mcol, snew[:, ds(b, 1)], ALU.max))
                d(TS(mcol_neg, mcol, -1.0, None, M))
                TS(dmx[0:FH, :], ident[0:FH, 0:FH], mcol_neg[0:FH, :], None, M).then_inc(S("dm_ok"), 1)
                dve.wait_ge(S("mb_mm"), b + 1)
                TT(zv, zv, PS[3][:, 0:FH].unsqueeze(1).broadcast_to([P, NPG, FH]), AD).then_inc(S("z_ok"), 1)
                dve.wait_ge(S("p_ok"), b + 1)
                d(dve.tensor_reduce(lsum, P32[:, :, 0, :].rearrange("p g h -> p h g"), AX.X, AD))
                CP(lrep.rearrange("p (r h) -> p r h", h=FH), lsum.unsqueeze(1).broadcast_to([P, 16, FH]))\
                    .then_inc(S("lp_ok"), 1)
                dve.wait_ge(S("l_mm"), b + 1)
                dve.wait_ge(S("pn_ok"), b + 1)
                d(TT(ltot, PS[4][:, 0:1], pnew, AD))
                d(dve.reciprocal(rl, ltot))
                d(TT(pnr, pnew, rl, M))
                dve.wait_ge(S("v_land_used"), CK * (b + 1))
                if not first:
                    dve.wait_ge(S("fo_mm"), b)
                ofm = ofmask.rearrange("p h d -> p (h d)")
                STT(of, PS[5][:, :], rl, ofm, M, M)
                d(STT(of2[0:FH, :], PS[1][0:FH, :], pnr[0:FH, :], ofm[0:FH, :], M, M))
                TT(of[0:FH, :], of[0:FH, :], of2[0:FH, :], AD).then_inc(S("of_ok"), 1)
                assert d.n - d0 == SEQ_STEPS, d.n - d0

            fox_seq(0)
            start = d.n
            with dve.Fori(1, B) as b:
                d.off = (b - 1) * SEQ_STEPS
                fox_seq(b)
            d.off, d.n = 0, start + (B - 1) * SEQ_STEPS

            dve.wait_ge(S("fo_ev"), B)
            for c in range(KC):
                mc = PT[:, mixc(c), :]
                if c >= 2:
                    dve.wait_ge(S("hs_mm"), c - 1)
                TT(sq[:, c % 2, :], mc, mc, M).then_inc(S("hs_ready"), 1)
                if c:
                    head_scale(c - 1)
            head_scale(KC - 1)
            for m_ in range(KC):
                dve.wait_ge(S("h_mm"), m_ + 1)
                TT(xT[:, m_, :], xT[:, m_, :], PS[m_ % 2][:, 0:NT], AD).then_inc(S("h_ev"), 1)
            dve.wait_ge(S("h_ev"), KC)
            dve.wait_ge(S("hs_mm"), KC)
            rms(KC, GMLP)
            dve.wait_ge(S("pe_stage"), AT["lg_mm"])
            for i, (t0, n) in enumerate(TILES):
                L = lg[0:n, i, :]
                r0, r1, r2, r3 = (rt4[0:n, k, :] for k in range(4))
                d(CP(L, PS[3][0:n, i * E:(i + 1) * E]))
                d(dve.max(m8[0:n, i, :], L))
                TS(m8neg[0:n, i:i + 1], m8[0:n, i, 0:1], -1.0, None, M).then_inc(S("top_ok"), 1)
                d(TS(r0, L, m8[0:n, i, 3:4], None, ALU.is_gt))
                d(dve.tensor_reduce(cnt[0:n, 0:1], r0, AX.X, AD))
                TS(r1, L, m8[0:n, i, 3:4], None, ALU.is_equal)
                d(dve.memset(r3, 1.0))
                d(dve.tensor_tensor_scan(r2, r3, r1, 0.0, M, AD))
                d(TS(r2, r2, cnt[0:n, 0:1], float(TOPK), AD, ALU.is_le))
                d(TT(r1, r1, r2, M))
                TT(selm[0:n, i, :], r0, r1, AD).then_inc(S("sel_t"), 1)
                dve.wait_ge(S("sel_t"), i + 1)
                dve.wait_ge(S("g_exp"), i + 1)
                G = gate[0:n, i, :]
                d(TT(G, G, selm[0:n, i, :], M))
                d(dve.tensor_reduce(cnt[0:n, 1:2], G, AX.X, AD))
                d(dve.reciprocal(cnt[0:n, 2:3], cnt[0:n, 1:2]))
                TS(G, G, cnt[0:n, 2:3], None, M).then_inc(S("sel_ok"), 1)
            for q in range(6):
                i, half = q // 2, q % 2
                n = TILES[i][1]
                src = PS[q % 2][0:n, :]
                c0 = 512 * half
                dve.wait_ge(S("u_hi"), q + 1)
                hi_, mi_, lo_ = (UB[0:n, s, i, c0:c0 + 512] for s in range(3))
                TT(a1[0:n, :], src, hi_, SU).then_inc(S("un_ev"), 1)
                dve.wait_ge(S("un_ev"), q + 1)
                d(CP(mi_, a1[0:n, :]))
                d(TT(lo_, a1[0:n, :], mi_, SU))
            dve.wait_ge(S("pe_stage"), AT["rk_mm"])
            d(dve.memset(RG[:, :, :], -1.0))
            for i, (t0, n) in enumerate(TILES):
                d(STT(rk[0:n, i, :], PS[4][0:n, i * E:(i + 1) * E], 1.0, selm[0:n, i, :], AD, M))
                d(TS(RG[0:n, :, i], rk[0:n, i, :], -1.0, None, AD))
                d(CP(RG[0:n, :, 3 + i], gate[0:n, i, :]))
            for k in range(NBLK):
                TS(flag[:, E * k:E * k + E], PS[4][0:XMAX, 128:128 + E], float(SLOTS * (k + 1)), None, ALU.is_gt)
            d(dve.memset(hit, 1.0))
            d(dve.tensor_tensor_scan(pos, hit, flag, 0.0, M, AD))
            d(TS(hit, pos, order_no[0:XMAX, :], None, ALU.is_equal))
            d(TT(hit, hit, flag, M))
            dve.wait_ge(S("codes_ok"), 1)
            for w in range(2):
                d(TT(flag, hit, codes[:, w * E * NBLK:(w + 1) * E * NBLK], M))
                d(dve.tensor_reduce(found[:, w:w + 1], flag, AX.X, AD))
            d(CP(found[:, 2:3], pos[:, E * NBLK - 1:E * NBLK]))
            for w in range(2):
                d(TS(dgl[:, 1 + w * XMAX:1 + (w + 1) * XMAX], ident[0:XMAX, 0:XMAX], found[:, w:w + 1], None, M))
            TS(dgl[:, 0:1], ident[0:XMAX, 0:1], found[:, 2:3], None, M).then_inc(S("dve_stage"), once("dve_stage", "tot_ok"))
            dve.wait_ge(S("pe_stage"), AT["tot_mm"])
            d(CP(xlist, PS[7][:, 0:2 * XMAX + 1]))
            CP(xint, xlist[0:1, 0:XMAX + 1]).then_inc(S("dve_stage"), once("dve_stage", "list_ok"))
            for c in range(KC):
                dve.wait_ge(S("bd_mm"), c + 1)
                TT(xT[:, c, :], xT[:, c, :], PS[c % 2][:, 0:NT], AD).then_inc(S("bd_ev"), 1)
            dve.memset(STz[:, :, :, :], 0.0).then_inc(S("dve_stage"), once("dve_stage", "stz_zero"))

            SEL_STEPS, ACT_STEPS = 1, 1

            def choose(n, e, u, first, after=None, start=None):
                if not first:
                    k = n - 1 if after is None else after
                    dve.wait_ge(S("xg_mm"), k)
                    dve.wait_ge(S("st_mm"), k)
                    dve.wait_ge(S("up_mm"), k)
                d(CP(cur[:, u, :], RG[:, ds(e, 1), :].rearrange("p a r -> p (a r)")))
                if start is not None:
                    d(CP(first_rank, start))
                    d(TS(cur[:, u, 0:3], cur[:, u, 0:3], first_rank, None, SU))
                CP(sel32[0:E, u, :], ident[0:E, ds(e, 1)].broadcast_to([E, 64]))
                for i, (t0, nn) in enumerate(TILES):
                    TS(SB[0:nn, u, i, :], slot_no[0:nn, 0:64], cur[0:nn, u, i:i + 1], None, ALU.is_equal)
                    last = TS(SG[0:nn, u, i, :], slot_no[0:nn, :], cur[0:nn, u, i:i + 1],
                              cur[0:nn, u, 3 + i:4 + i], ALU.is_equal, M)
                last.then_inc(S("sel_e"), 1)

            def swiglu(n):
                dve.wait_ge(S("up_mm"), n + 1)
                TS(a1, PS[0][:, :], LIMIT, None, ALU.min).then_inc(S("glu_ok"), 1)
                TS(a2, PS[1][:, :], LIMIT, -LIMIT, ALU.min, ALU.max).then_inc(S("h_read"), 1)
                dve.wait_ge(S("h_read"), n + 1)
                d(STT(a2, a2, 1.0, a1, AD, M))
                dve.wait_ge(S("sig_ok"), n + 1)
                TT(a3, a3, a2, M).then_inc(S("act_ok"), 1)

            def add_up(n):
                for c in range(KC):
                    dve.wait_ge(S("y_mm"), KC * n + c + 1)
                    TT(xT[:, c, :], xT[:, c, :], PS[6 + c % 2][:, 0:NT], AD).then_inc(S("y_add"), 1)

            def experts(base, i, first, last):
                for u in range(2):
                    n = base + 2 * i + u
                    if not (last and u == 1):
                        choose(n + 1, 2 * i + u + 1, 1 - u, isinstance(n, int) and n == 0)
                    swiglu(n)
                    if not (first and u == 0):
                        add_up(n - 1)

            def moe_pass(base):
                choose(base, 0, 0, isinstance(base, int))
                experts(base, 0, True, False)
                start, off = d.n, d.off
                with dve.Fori(1, PAIRS - 1) as i:
                    d.off = off + (i - 1) * 4
                    experts(base, i, False, False)
                assert d.n - start == 4
                d.n, d.off = start + 4 * (PAIRS - 2), off
                experts(base, PAIRS - 1, False, True)
                add_up(base + E - 1)

            moe_pass(0)
            start = d.n
            with further(dve) as x:
                d.off = x * 4
                n = E + x
                e = dve.value_load(xint[0:1, ds(x + 1, 1)], min_val=0, max_val=E - 1)
                choose(n, e, 0, False, after=n, start=xlist[:, ds(x + (1 + XMAX), 1)])
                swiglu(n)
                add_up(n)
            assert d.n - start == 4, d.n - start
            d.sem, d.n, d.off = S("dve_chain_tail"), 0, 0
            dve.memset(small[:, 110:111], 0.0).then_inc(S("dve_stage"), once("dve_stage", "moe_done"))
            for m_ in range(KC):
                dve.wait_ge(S("sg_ev"), m_ + 1)
                TT(sgT[:, m_, :], sgT[:, m_, :], pwT[:, m_, :], M).then_inc(S("sp_ok"), 1)
                dve.wait_ge(S("sp_ok"), m_ + 1)
                if m_ == KC - 1:
                    dve.wait_ge(S("sg_mm"), KC)
            for m_ in range(KC):
                last = TT(xT[:, m_, :], xT[:, m_, :], sgT[:, m_, :], AD)
            d(last)
            rms(2 * KC, GFIN)
            for q in range(0, 6, 2):
                i = q // 2
                n = TILES[i][1]
                dve.wait_ge(S("yo_mm"), q + 1)
                CP(yout[0:n, i, 0:512], PS[0][0:n, :]).then_inc(S("yo_lo"), 1)


_INS = ['x_prompt', 'x_sample', 'state_hgrn', 'cache_k', 'cache_v', 'cache_logf', 'page_table', 'p_prompt', 'p_sample',
        'g_mix', 'w_in', 'hg_lb_logits', 'g_hg_out', 'fox_f_bias', 'g_fox_out', 'w_out', 'g_mlp', 'w_router',
        'b_router', 'w_up', 'b_up', 'w_down', 'b_down', 'w_ple', 'w_ple_gate', 'g_final']
_OUTS = [(1, 256, 1024), (8, 1, 1024), (1, 1, 4, 128, 128), (1, 1, 256, 8, 64), (1, 1, 256, 8, 64), (1, 1, 256, 8),
         (1, 8, 4, 128, 128), (1, 8, 1, 8, 64), (1, 8, 1, 8, 64), (1, 8, 1, 8)]


def kernel(**inputs):
    import numpy as _np
    import concourse.bacc as _bacc
    from concourse import mybir as _mybir
    from concourse.bass_utils import run_bass_kernel_spmd as _run

    nc = _bacc.Bacc("TRN2", target_bir_lowering=False, num_devices=1)
    arrays, args = {}, []
    for name in _INS:
        a = _np.ascontiguousarray(inputs[name])
        arrays[f"in_{name}_dram"] = a
        args.append(nc.dram_tensor(f"in_{name}_dram", a.shape, _mybir.dt.from_np(a.dtype), kind="ExternalInput").ap())
    for i, shape in enumerate(_OUTS):
        args.append(nc.dram_tensor(f"out_{i}_dram", shape, _mybir.dt.float32, kind="ExternalOutput").ap())
    hybrid_layer_kernel(nc, *args)
    r = _run(nc, [arrays], core_ids=[0])
    return tuple(r.results[0][f"out_{i}_dram"] for i in range(len(_OUTS)))
```

```python
from contextlib import ExitStack, contextmanager

import concourse.bass as bass
from concourse import mybir

F32 = mybir.dt.float32
BF16 = mybir.dt.bfloat16
I32 = mybir.dt.int32
U32 = mybir.dt.uint32
ALU = mybir.AluOpType
ACT = mybir.ActivationFunctionType
AX = mybir.AxisListType
ds = bass.ds

P = 128
EPS = 1e-6
NEG = -1.0e30
TOPK = 4
LIMIT = 7.0


class Chain:

    def __init__(self, eng, sem):
        self.eng, self.sem, self.n, self.off = eng, sem, 0, 0

    def __call__(self, ins):
        self.n += 1
        ins.then_inc(self.sem, 1)
        self.eng.wait_ge(self.sem, self.off + self.n)


def hybrid_layer_kernel(nc, x_prompt, x_sample, state_hgrn, cache_k, cache_v, cache_logf, page_table,
                        p_prompt, p_sample, g_mix, w_in, hg_lb_logits, g_hg_out, fox_f_bias, g_fox_out,
                        w_out, g_mlp, w_router, b_router, w_up, b_up, w_down, b_down, w_ple, w_ple_gate,
                        g_final, y_p, y_s, st_p, k_p, v_p, lf_p, st_s, k_s, v_s, lf_s, SLOTS=64):
    D = x_prompt.shape[2]
    T = x_prompt.shape[1]
    B = x_sample.shape[0]
    NT = T + B
    KC = D // P
    NTILE = T // P
    TILES = [(i * P, P) for i in range(NTILE)] + [(T, B)]
    HH, DK = state_hgrn.shape[2], state_hgrn.shape[3]
    FH, DH = cache_k.shape[3], cache_k.shape[4]
    FW = FH * DH
    NPG = page_table.shape[1]
    NPAGE = B * NPG
    E = w_up.shape[1]
    PLE = w_ple.shape[1]
    SCALE = float(DH) ** -0.5
    CH = 32
    NCH = T // CH
    NB = w_in.shape[2] // 512
    FC = FW // P
    HQ, HF, HI, HG, FQ, FK, FV = (4 * j for j in range(7))
    ORDER = [4, 5, 6, 1, 0, 2, 3]
    BLOCK_SLOT = [0, 2, 4, 8, 10, 8, 10]
    RING = 12
    CK = 4
    CPG = NPG // CK
    assert D == 1024 and T == 256 and B == 8 and FW == 512 and DK == P and NB == 7 and NPAGE == P

    with ExitStack() as ctx:
        def sb(name, shape, dt=F32):
            return ctx.enter_context(nc.sbuf_tensor(name, shape, dt))

        def sem(name):
            return ctx.enter_context(nc.semaphore(name))

        PS = [ctx.enter_context(nc.psum_tensor(f"bank{i}", [P, 512], F32)) for i in range(8)]

        ring = sb("ring", [P, RING, 2048])
        xT = sb("xT", [P, KC, NT])
        uT = sb("uT", [P, KC, NT])
        PT = sb("PT", [P, 28, NT])
        XN = sb("XN", [P, 3, D])
        hin = sb("hin", [P, 3, 512])
        arena = sb("arena", [P, 8064])

        ident = sb("ident", [P, P])
        ones = sb("ones", [P, P])
        pair_ones = sb("pair_ones", [P, P])
        hmask = sb("hmask", [P, P])
        cmask = sb("cmask", [P, P])
        tri_after = sb("tri_after", [P, P])
        tri_before = sb("tri_before", [P, P])
        later = sb("later", [P, P])
        slot_no = sb("slot_no", [P, P])
        reset = sb("reset", [P, T])
        ofmask = arena[:, 7040:7552].rearrange("p (h d) -> p h d", h=FH)
        hsel = arena[:, 7552:8064].rearrange("p (c r h) -> p c r h", c=FC, h=FH)
        negsel = sb("negsel", [B, FH, P])
        gcols = sb("gcols", [P, 40])
        small = sb("small", [P, 256])
        sq = sb("sq", [P, 2, NT])
        rt = sb("rt", [P, 2, NT])
        rstd = sb("rstd", [P, NT])
        snew = sb("snew", [P, B])
        page_i = sb("page_i", [1, NPAGE], I32)
        page_c = sb("page_c", [P, 1], I32)
        cnat = sb("cnat", [P, 2, FH])

        GMIX, GMLP, GFIN, GHG, GFOX, LB0, LB1 = 0, 8, 16, 24, 28, 32, 36
        eps = small[:, 0:1]
        lb = small[:, 4:8]
        oml = small[:, 8:12]
        lbt = small[:, 12:24].rearrange("p (a b) -> p a b", b=4)
        ffb = small[0:FH, 24:25]
        rb = small[0:E, 25:26]
        lfn = small[:, 32:56].rearrange("p (i h) -> p i h", i=3)

        sems = {}

        def S(name):
            if name not in sems:
                sems[name] = sem(name)
            return sems[name]

        STAGES = {
            "pe_stage": ["g_ready", "ff_mm", "qnat_mm", "lfn_mm", "snew_mm", "st_o", "lgT_mm", "lg_mm", "rk_mm", "tot_mm"],
            "act_stage": ["lb_exp", "ff_exp", "ff_ln", "snew_ok", "hf_sig", "st_o_ev", "lgT_ok", "gT_ok"],
            "dve_stage": ["lb_in", "ff_na", "ff_w", "lf_one", "lfT_ok", "qk_new", "q_nat", "fkv_nat", "lf_nat", "lnew_cp", "f_ok", "tot_ok", "list_ok", "stz_zero", "moe_done"],
        }
        AT = {name: k + 1 for names in STAGES.values() for k, name in enumerate(names)}
        told = {stage: 0 for stage in STAGES}

        def once(stage, name):
            told[stage] += 1
            assert STAGES[stage][told[stage] - 1] == name, name
            return 1

        dchain, achain, gchain = S("dve_chain"), S("act_chain"), S("pool_chain")

        def av(a, n):
            return arena[:, a:a + n]
        qe, kd, bb, ko, qi, ats, kn, kh = (av(256 * i, 256) for i in range(8))
        St = av(2048, 1152).rearrange("p (c v) -> p c v", v=P)
        sfin = av(3200, 512).rearrange("p (h v) -> p h v", h=HH)
        tmp4 = av(2048, 1056).rearrange("p (h t) -> p h t", h=HH)
        zz, pp, ptr = av(0, 512), av(512, 384), av(896, 384)
        Lrow = av(1280, 2048).rearrange("p (h two g) -> p h two g", h=FH, two=2)
        SF = av(3712, 1024).rearrange("p (h g) -> p h g", h=FH)
        sc, z = av(4736, 128), av(4864, 128)
        LF = av(4992, 1024)
        P32 = av(4992, 512).rearrange("p (g r h) -> p g r h", g=NPG, r=4)
        of = av(5504, 512)
        qb = av(6016, 1024).rearrange("p (u n) -> p u n", u=2)
        of2 = av(7552, 512)
        stt = ring[:, 8:10, :].rearrange("p a (b h v) -> p (a b) h v", h=HH, v=P)
        fkn, fvn = XN[:, :, 0:512], XN[:, :, 512:1024]
        qnat = sq[0:B, :, :].rearrange("p a b -> p (a b)")[:, 0:512]
        PTf = PT[:, :, :].rearrange("p a b -> p (a b)")
        knew = small[:, 160:192].rearrange("p (h b) -> p h b", h=HH)
        dec = rstd
        mrep, lrep = dec[:, 0:128], dec[:, 128:256]
        mx, dmx, lsum = small[:, 192:200], small[:, 200:208], small[:, 208:216]
        mcol, pnew, ltot, rl, pnr = (small[:, 216 + i:217 + i] for i in range(5))
        qkn = small[:, 64:96].rearrange("p (c b) -> p c b", c=4)
        mcol_neg = small[:, 221:222]
        lfT = rt[0:FH, 1, :]
        cT8 = rt[0:FH, 0, 0:T]
        fft = arena[0:FH, 0:4 * NT].rearrange("p (i t) -> p i t", i=4)
        lnewv = arena[0:B, 0:FH * NPAGE].rearrange("p (h g) -> p h g", h=FH)

        def zrep(z):
            return z.rearrange("p (g h) -> p g h", h=FH).unsqueeze(2).broadcast_to([P, NPG, 4, FH])

        def mixc(c):
            return HI + c if c < HH else FQ + c - HH

        def wslot(n):
            return BLOCK_SLOT[n]

        def wview(n):
            return ring[:, wslot(n):wslot(n) + 2, :].rearrange("p a (c n) -> p (a c) n", n=512)

        wff = hin[:, 2, 0:KC * FH].rearrange("p (c n) -> p c n", n=FH)
        wout = ring[:, 8:12, :].rearrange("p a (c n) -> p (a c) n", n=D)

        PTf = PT[:, :, :].rearrange("p a b -> p (a b)")
        UB = PTf[:, 0:4608].bitcast(BF16).rearrange("p (s i d) -> p s i d", s=3, i=3)
        XTe = PTf[:, 4608:5632].rearrange("p (u n) -> p u n", u=2)
        RG = PTf[:, 5632:5824].rearrange("p (e r) -> p e r", r=6)
        lg = PTf[:, 5824:5920].rearrange("p (i e) -> p i e", i=3)
        gate = PTf[:, 5920:6016].rearrange("p (i e) -> p i e", i=3)
        selm = PTf[:, 6016:6112].rearrange("p (i e) -> p i e", i=3)
        rk = PTf[:, 6112:6208].rearrange("p (i e) -> p i e", i=3)
        m8neg = PTf[:, 6232:6235]
        m8 = PTf[:, 6208:6232].rearrange("p (i e) -> p i e", i=3)
        rt4 = PTf[:, 6240:6368].rearrange("p (i e) -> p i e", i=4)
        cnt = PTf[:, 6368:6384]
        lgT = PTf[:, 6400:6664]
        gT = PTf[:, 6664:6928]
        cur = PTf[:, 6928:6940].rearrange("p (u r) -> p u r", u=2)
        first_rank = PTf[:, 6940:6941]
        sel32 = PTf[:, 6944:7072].rearrange("p (u r) -> p u r", u=2)
        XMAX = NT * TOPK // SLOTS
        NBLK = (NT - 1) // SLOTS
        flag, pos, hit = (hin[0:XMAX, k, 0:E * NBLK] for k in range(3))
        codes = sq[0:XMAX, :, :].rearrange("p a b -> p (a b)")[:, 0:2 * E * NBLK]
        found = dec[0:XMAX, 0:3]
        dgl = dec[0:XMAX, 8:8 + 2 * XMAX + 1]
        xlist = dec[:, 128:128 + 2 * XMAX + 1]
        xint = small[0:1, 128:128 + XMAX + 1].bitcast(I32)
        order_no = small[:, 112:113]
        a1, a2, a3, AT2, YG = (av(512 * i, 512) for i in range(5))
        STz = av(2560, 4 * NT).rearrange("p (u d t) -> p u d t", u=2, d=2)
        SG = av(4672, 768).rearrange("p (u i s) -> p u i s", u=2, i=3)
        SB = av(5440, 192).bitcast(BF16).rearrange("p (u i s) -> p u i s", u=2, i=3)
        bup = uT[:, :, :].rearrange("p a b -> p (a b)")[0:E, 0:2048]
        pwT = XN[:, :, :].rearrange("p a b -> p (a b)")[:, 0:KC * NT].rearrange("p (c t) -> p c t", c=KC)
        wrt = ring[:, 6, 0:KC * E].rearrange("p (c e) -> p c e", e=E)
        bdn = ring[0:E, 6, 256:1280]
        wple = ring[:, 7, :].rearrange("p (c n) -> p c n", n=D)
        pnat = ring[:, 6, 1280:1280 + 3 * PLE].rearrange("p (i d) -> p i d", i=3)
        pT = av(4992, 2 * NT).rearrange("p (c t) -> p c t", c=2)
        wgate = ring[:, 0:4, :].rearrange("p a (c n) -> p (a c) n", n=D)
        sgT = PTf[:, 0:KC * NT].rearrange("p (c t) -> p c t", c=KC)
        yout = PTf[:, 2112:2112 + 3 * D].rearrange("p (i d) -> p i d", i=3)

        w_in_c = w_in[0].rearrange("(c p) n -> p c n", p=P)
        wo_c = w_out[0].rearrange("(c p) n -> p c n", p=P)
        wg_c = w_ple_gate[0].rearrange("(c p) n -> p c n", p=P)
        PAIRS = E // 2

        def between(*extra):
            extra = list(extra)
            while len(extra) < 8:
                extra.append([])
            return extra

        def quarter(n):
            return [[("block", n, m)] for m in range(4)]

        def head(h):
            return [("fox_a", h)], [("fox_b", h)], [("fox_c", h)]

        B3, B4, B5, B6 = (quarter(n) for n in (3, 4, 5, 6))
        f = [head(h) for h in range(FH)]
        g = [[[(f"hg_{p}", h)] for p in "abcd"] for h in range(HH)]
        FILL = [
            between(B3[0], B3[1], B3[2], B3[3], f[0][0], f[0][1], f[0][2]),
            between(B4[0] + f[1][0], B4[1] + f[1][1], B4[2] + f[1][2], B4[3] + [("gates",)], f[2][0], f[2][1], f[2][2]),
            between(B5[0] + f[3][0], B5[1] + f[3][1], B5[2] + f[3][2], B5[3], f[4][0], f[4][1], f[4][2]),
            between(B6[0] + f[5][0], B6[1] + f[5][1], B6[2] + f[5][2], B6[3], [("hi_nat",)], f[6][0], f[6][1], f[6][2]),
            between(f[7][0], f[7][1], f[7][2], [("hgd_a",)], [("hgd_b",)], g[0][0]),
            between(g[0][1], g[0][2], g[0][3], g[1][0], [], g[1][1], g[1][2], g[1][3]),
            between(g[2][0], g[2][1], g[2][2], g[2][3], [("w_out",)], g[3][0]),
            between(g[3][1], g[3][2], g[3][3]),
        ]
        STEPS = []
        for b_ in range(B):
            STEPS.append(("seq_q", b_))
            for c_ in range(CK):
                STEPS += [("seq_k", b_, c_)] + FILL[b_][c_]
            for c_, name in enumerate(("seq_max", "seq_exp", "seq_pv", "seq_out")):
                STEPS += [(name, b_)] + FILL[b_][CK + c_]

        def run(parts):
            for name, *args in STEPS:
                if name in parts:
                    parts[name](*args)

        @contextmanager
        def further(eng):
            eng.wait_ge(S("dve_stage"), AT["list_ok"])
            count = eng.value_load(xint[0:1, 0:1], min_val=0, max_val=XMAX)
            with eng.If(count > 0):
                with eng.Fori(0, count) as x:
                    yield x

        block = ctx.enter_context(nc.Block())

        @block.sync
        def _(sp):
            def load(dst, src, s, k=16):
                sp.dma_start(dst, src).then_inc(S(s), k)

            load(XN[:, 0:2, :], x_prompt[0].rearrange("(i p) d -> p i d", p=P), "x_in")
            load(XN[0:B, 2, :], x_sample[:, 0, :], "x_in")
            for r, v in ((GMIX, g_mix[0]), (GMLP, g_mlp[0]), (GFIN, g_final), (GHG, g_hg_out[0]), (GFOX, g_fox_out[0]),
                         (LB0, hg_lb_logits[0]), (LB1, hg_lb_logits[1])):
                n = v.shape[0] // P
                load(hin[r:r + n, 0, 0:P], v.rearrange("(c p) -> c p", p=P), "rows_in")
            load(ffb, fox_f_bias.rearrange("a h -> h a"), "rows_in")
            load(rb, b_router.rearrange("a h -> h a"), "rows_in")
            load(page_i[:, :], page_table.rearrange("b g -> (b g)").rearrange("(a n) -> a n", a=1), "page_in")
            load(page_c[:, :], page_table.rearrange("b g -> (b g)").rearrange("(n a) -> n a", a=1), "page_in")
            for n in range(5):
                load(wview(n), w_in_c[:, :, 512 * ORDER[n]:512 * ORDER[n] + 512], f"w_in{n}")
                if n == 2:
                    load(wff, w_in_c[:, :, NB * 512:NB * 512 + FH], "wff_in")
            sp.wait_ge(S("page_in"), 32)

            def pages(cache, slot0, b, land):
                for c in range(CK):
                    for g in range(CPG):
                        r = sp.value_load(page_i[0:1, ds(b * NPG + c * CPG + g, 1)], min_val=0,
                                          max_val=cache_k.shape[1] - 1)
                        if g == 0 and isinstance(b, int) and b == 0 and c in (0, 2) and slot0 + c < 6:
                            sp.wait_ge(S("pt_mm"), 4 * ((slot0 + c) // 2) + 4)
                        if g == 0 and not (isinstance(b, int) and b == 0):
                            sp.wait_ge(S(land + "_used"), CK * b + c - CK + 1)
                        sp.dma_start(ring[:, slot0 + c, 512 * g:512 * g + 512],
                                     cache[0][ds(r, 1)].rearrange("a r h d -> r (a h d)")).then_inc(S(f"{land}{c}"), 16)

            def seq(b):
                pages(cache_k, 0, b, "k_land")
                pages(cache_v, CK, b, "v_land")

            seq(0)
            sp.wait_ge(S("dve_stage"), AT["fkv_nat"])
            load(k_p[0, 0].rearrange("(i p) h d -> p i (h d)", p=P), fkn[:, 0:2, :], "out")
            load(k_s[0, :, 0].rearrange("b h d -> b (h d)"), fkn[0:B, 2, :], "out")
            load(v_p[0, 0].rearrange("(i p) h d -> p i (h d)", p=P), fvn[:, 0:2, :], "out")
            load(v_s[0, :, 0].rearrange("b h d -> b (h d)"), fvn[0:B, 2, :], "out")
            sp.wait_ge(S("dve_stage"), AT["lf_nat"])
            load(lf_p[0, 0].rearrange("(i p) h -> p i h", p=P), lfn[:, 0:2, :], "out")
            load(lf_s[0, :, 0], lfn[0:B, 2, :], "out")
            with sp.Fori(1, B) as b:
                seq(b)
            sp.wait_ge(S("k_land_used"), CK * B)
            sp.wait_ge(S("v_land_used"), CK * B)
            load(wrt, w_router[0].rearrange("(c p) e -> p c e", p=P), "wr_in")
            load(bdn, b_down[0], "wr_in")
            load(wple, w_ple[0].rearrange("(c p) n -> p c n", p=P), "wple_in")
            load(pnat[:, 0:2, :], p_prompt[0, 0].rearrange("(i p) d -> p i d", p=P), "wple_in")
            load(pnat[0:B, 2, :], p_sample[0, :, 0, :], "wple_in")
            def expert(src_e, n, first, s):
                if not first:
                    sp.wait_ge(S("w_used"), 12 * n + s - 11)
                if s < 8:
                    src = w_up[0][ds(src_e, 1)].rearrange("a (c p) n -> p (a c) n", p=P)[:, s, :]
                    sp.dma_start(ring[:, s, :], src).then_inc(S(f"w_land{s}"), 16)
                else:
                    j = s - 8
                    src = w_down[0][ds(src_e, 1)].rearrange("a (c p) n -> p (a c) n", p=P)[:, 2 * j:2 * j + 2, :]
                    sp.dma_start(ring[:, s, :].rearrange("p (c n) -> p c n", c=2), src)\
                      .then_inc(S(f"w_land{s}"), 16)

            for s in range(6):
                expert(0, 0, True, s)
            sp.wait_ge(S("h_mm"), KC)
            for s in range(8, RING):
                expert(0, 0, True, s)
            sp.wait_ge(S("un_mm"), 6)
            sp.wait_ge(S("pe_stage"), AT["lgT_mm"])
            load(bup, b_up[0], "bup_in")
            sp.wait_ge(S("bd_mm"), KC)
            sp.wait_ge(S("pw_mm"), KC)
            for s in (6, 7):
                expert(0, 0, True, s)
            with sp.Fori(1, E) as e:
                for s in range(RING):
                    expert(e, e, False, s)
            with further(sp) as x:
                e = sp.value_load(xint[0:1, ds(x + 1, 1)], min_val=0, max_val=E - 1)
                for s in range(RING):
                    expert(e, E + x, False, s)
            sp.wait_ge(S("dve_stage"), AT["moe_done"])
            load(wgate, wg_c, "wg_in")
            sp.wait_ge(S("yo_lo"), 3)
            sp.wait_ge(S("yo_hi"), 3)
            load(y_p[0].rearrange("(i p) d -> p i d", p=P), yout[:, 0:2, :], "out")
            load(y_s[:, 0, :], yout[0:B, 2, :], "out")
            sp.wait_ge(S("out"), 16 * 8)
            sp.wait_ge(S("sfin_out"), 16)

        @block.gpsimd
        def _(gp):
            g = Chain(gp, gchain)

            def fill(t, v):
                g(gp.memset(t, v))

            def keep(t, base, cm, pattern, op=ALU.is_ge, fillv=0.0):
                g(gp.affine_select(out=t, in_=t, compare_op=op, fill=fillv, base=base, pattern=pattern,
                                   channel_multiplier=cm))

            fill(eps, EPS)
            fill(ident[:, :], 0.0)
            keep(ident[:, :], 0, 1, [[-1, P]], ALU.not_equal, 1.0)
            fill(ones[:, :], 1.0)
            gp.nop().then_inc(S("const_a"), 1)
            po = pair_ones[:, :].rearrange("p (a b) -> p a b", a=2)
            fill(po, 1.0)
            keep(po, 0, 1, [[-DH, 2], [0, DH]])
            keep(po, DH - 1, -1, [[DH, 2], [0, DH]])
            fill(hmask[:, :], 1.0)
            hm = hmask[:, :].rearrange("p (a b) -> p a b", b=CH)
            keep(hm, 0, 1, [[-CH, P // CH], [0, CH]])
            keep(hm, 0, -1, [[CH, P // CH], [1, CH]])
            fill(cmask[:, :], 0.0)
            keep(cmask[:, :], 0, 1, [[-1, P]], ALU.is_ge, NEG)
            fill(tri_after[:, :], 1.0)
            keep(tri_after[:, :], -1, 1, [[-1, P]])
            fill(tri_before[:, :], 1.0)
            keep(tri_before[:, :], -1, -1, [[1, P]])
            fill(later[:, :], 1.0)
            lt = later[:, :].rearrange("p (a b) -> p a b", b=NPG)
            keep(lt, -1, 1, [[-NPG, B], [-1, NPG]])
            keep(lt, NPG - 1, -1, [[NPG, B], [0, NPG]])
            fill(negsel[:, :, :], 0.0)
            keep(negsel[:, :, :], 0, 1, [[-1, FH], [0, P]], ALU.not_equal, -1.0)
            fill(reset[:, :], 1.0)
            fill(reset[:, :].rearrange("p (c r) -> p c r", r=CH)[:, :, 0:1], 0.0)
            g(gp.iota(slot_no[:, :], [[0, P // 64], [1, 64]], base=0, channel_multiplier=0,
                      allow_small_or_imprecise_dtypes=True))
            if SLOTS < 64:
                fill(slot_no[:, :].rearrange("p (a b) -> p a b", a=2)[:, :, SLOTS:64], -1.0e4)
            g(gp.iota(order_no, [[0, 1]], base=1, channel_multiplier=1, allow_small_or_imprecise_dtypes=True))
            gp.nop().then_inc(S("const_b"), 1)
            fill(ofmask, 0.0)
            for q in range(4):
                keep(ofmask, -CH * q, 1, [[-1, FH], [0, DH]], ALU.not_equal, 1.0)
            fill(hsel, 1.0)
            keep(hsel, 0, 1, [[P, FC], [0, 16], [-DH, FH]])
            keep(hsel, DH - 1, -1, [[-P, FC], [0, 16], [DH, FH]])
            gp.nop().then_inc(S("const_c"), 1)
            gp.wait_ge(S("page_in"), 32)
            gp.indirect_dma_start(
                LF, None, cache_logf[0].rearrange("n r h -> n (r h)"),
                bass.IndirectOffsetOnAxis(ap=page_c[:, :].bitcast(U32), axis=0)).then_inc(S("lf_past"), 16)
            gp.wait_ge(S("dve_stage"), AT["lnew_cp"])
            lv = lnewv.rearrange("p h (b g) -> p h b g", b=B)
            keep(lv, 0, 1, [[0, FH], [-1, B], [0, NPG]], ALU.is_equal, 0.0)
            gp.nop().then_inc(S("lnew_ok"), 1)

            def seq_k(b, c):
                if c == 0:
                    gp.wait_ge(S("qb_ok"), b + 1)
                gp.wait_ge(S(f"k_land{c}"), 16 * CPG * (b + 1))
                kv = ring[:, c, :].rearrange("p (g n) -> p g n", n=512)
                gp.tensor_tensor(kv, kv, qb[:, b % 2, :].unsqueeze(1).broadcast_to([P, CPG, 512]), ALU.mult)\
                    .then_inc(S("k_mul"), 1)

            run({"seq_k": seq_k})
            gp.wait_ge(S("u_ready"), 2 * KC)
            c4 = codes.rearrange("p (w b e) -> p w b e", w=2, e=E)
            g(gp.iota(c4[:, 0], [[0, NBLK], [1, E]], base=0, channel_multiplier=0,
                      allow_small_or_imprecise_dtypes=True))
            g(gp.iota(c4[:, 1], [[SLOTS, NBLK], [0, E]], base=SLOTS, channel_multiplier=0,
                      allow_small_or_imprecise_dtypes=True))
            gp.nop().then_inc(S("codes_ok"), 1)

        @block.tensor
        def _(pe):
            mm, tr = pe.matmul, pe.transpose

            def rms_sum(k, n=KC, lhs=None, per=1):
                for c in range(n):
                    pe.wait_ge(S("sq_ready"), k + c + 1)
                    mm(PS[4][:, 0:NT], ones[:, :], sq[:, (k + c) % 2, :], start=c == 0, stop=c == n - 1)\
                        .then_inc(S("sq_used"), 1)

            pe.wait_ge(S("const_a"), 1)
            pe.wait_ge(S("rows_in"), 16 * 9)
            tr(PS[7][:, 0:40], hin[0:40, 0, 0:P], ident[0:40, 0:40]).then_inc(S("pe_stage"), once("pe_stage", "g_ready"))
            pe.wait_ge(S("x_in"), 32)
            for c in range(KC):
                if c >= 4:
                    pe.wait_ge(S("xt_ev"), c - 3)
                for i, (t0, n) in enumerate(TILES):
                    m = tr(PS[c % 4][:, t0:t0 + n], XN[0:n, i, c * P:(c + 1) * P], ident[0:n, 0:n])
                m.then_inc(S("xt_mm"), 1)
            rms_sum(0)
            pe.wait_ge(S("u_ready"), KC)
            pe.wait_ge(S("xt_ev"), KC)
            def block_quarter(n, m):
                q = 4 * n + m
                if m == 0:
                    pe.wait_ge(S(f"w_in{n}"), 16)
                if q >= 2:
                    pe.wait_ge(S("pt_ev"), q - 1)
                for c in range(KC):
                    last = mm(PS[q % 2][:, 0:NT], wview(n)[:, c, m * P:(m + 1) * P], uT[:, c, :],
                              start=c == 0, stop=c == KC - 1)
                last.then_inc(S("pt_mm"), 1)

            for n in range(3):
                for m in range(4):
                    block_quarter(n, m)
                if n == 1:
                    pe.wait_ge(S("wff_in"), 16)
                    for c in range(KC):
                        last = mm(PS[5][0:FH, 0:NT], wff[:, c, :], uT[:, c, :], start=c == 0, stop=c == KC - 1)
                    last.then_inc(S("pe_stage"), once("pe_stage", "ff_mm"))

            def natural(q0, bases, banks):
                q = q0
                for base in bases:
                    for i, (t0, n) in enumerate(TILES):
                        if q - q0 >= 2:
                            pe.wait_ge(S("nat_ev"), q - 1)
                        for c in range(4):
                            m = tr(PS[banks[q % 2]][0:n, c * P:(c + 1) * P], PT[:, base + c, t0:t0 + n], ident[:, :])
                        m.then_inc(S("nat_mm"), 1)
                        q += 1

            pe.wait_ge(S("pt_ev"), 12)
            for c in range(4):
                m = tr(PS[2][0:B, c * P:(c + 1) * P], PT[:, FQ + c, T:NT], ident[:, :])
            m.then_inc(S("pe_stage"), once("pe_stage", "qnat_mm"))
            natural(0, (FK, FV), (6, 7))
            pe.wait_ge(S("dve_stage"), AT["lfT_ok"])
            for i, (t0, n) in enumerate(TILES):
                m = tr(PS[3][0:n, i * FH:(i + 1) * FH], lfT[:, t0:t0 + n], ident[0:FH, 0:FH])
            for i in range(2):
                m = tr(PS[3][:, 32 + i * FH:32 + (i + 1) * FH], cT8[:, i * P:(i + 1) * P], ident[0:FH, 0:FH])
            m.then_inc(S("pe_stage"), once("pe_stage", "lfn_mm"))
            pe.wait_ge(S("const_b"), 1)
            pe.wait_ge(S("lf_past"), 16)
            pe.wait_ge(S("nat_ev"), 6)
            for h in range(FH):
                if h >= 2:
                    pe.wait_ge(S("lr_ev"), h - 1)
                lfh = LF.rearrange("p (r h) -> p h r", h=FH)[:, h, :]
                tr(PS[6 + h % 2][:, 0:P], lfh, ident[:, :])
                mm(PS[6 + h % 2][:, P:2 * P], lfh, later[:, :], start=True, stop=True).then_inc(S("lr_mm"), 1)
            pe.wait_ge(S("dve_stage"), AT["qk_new"])
            pe.wait_ge(S("const_c"), 1)
            for c in range(FC):
                m = mm(PS[4][:, 0:B], hsel[:, c, :, :].rearrange("p r h -> p (r h)"), qkn[:, c, :],
                       start=c == 0, stop=c == FC - 1)
            m.then_inc(S("pe_stage"), once("pe_stage", "snew_mm"))
            pe.wait_ge(S("lr_ev"), FH)
            pe.wait_ge(S("lnew_ok"), 1)
            for q in range(2):
                hs = slice(4 * q, 4 * q + 4)
                O = PS[6 + q][:, :].rearrange("p (h g) -> p h g", h=4)
                mm(O, tri_after[:, :], Lrow[:, hs, 0, :], start=True, stop=False)
                mm(O, ones[:, :], Lrow[:, hs, 1, :], start=False, stop=False)
                mm(O, ones[0:B, :], lnewv[:, hs, :], start=False, stop=True).then_inc(S("sf_mm"), 1)
            pe.wait_ge(S("dve_stage"), AT["lf_nat"])
            pe.wait_ge(S("dve_stage"), AT["q_nat"])
            pe.wait_ge(S("sf_ok"), 2)
            pe.wait_ge(S("act_stage"), AT["snew_ok"])

            def seq_q(b):
                mm(PS[2][:, :], negsel[:, b, :], qnat, start=True, stop=True).then_inc(S("qb_mm"), 1)

            def seq_max(b):
                pe.wait_ge(S("mx_ok"), b + 1)
                tr(PS[3][:, 0:P], mrep, ident[:, :]).then_inc(S("mx_tr"), 1)

            def seq_exp(b):
                pe.wait_ge(S("dm_ok"), b + 1)
                mm(PS[3][:, 128:128 + FH], ones[0:FH, :], dmx[0:FH, :], start=True, stop=True)\
                    .then_inc(S("mb_mm"), 1)
                pe.wait_ge(S("qb_ok"), b + 1)
                mm(PS[2][:, :], negsel[:, b, :], fvn[0:B, 2, :], start=True, stop=True).then_inc(S("vb2_mm"), 1)

            def seq_pv(b):
                pe.wait_ge(S("lp_ok"), b + 1)
                mm(PS[3][:, 136:137], lrep, ones[:, 0:1], start=True, stop=True).then_inc(S("l_mm"), 1)
                for c in range(CK):
                    pe.wait_ge(S(f"v_land{c}"), 16 * CPG * (b + 1))
                    for g in range(CPG):
                        m = mm(PS[4][CH * g:CH * g + CH, :],
                               P32[:, c * CPG + g, :, :].rearrange("p r h -> p (r h)"),
                               ring[:, CK + c, 512 * g:512 * g + 512], start=c == 0, stop=c == CK - 1,
                               tile_position=(0, CH * g))
                    m.then_inc(S("v_land_used"), 1)

            def seq_out(b):
                pe.wait_ge(S("of_ok"), b + 1)
                for c in range(FC):
                    m = mm(PS[3][:, 140 + c:141 + c], of[:, c * P:(c + 1) * P], ones[:, 0:1], start=True, stop=True)
                m.then_inc(S("fo_mm"), 1)

            def fox_a(h):
                c, o = h // 2, DH * (h % 2)
                if h:
                    pe.wait_ge(S("fx_z"), h)
                qh, kh_ = PT[o:o + DH, FQ + c, :], PT[o:o + DH, FK + c, :]
                for i, (a, n) in enumerate(((0, P), (P, 2 * P))):
                    mm(PS[6][:, a:a + n], qh[:, i * P:(i + 1) * P], kh_[:, 0:n], start=True, stop=False,
                       tile_position=(o, 0))
                    m = mm(PS[6][:, a:a + n], negsel[:, h, :], cT8[:, 0:n], start=False, stop=True)
                m.then_inc(S("fx_s"), 1)

            def fox_b(h):
                pe.wait_ge(S("fx_p"), h + 1)
                if h:
                    pe.wait_ge(S("fx_pt"), h)
                for k in range(3):
                    m = tr(PS[7][:, k * P:(k + 1) * P], pp[:, k * P:(k + 1) * P], ident[:, :])
                m.then_inc(S("fx_tr"), 1)

            def fox_c(h):
                c, o = h // 2, DH * (h % 2)
                pe.wait_ge(S("fx_pt"), h + 1)
                if h >= 2 and h % 2 == 0:
                    pe.wait_ge(S("fx_o_ev"), c)
                O = PS[5]
                v = fvn[:, :, h * DH:(h + 1) * DH]
                mm(O[o:o + DH, 0:P], v[:, 0, :], ptr[:, 0:P], start=True, stop=True, tile_position=(0, o))
                mm(O[o:o + DH, P:2 * P], v[:, 0, :], ptr[:, P:2 * P], start=True, stop=False, tile_position=(0, o))
                mm(O[o:o + DH, P:2 * P], v[:, 1, :], ptr[:, 2 * P:3 * P], start=False, stop=True,
                   tile_position=(0, o)).then_inc(S("fx_o"), 1)

            def hi_nat():
                pe.wait_ge(S("pt_ev"), 24)
                pe.wait_ge(S("pt_ev"), 28)
                natural(6, (HI,), (0, 1))

            def hgd_a():
                pe.wait_ge(S("nat_ev"), 9)
                for b in range(B):
                    if b >= 2:
                        pe.wait_ge(S("vb_used"), b - 1)
                    mm(PS[b % 2][:, :], negsel[:, b, :], hin[0:B, 2, :], start=True, stop=True)\
                        .then_inc(S("vb_mm"), 1)

            def hgd_b():
                pe.wait_ge(S("st_new"), B)
                pe.wait_ge(S("fx_o_ev"), FC)
                for b in range(B):
                    for h in range(HH):
                        m = mm(PS[5][:, h * B + b:h * B + b + 1], stt[:, b, h, :], PT[:, HQ + h, T + b:T + b + 1],
                               start=True, stop=True)
                m.then_inc(S("pe_stage"), once("pe_stage", "st_o"))

            UB_ = (0, 1, 5, 6)

            def hg_b(h):
                if h == 0:
                    pe.wait_ge(S("fx_z"), FH)
                    pe.wait_ge(S("fx_pt"), FH)
                pe.wait_ge(S("hg_qk"), h + 1)
                if h:
                    pe.wait_ge(S("hg_S"), h)
                    pe.wait_ge(S("hg_o_ev"), h)
                for i in range(NTILE):
                    m = mm(PS[6][:, i * P:(i + 1) * P], kd[:, i * P:(i + 1) * P], qe[:, i * P:(i + 1) * P],
                           start=True, stop=True)
                m.then_inc(S("hg_A"), 1)
                for i in range(NTILE):
                    m = tr(PS[7][:, i * P:(i + 1) * P], ko[:, i * P:(i + 1) * P], ident[:, :])
                m.then_inc(S("hg_koT"), 1)

            def hg_c(h):
                if h == 0:
                    pe.wait_ge(S("act_stage"), AT["st_o_ev"])
                    pe.wait_ge(S("vb_used"), B)
                pe.wait_ge(S("hg_ats"), h + 1)
                pe.wait_ge(S("hg_kn"), h + 1)
                for c in range(NCH):
                    i, j = c // 4, c % 4
                    m = mm(PS[UB_[j]][:, i * P:(i + 1) * P], kn[CH * j:CH * j + CH, i * P:(i + 1) * P],
                           hin[CH * j:CH * j + CH, i, h * P:(h + 1) * P], start=True, stop=True,
                           tile_position=(CH * j, 0))
                m.then_inc(S("hg_U"), 1)

            def hg_d(h):
                pe.wait_ge(S("hg_S"), h + 1)
                for i in range(NTILE):
                    O = PS[7]
                    mm(O[:, i * P:(i + 1) * P], hin[:, i, h * P:(h + 1) * P], ats[:, i * P:(i + 1) * P],
                       start=True, stop=False, skip_group_check=True)
                    for j in range(4):
                        c = 4 * i + j
                        if c:
                            m = mm(O[:, c * CH:(c + 1) * CH], St[:, c, :], qi[:, c * CH:(c + 1) * CH],
                                   start=False, stop=j == 3, skip_group_check=True)
                m.then_inc(S("hg_o"), 1)

            run({"seq_q": seq_q, "seq_max": seq_max, "seq_exp": seq_exp, "seq_pv": seq_pv, "seq_out": seq_out,
                 "block": block_quarter, "fox_a": fox_a, "fox_b": fox_b, "fox_c": fox_c, "hi_nat": hi_nat,
                 "hgd_a": hgd_a, "hgd_b": hgd_b, "hg_b": hg_b, "hg_c": hg_c, "hg_d": hg_d})
            pe.wait_ge(S("hg_o_ev"), HH)
            pe.wait_ge(S("fo_ev"), B)

            for c in range(KC):
                pe.wait_ge(S("hs_ready"), c + 1)
                if c >= 2:
                    pe.wait_ge(S("hs_ev"), c - 1)
                mm(PS[c % 2][:, 0:NT], ones[:, :] if c < HH else pair_ones[:, :], sq[:, c % 2, :],
                   start=True, stop=True).then_inc(S("hs_mm"), 1)
            pe.wait_ge(S("mix_ok"), KC)
            pe.wait_ge(S("w_out"), 16)
            pe.wait_ge(S("hs_ev"), KC)
            for m_ in range(KC):
                if m_ >= 2:
                    pe.wait_ge(S("h_ev"), m_ - 1)
                for c in range(KC):
                    last = mm(PS[m_ % 2][:, 0:NT], wout[:, c, m_ * P:(m_ + 1) * P], PT[:, mixc(c), :],
                              start=c == 0, stop=c == KC - 1)
                last.then_inc(S("h_mm"), 1)
            rms_sum(KC)
            pe.wait_ge(S("u_ready"), 2 * KC)
            pe.wait_ge(S("wr_in"), 32)
            for c in range(KC):
                last = mm(PS[2][0:E, 0:NT], wrt[:, c, :], uT[:, c, :], start=c == 0, stop=c == KC - 1)
            last.then_inc(S("pe_stage"), once("pe_stage", "lgT_mm"))
            pe.wait_ge(S("act_stage"), AT["lgT_ok"])
            for i, (t0, n) in enumerate(TILES):
                last = tr(PS[3][0:n, i * E:(i + 1) * E], lgT[0:E, t0:t0 + n], ident[0:E, 0:E])
            last.then_inc(S("pe_stage"), once("pe_stage", "lg_mm"))
            q = 0
            for i, (t0, n) in enumerate(TILES):
                for half in range(2):
                    if q >= 2:
                        pe.wait_ge(S("un_ev"), q - 1)
                    for c in range(4):
                        last = tr(PS[q % 2][0:n, c * P:(c + 1) * P], uT[:, 4 * half + c, t0:t0 + n], ident[:, :])
                    last.then_inc(S("un_mm"), 1)
                    q += 1
            pe.wait_ge(S("un_ev"), 6)
            pe.wait_ge(S("wple_in"), 48)
            for c in range(2):
                for i, (t0, n) in enumerate(TILES):
                    last = tr(PS[5 + c][:, t0:t0 + n], pnat[0:n, i, c * P:(c + 1) * P], ident[0:n, 0:n])
                last.then_inc(S("pT_mm"), 1)
            pe.wait_ge(S("pT_ok"), 2)
            for m_ in range(KC):
                if m_ >= 2:
                    pe.wait_ge(S("pw_ev"), m_ - 1)
                for c in range(2):
                    last = mm(PS[m_ % 2][:, 0:NT], wple[:, c, m_ * P:(m_ + 1) * P], pT[:, c, :],
                              start=c == 0, stop=c == 1)
                last.then_inc(S("pw_mm"), 1)
            pe.wait_ge(S("sel_ok"), 3)
            for i, (t0, n) in enumerate(TILES):
                for j in range(i):
                    mm(PS[4][0:n, i * E:(i + 1) * E], ones[:, 0:n], selm[:, j, :], start=j == 0, stop=False)
                last = mm(PS[4][0:n, i * E:(i + 1) * E], tri_before[0:n, 0:n], selm[0:n, i, :],
                          start=i == 0, stop=True)
            for j, (t0, n) in enumerate(TILES):
                last = mm(PS[4][0:XMAX, 128:128 + E], ones[0:n, 0:XMAX], selm[0:n, j, :], start=j == 0, stop=j == 2)
            for i, (t0, n) in enumerate(TILES):
                last = tr(PS[5][0:E, t0:t0 + n], gate[0:n, i, :], ident[0:n, 0:n])
            last.then_inc(S("pe_stage"), once("pe_stage", "rk_mm"))
            pe.wait_ge(S("dve_stage"), AT["tot_ok"])
            mm(PS[7][:, 0:2 * XMAX + 1], ones[0:XMAX, :], dgl, start=True, stop=True).then_inc(S("pe_stage"), once("pe_stage", "tot_mm"))
            pe.wait_ge(S("act_stage"), AT["gT_ok"])
            pe.wait_ge(S("pw_ev"), KC)
            for c in range(KC):
                if c >= 2:
                    pe.wait_ge(S("bd_ev"), c - 1)
                mm(PS[c % 2][:, 0:NT], bdn[:, c * P:(c + 1) * P], gT[0:E, :], start=True, stop=True)\
                    .then_inc(S("bd_mm"), 1)
            pe.wait_ge(S("bd_ev"), KC)
            pe.wait_ge(S("bup_in"), 16)

            def gather(n, u):
                pe.wait_ge(S("sel_e"), n + 1)
                if not (isinstance(n, int) and n == 0):
                    pe.wait_ge(S("xg_ev"), n)
                    pe.wait_ge(S("stz_ok"), n)
                for k in range(KC):
                    for i, (t0, nn) in enumerate(TILES):
                        for s in range(3):
                            last = mm(PS[2][:, k * 64:(k + 1) * 64], UB[0:nn, s, i, k * P:(k + 1) * P],
                                      SB[0:nn, u, i, :], start=(i == 0 and s == 0), stop=(i == 2 and s == 2))
                last.then_inc(S("xg_mm"), 1)
                for i, (t0, nn) in enumerate(TILES):
                    last = tr(PS[5][:, t0:t0 + nn], SG[0:nn, u, i, :], ident[0:nn, 0:nn])
                last.then_inc(S("st_mm"), 1)

            def up(n, u, first):
                pe.wait_ge(S("xg_ev"), n + 1)
                if not first:
                    pe.wait_ge(S("h_read"), n)
                for k in range(KC):
                    pe.wait_ge(S(f"w_land{k}"), 16 * n + 16)
                    for q in range(2):
                        for hf in range(2):
                            last = mm(PS[q][64 * hf:64 * hf + 64, :], XTe[:, u, k * 64:(k + 1) * 64],
                                      ring[:, k, q * 1024 + hf * 512:q * 1024 + hf * 512 + 512],
                                      start=k == 0, stop=False, tile_position=(0, 64 * hf))
                    last.then_inc(S("w_used"), 1)
                for q in range(2):
                    for hf in range(2):
                        last = mm(PS[q][64 * hf:64 * hf + 64, :], sel32[0:E, u, :],
                                  bup[:, q * 1024 + hf * 512:q * 1024 + hf * 512 + 512],
                                  start=False, stop=True)
                last.then_inc(S("up_mm"), 1)

            def down(n, u, first):
                pe.wait_ge(S("act_ok"), n + 1)
                for j in range(4):
                    last = tr(PS[3][:, j * P:(j + 1) * P], a3[:, j * P:(j + 1) * P], ident[:, :])
                last.then_inc(S("at_mm"), 1)
                pe.wait_ge(S("at_ev"), n + 1)
                if not first:
                    pe.wait_ge(S("yg_ev"), n)
                for kk in range(KC):
                    if kk % 2 == 0:
                        pe.wait_ge(S(f"w_land{8 + kk // 2}"), 16 * n + 16)
                    for dh in range(2):
                        last = mm(PS[4][64 * dh:64 * dh + 64, :],
                                  AT2[:, (kk % 4) * P + (kk // 4) * 64:(kk % 4) * P + (kk // 4) * 64 + 64],
                                  ring[:, 8 + kk // 2, (kk % 2) * 1024 + dh * 512:(kk % 2) * 1024 + dh * 512 + 512],
                                  start=kk == 0, stop=kk == KC - 1, tile_position=(0, 64 * dh))
                    if kk % 2:
                        last.then_inc(S("w_used"), 1)

            def scatter(n, u, first):
                pe.wait_ge(S("yg_ev"), n + 1)
                pe.wait_ge(S("stz_ok"), n + 1)
                for c in range(KC):
                    if not (first and c < 2):
                        pe.wait_ge(S("y_add"), KC * n + c - 1)
                    last = mm(PS[6 + c % 2][:, 0:NT], YG[:, (c % 4) * P:(c % 4) * P + P], STz[:, u, c // 4, :],
                              start=True, stop=True)
                    last.then_inc(S("y_mm"), 1)

            def experts(base, i, first, last):
                for u in range(2):
                    n = base + 2 * i + u
                    z0 = isinstance(n, int) and n == 0
                    up(n, u, z0)
                    if not (last and u == 1):
                        gather(n + 1, 1 - u)
                    if not (first and u == 0):
                        scatter(n - 1, 1 - u, isinstance(n, int) and n == 1)
                    down(n, u, z0)

            def moe_pass(base):
                gather(base, 0)
                experts(base, 0, True, False)
                with pe.Fori(1, PAIRS - 1) as i:
                    experts(base, i, False, False)
                experts(base, PAIRS - 1, False, True)
                scatter(base + E - 1, 1, False)

            moe_pass(0)
            with further(pe) as x:
                gather(E + x, 0)
                up(E + x, 0, False)
                down(E + x, 0, False)
                scatter(E + x, 0, False)

            pe.wait_ge(S("dve_stage"), AT["moe_done"])
            pe.wait_ge(S("wg_in"), 16)
            for m_ in range(KC):
                if m_ >= 2:
                    pe.wait_ge(S("sg_ev"), m_ - 1)
                for c in range(KC):
                    last = mm(PS[m_ % 2][:, 0:NT], wgate[:, c, m_ * P:(m_ + 1) * P], xT[:, c, :],
                              start=c == 0, stop=c == KC - 1)
                last.then_inc(S("sg_mm"), 1)
            rms_sum(2 * KC)
            pe.wait_ge(S("u_ready"), 3 * KC)
            pe.wait_ge(S("sg_ev"), KC)
            q = 0
            for i, (t0, n) in enumerate(TILES):
                for half in range(2):
                    if q >= 2:
                        pe.wait_ge(S("yo_lo" if q % 2 == 0 else "yo_hi"), q // 2)
                    for c in range(4):
                        last = tr(PS[q % 2][0:n, c * P:(c + 1) * P], uT[:, 4 * half + c, t0:t0 + n], ident[:, :])
                    last.then_inc(S("yo_mm"), 1)
                    q += 1

        @block.scalar
        def _(act):
            a = Chain(act, achain)
            A = act.activation

            def root(out, in_, width):
                return A(out, in_, ACT.Sqrt, bias=eps[0:out.shape[0]], scale=1.0 / width)

            act.wait_ge(S("const_a"), 1)
            act.wait_ge(S("dve_stage"), AT["lb_in"])
            A(lbt[:, 0:2, :], lbt[:, 0:2, :], ACT.Exp).then_inc(S("act_stage"), once("act_stage", "lb_exp"))
            for c in range(KC):
                act.wait_ge(S("xt_mm"), c + 1)
                A(xT[:, c, :], PS[c % 4][:, 0:NT], ACT.Copy).then_inc(S("xt_ev"), 1)
            act.wait_ge(S("sq_used"), KC)
            root(rt[:, 0, :], PS[4][:, 0:NT], D).then_inc(S("rt_ok"), 1)
            def block_quarter(n, m):
                q = 4 * n + m
                act.wait_ge(S("pt_mm"), q + 1)
                A(PT[:, 4 * ORDER[n] + m, :], PS[q % 2][:, 0:NT], ACT.Copy).then_inc(S("pt_ev"), 1)
                if n in (3, 4) and m == 3:
                    act.dma_start(wview(n + 2), w_in_c[:, :, 512 * ORDER[n + 2]:512 * ORDER[n + 2] + 512])\
                       .then_inc(S(f"w_in{n + 2}"), 16)
                if n == 5 and m == 3:
                    act.dma_start(stt, state_hgrn[0].rearrange("b h k v -> k b h v")).then_inc(S("st_in"), 16)

            for n in range(3):
                for m in range(4):
                    block_quarter(n, m)
                    if n == 2 and m == 0:
                        act.wait_ge(S("dve_stage"), AT["ff_na"])
                        A(fft[:, 1, :], fft[:, 1, :], ACT.Exp).then_inc(S("act_stage"), once("act_stage", "ff_exp"))
                        act.wait_ge(S("dve_stage"), AT["ff_w"])
                        A(fft[:, 3, :], fft[:, 2, :], ACT.Ln).then_inc(S("act_stage"), once("act_stage", "ff_ln"))
            for h in range(FH):
                act.wait_ge(S("lr_mm"), h + 1)
                A(Lrow[:, h, :, :], PS[6 + h % 2][:, 0:2 * P].rearrange("p (a b) -> p a b", a=2), ACT.Copy)\
                    .then_inc(S("lr_ev"), 1)
            act.wait_ge(S("pe_stage"), AT["snew_mm"])
            A(snew[:, :], PS[4][:, 0:B], ACT.Copy, scale=SCALE)\
                .then_inc(S("act_stage"), once("act_stage", "snew_ok"))
            for q in range(2):
                act.wait_ge(S("sf_mm"), q + 1)
                A(SF[:, 4 * q:4 * q + 4, :], PS[6 + q][:, :].rearrange("p (h g) -> p h g", h=4), ACT.Copy)\
                    .then_inc(S("sf_ok"), 1)

            def seq_q(b):
                act.wait_ge(S("qb_mm"), b + 1)
                if b >= 2:
                    act.wait_ge(S("k_mul"), CK * (b - 1))
                A(qb[:, b % 2, :], PS[2][:, :], ACT.Copy).then_inc(S("qb_ok"), 1)

            def seq_exp(b):
                act.wait_ge(S("z_ok"), b + 1)
                if b:
                    act.wait_ge(S("v_land_used"), CK * b)
                A(P32[:, :, :, :], zrep(z), ACT.Exp).then_inc(S("p_ok"), 1)
                A(pnew, snew[:, b:b + 1], ACT.Exp, bias=mcol_neg).then_inc(S("pn_ok"), 1)

            def seq_out(b):
                act.wait_ge(S("fo_mm"), b + 1)
                A(PT[:, FQ:FQ + FC, b + T:b + T + 1], PS[3][:, 140:140 + FC].rearrange("p (c a) -> p c a", a=1),
                  ACT.Copy).then_inc(S("fo_ev"), 1)

            def fox_a(h):
                act.wait_ge(S("fx_max"), h + 1)
                if h:
                    act.wait_ge(S("fx_tr"), h)
                A(pp[:, 0:P], zz[:, 0:P], ACT.Exp, bias=small[:, 100:101], accum_out=small[:, 102:103])
                A(pp[:, P:3 * P], zz[:, P:3 * P], ACT.Exp, bias=small[:, 101:102], accum_out=small[:, 103:104])\
                    .then_inc(S("fx_exp"), 1)

            def fox_b(h):
                act.wait_ge(S("fx_tr"), h + 1)
                if h:
                    act.wait_ge(S("fx_o"), h)
                A(ptr, PS[7][:, 0:3 * P], ACT.Copy).then_inc(S("fx_pt"), 1)

            def fox_c(h):
                if h % 2:
                    c = h // 2
                    act.wait_ge(S("fx_o"), h + 1)
                    A(PT[:, FQ + c, 0:T], PS[5][:, 0:T], ACT.Copy).then_inc(S("fx_o_ev"), 1)

            def gates():
                act.wait_ge(S("pt_ev"), 20)
                A(PT[:, HF:HF + 4, :], PT[:, HF:HF + 4, :], ACT.Sigmoid)\
                    .then_inc(S("act_stage"), once("act_stage", "hf_sig"))
                act.wait_ge(S("sf_ok"), 2)
                A(tmp4, PT[:, HQ:HQ + 4, :], ACT.Sigmoid).then_inc(S("silu_sig"), 1)

            def hi_nat():
                act.wait_ge(S("pt_ev"), 28)
                act.wait_ge(S("silu"), 1)
                A(tmp4, PT[:, HG:HG + 4, :], ACT.Sigmoid).then_inc(S("silu_sig"), 1)

            def hgd_b():
                act.wait_ge(S("pe_stage"), AT["st_o"])
                A(PT[:, HI:HI + HH, T:NT], PS[5][:, 0:HH * B].rearrange("p (h b) -> p h b", h=HH), ACT.Copy)\
                    .then_inc(S("act_stage"), once("act_stage", "st_o_ev"))
                act.wait_ge(S("st_new"), B)
                act.dma_start(st_s[0].rearrange("b h k v -> k b h v"), stt).then_inc(S("st_out"), 16)

            def load_w_out():
                act.wait_ge(S("st_out"), 16)
                act.dma_start(wout, wo_c).then_inc(S("w_out"), 16)

            def hg_a(h):
                if h == 0:
                    act.wait_ge(S("fx_o"), FH)
                    act.wait_ge(S("fx_tr"), FH)
                    act.wait_ge(S("dve_stage"), AT["f_ok"])
                else:
                    act.wait_ge(S("hg_A"), h)
                A(qe, PT[:, HF + h, 0:T], ACT.Ln).then_inc(S("hg_ln"), 1)
                act.wait_ge(S("hg_d"), h + 1)
                A(kd, qe, ACT.Exp, scale=-1.0).then_inc(S("act_chain"), 1)
                act.wait_ge(S("act_chain"), 3 * h + 1)
                A(qe, qe, ACT.Exp).then_inc(S("act_chain"), 1)
                A(bb, bb, ACT.Exp).then_inc(S("act_chain"), 1)
                A(ko, ko, ACT.Exp).then_inc(S("hg_exp"), 1)

            def hg_b(h):
                act.wait_ge(S("hg_koT"), h + 1)
                if h:
                    act.wait_ge(S("hg_U"), h)
                A(kn, PS[7][:, 0:T], ACT.Copy).then_inc(S("hg_kn"), 1)

            def hg_d(h):
                act.wait_ge(S("hg_o"), h + 1)
                A(PT[:, HI + h, 0:T], PS[7][:, 0:T], ACT.Copy).then_inc(S("hg_o_ev"), 1)
                if h == HH - 1:
                    act.wait_ge(S("sfin_ok"), HH)
                    act.dma_start(st_p[0, 0].rearrange("h k v -> k h v"), sfin).then_inc(S("sfin_out"), 16)

            run({"seq_q": seq_q, "seq_exp": seq_exp, "seq_out": seq_out, "block": block_quarter, "fox_a": fox_a,
                 "fox_b": fox_b, "fox_c": fox_c, "gates": gates, "hi_nat": hi_nat, "hgd_b": hgd_b,
                 "w_out": load_w_out, "hg_a": hg_a, "hg_b": hg_b, "hg_d": hg_d})
            for c in range(KC):
                act.wait_ge(S("hs_mm"), c + 1)
                if c >= 2:
                    act.wait_ge(S("hs_rstd"), c - 1)
                root(rt[:, c % 2, :], PS[c % 2][:, 0:NT], DK if c < HH else DH).then_inc(S("hs_ev"), 1)
            act.wait_ge(S("sq_used"), 2 * KC)
            act.wait_ge(S("hs_rstd"), KC)
            root(rt[:, 0, :], PS[4][:, 0:NT], D).then_inc(S("rt_ok"), 1)
            act.wait_ge(S("pe_stage"), AT["lgT_mm"])
            A(lgT[0:E, :], PS[2][0:E, 0:NT], ACT.Identity, bias=rb).then_inc(S("act_stage"), once("act_stage", "lgT_ok"))
            for i in range(3):
                n = TILES[i][1]
                act.wait_ge(S("top_ok"), i + 1)
                A(gate[0:n, i, :], lg[0:n, i, :], ACT.Exp, bias=m8neg[0:n, i:i + 1]).then_inc(S("g_exp"), 1)
            for q in range(6):
                i, half = q // 2, q % 2
                n = TILES[i][1]
                act.wait_ge(S("un_mm"), q + 1)
                A(UB[0:n, 0, i, 512 * half:512 * half + 512], PS[q % 2][0:n, :], ACT.Copy).then_inc(S("u_hi"), 1)
            for c in range(2):
                act.wait_ge(S("pT_mm"), c + 1)
                A(pT[:, c, :], PS[5 + c][:, 0:NT], ACT.Copy).then_inc(S("pT_ok"), 1)
            for m_ in range(KC):
                act.wait_ge(S("pw_mm"), m_ + 1)
                A(pwT[:, m_, :], PS[m_ % 2][:, 0:NT], ACT.Copy).then_inc(S("pw_ev"), 1)
            act.wait_ge(S("pe_stage"), AT["rk_mm"])
            A(gT[0:E, :], PS[5][0:E, 0:NT], ACT.Copy).then_inc(S("act_stage"), once("act_stage", "gT_ok"))
            act.wait_ge(S("dve_stage"), AT["stz_zero"])

            def gathered(n, u):
                act.wait_ge(S("xg_mm"), n + 1)
                A(XTe[:, u, :], PS[2][:, :], ACT.Copy).then_inc(S("xg_ev"), 1)

            def turned(n, u, first, after=None):
                act.wait_ge(S("st_mm"), n + 1)
                if not first:
                    act.wait_ge(S("y_mm"), KC * (n - 1 if after is None else after))
                A(STz[0:64, u, 0, :], PS[5][0:64, 0:NT], ACT.Copy)
                A(STz[64:128, u, 1, :], PS[5][64:128, 0:NT], ACT.Copy).then_inc(S("stz_ok"), 1)

            def experts(base, i, first, last):
                for u in range(2):
                    n = base + 2 * i + u
                    z0 = isinstance(n, int) and n == 0
                    act.wait_ge(S("glu_ok"), n + 1)
                    A(a3, a1, ACT.Sigmoid, scale=1.702).then_inc(S("sig_ok"), 1)
                    if not (last and u == 1):
                        gathered(n + 1, 1 - u)
                        turned(n + 1, 1 - u, z0)
                    act.wait_ge(S("at_mm"), n + 1)
                    A(AT2, PS[3][:, :], ACT.Copy).then_inc(S("at_ev"), 1)
                    act.wait_ge(S("w_used"), 12 * n + 12)
                    if not z0:
                        act.wait_ge(S("y_mm"), KC * n)
                    A(YG, PS[4][:, :], ACT.Copy).then_inc(S("yg_ev"), 1)

            def moe_pass(base):
                gathered(base, 0)
                turned(base, 0, isinstance(base, int))
                experts(base, 0, True, False)
                with act.Fori(1, PAIRS - 1) as i:
                    experts(base, i, False, False)
                experts(base, PAIRS - 1, False, True)

            moe_pass(0)
            with further(act) as x:
                n = E + x
                gathered(n, 0)
                turned(n, 0, False, after=n)
                act.wait_ge(S("glu_ok"), n + 1)
                A(a3, a1, ACT.Sigmoid, scale=1.702).then_inc(S("sig_ok"), 1)
                act.wait_ge(S("at_mm"), n + 1)
                A(AT2, PS[3][:, :], ACT.Copy).then_inc(S("at_ev"), 1)
                act.wait_ge(S("w_used"), 12 * n + 12)
                act.wait_ge(S("y_mm"), KC * n)
                A(YG, PS[4][:, :], ACT.Copy).then_inc(S("yg_ev"), 1)
            act.wait_ge(S("dve_stage"), AT["moe_done"])
            for m_ in range(KC):
                act.wait_ge(S("sg_mm"), m_ + 1)
                A(sgT[:, m_, :], PS[m_ % 2][:, 0:NT], ACT.Sigmoid).then_inc(S("sg_ev"), 1)
            act.wait_ge(S("sq_used"), 3 * KC)
            root(rt[:, 0, :], PS[4][:, 0:NT], D).then_inc(S("rt_ok"), 1)
            for q in range(1, 6, 2):
                i, half = q // 2, q % 2
                n = TILES[i][1]
                act.wait_ge(S("yo_mm"), q + 1)
                A(yout[0:n, i, 512:1024], PS[1][0:n, :], ACT.Copy).then_inc(S("yo_hi"), 1)

        @block.vector
        def _(dve):
            d = Chain(dve, dchain)

            def head_scale(c):
                dve.wait_ge(S("hs_ev"), c + 1)
                d(dve.reciprocal(rstd[:, :], rt[:, c % 2, :]))
                mc = PT[:, mixc(c), :]
                g = (GHG + c) if c < HH else (GFOX + c - HH)
                out = STT(mc, mc, gcols[:, g:g + 1], rstd[:, :], ALU.mult, ALU.mult)
                out.then_inc(S("hs_rstd"), 1)
                dve.wait_ge(S("hs_rstd"), c + 1)
                if c < HH:
                    dve.tensor_tensor(mc, mc, PT[:, HG + c, :], ALU.mult).then_inc(S("mix_ok"), 1)
                else:
                    dve.nop().then_inc(S("mix_ok"), 1)
            TT, TS, STT, CP = dve.tensor_tensor, dve.tensor_scalar, dve.scalar_tensor_tensor, dve.tensor_copy
            M, AD, SU = ALU.mult, ALU.add, ALU.subtract

            def bcast(ap, n):
                return ap.unsqueeze(len(ap.shape)).broadcast_to(list(ap.shape) + [n])

            def squares(k, src, c):
                if k + c >= 2:
                    dve.wait_ge(S("sq_used"), k + c - 1)
                TT(sq[:, (k + c) % 2, :], src, src, M).then_inc(S("sq_ready"), 1)

            def rms(k, g):
                for c in range(KC):
                    squares(k, xT[:, c, :], c)
                dve.wait_ge(S("rt_ok"), k // KC + 1)
                d(dve.reciprocal(rstd[:, :], rt[:, 0, :]))
                for c in range(KC):
                    STT(uT[:, c, :], xT[:, c, :], gcols[:, g + c:g + c + 1], rstd[:, :], M, M)\
                        .then_inc(S("u_ready"), 1)

            dve.wait_ge(S("pe_stage"), AT["g_ready"])
            d(CP(gcols[:, :], PS[7][:, 0:40]))
            l0, l1 = gcols[:, LB0:LB0 + 4], gcols[:, LB1:LB1 + 4]
            d(TT(lbt[:, 2, :], l0, l1, ALU.max))
            TT(lbt[:, 0, :], l0, lbt[:, 2, :], SU)
            TT(lbt[:, 1, :], l1, lbt[:, 2, :], SU).then_inc(S("dve_stage"), once("dve_stage", "lb_in"))
            dve.wait_ge(S("act_stage"), AT["lb_exp"])
            d(TT(lbt[:, 2, :], lbt[:, 0, :], lbt[:, 1, :], AD))
            d(dve.reciprocal(oml, lbt[:, 2, :]))
            d(TT(lb, lbt[:, 0, :], oml, M))
            d(TS(oml, lb, -1.0, 1.0, M, AD))
            dve.wait_ge(S("xt_ev"), KC)
            rms(0, GMIX)

            dve.wait_ge(S("pe_stage"), AT["ff_mm"])
            x, e, w, l = (fft[:, i, :] for i in range(4))
            d(TS(x, PS[5][0:FH, 0:NT], ffb, None, AD))
            d(TS(w, x, -1.0, None, M))
            TT(e, x, w, ALU.min).then_inc(S("dve_stage"), once("dve_stage", "ff_na"))
            dve.wait_ge(S("act_stage"), AT["ff_exp"])
            TS(w, e, 1.0, None, AD).then_inc(S("dve_stage"), once("dve_stage", "ff_w"))
            dve.wait_ge(S("dve_stage"), AT["ff_w"])
            t1, t2 = lfT, sq[0:FH, 0, :]
            d(TS(t1, w, -1.0, None, AD))
            d(TS(t2, t1, 0.0, None, ALU.is_equal))
            d(TT(t1, t1, t2, AD))
            dve.wait_ge(S("act_stage"), AT["ff_ln"])
            d(dve.reciprocal(w, t1))
            d(TT(l, l, w, M))
            d(TT(l, l, t2, AD))
            d(TT(l, l, e, M))
            d(TS(x, x, 0.0, None, ALU.min))
            d(TT(lfT, x, l, SU))
            dve.memset(fft[:, 1, 0:T], 1.0).then_inc(S("dve_stage"), once("dve_stage", "lf_one"))
            dve.wait_ge(S("dve_stage"), AT["lf_one"])
            dve.tensor_tensor_scan(cT8, fft[:, 1, 0:T], lfT[:, 0:T], 0.0, M, AD).then_inc(S("dve_stage"), once("dve_stage", "lfT_ok"))
            TT(qkn, PT[:, FQ:FQ + 4, T:NT], PT[:, FK:FK + 4, T:NT], M)\
                .then_inc(S("dve_stage"), once("dve_stage", "qk_new"))
            dve.wait_ge(S("pe_stage"), AT["qnat_mm"])
            CP(qnat, PS[2][0:B, :]).then_inc(S("dve_stage"), once("dve_stage", "q_nat"))

            def natural(q0, dsts, banks):
                q = q0
                for dst in dsts:
                    for i, (t0, n) in enumerate(TILES):
                        dve.wait_ge(S("nat_mm"), q + 1)
                        CP(dst[0:n, i, :], PS[banks[q % 2]][0:n, :]).then_inc(S("nat_ev"), 1)
                        q += 1
                dve.wait_ge(S("nat_ev"), q)

            natural(0, (fkn, fvn), (6, 7))
            dve.nop().then_inc(S("dve_stage"), once("dve_stage", "fkv_nat"))
            dve.wait_ge(S("pe_stage"), AT["lfn_mm"])
            for i, (t0, n) in enumerate(TILES):
                CP(lfn[0:n, i, :], PS[3][0:n, i * FH:(i + 1) * FH])
            d(CP(cnat[:, :, :], PS[3][:, 32:32 + 2 * FH].rearrange("p (i h) -> p i h", i=2)))
            dve.nop().then_inc(S("dve_stage"), once("dve_stage", "lf_nat"))
            CP(lnewv, bcast(lfn[0:B, 2, :], NPAGE)).then_inc(S("dve_stage"), once("dve_stage", "lnew_cp"))
            d(TS(cT8, cT8, 1.0 / SCALE, None, M))
            dve.wait_ge(S("sf_ok"), 2)
            dve.wait_ge(S("act_stage"), AT["snew_ok"])
            dve.wait_ge(S("const_b"), 1)
            dve.wait_ge(S("const_c"), 1)

            zv = z.rearrange("p (g h) -> p g h", h=FH)
            ofm = ofmask.rearrange("p h d -> p (h d)")

            def seq_k(b, c):
                dve.wait_ge(S("k_mul"), CK * b + c + 1)
                last = dve.tensor_reduce(sc[:, 32 * c:32 * c + 32], ring[:, c, :].rearrange("p (a b) -> p a b", b=DH),
                                         AX.X, AD)
                last.then_inc(S("k_land_used"), 1)
                if c < CK - 1:
                    return
                dve.wait_ge(S("k_land_used"), CK * (b + 1))
                if b:
                    dve.wait_ge(S("p_ok"), b)
                d(STT(zv, sc.rearrange("p (g h) -> p g h", h=FH), -SCALE,
                      SF[:, :, b * NPG:(b + 1) * NPG].rearrange("p h g -> p g h"), M, AD))
                d(dve.tensor_reduce(mx, z.rearrange("p (g h) -> p h g", h=FH), AX.X, ALU.max))
                CP(mrep.rearrange("p (r h) -> p r h", h=FH), mx.unsqueeze(1).broadcast_to([P, 16, FH]))\
                    .then_inc(S("mx_ok"), 1)

            def seq_max(b):
                dve.wait_ge(S("mx_tr"), b + 1)
                if b:
                    dve.wait_ge(S("pn_ok"), b)
                d(dve.tensor_reduce(mcol, PS[3][:, 0:P], AX.X, ALU.max))
                d(TT(mcol, mcol, snew[:, b:b + 1], ALU.max))
                d(TS(mcol_neg, mcol, -1.0, None, M))
                TS(dmx[0:FH, :], ident[0:FH, 0:FH], mcol_neg[0:FH, :], None, M).then_inc(S("dm_ok"), 1)

            def seq_exp(b):
                dve.wait_ge(S("mb_mm"), b + 1)
                TT(zv, zv, PS[3][:, 128:128 + FH].unsqueeze(1).broadcast_to([P, NPG, FH]), AD)\
                    .then_inc(S("z_ok"), 1)

            def seq_pv(b):
                dve.wait_ge(S("p_ok"), b + 1)
                d(dve.tensor_reduce(lsum, P32[:, :, 0, :].rearrange("p g h -> p h g"), AX.X, AD))
                CP(lrep.rearrange("p (r h) -> p r h", h=FH), lsum.unsqueeze(1).broadcast_to([P, 16, FH]))\
                    .then_inc(S("lp_ok"), 1)

            def seq_out(b):
                dve.wait_ge(S("l_mm"), b + 1)
                dve.wait_ge(S("pn_ok"), b + 1)
                d(TT(ltot, PS[3][:, 136:137], pnew, AD))
                d(dve.reciprocal(rl, ltot))
                d(TT(pnr, pnew, rl, M))
                dve.wait_ge(S("v_land_used"), CK * (b + 1))
                if b:
                    dve.wait_ge(S("fo_mm"), b)
                STT(of, PS[4][:, :], rl, ofm, M, M)
                dve.wait_ge(S("vb2_mm"), b + 1)
                d(STT(of2[0:FH, :], PS[2][0:FH, :], pnr[0:FH, :], ofm[0:FH, :], M, M))
                TT(of[0:FH, :], of[0:FH, :], of2[0:FH, :], SU).then_inc(S("of_ok"), 1)

            nm, ls, rs = small[:, 100:102], small[:, 102:104], small[:, 104:106]
            mxs = small[:, 106:108]

            def fox_a(h):
                dve.wait_ge(S("fx_s"), h + 1)
                if h:
                    dve.wait_ge(S("fx_exp"), h)
                TS(zz[:, 0:P], PS[6][:, 0:P], SCALE, cnat[:, 0, h:h + 1], M, AD)
                TS(zz[:, P:3 * P], PS[6][:, P:3 * P], SCALE, cnat[:, 1, h:h + 1], M, AD).then_inc(S("fx_z"), 1)
                dve.wait_ge(S("fx_z"), h + 1)
                for z_ in (zz[:, 0:P], zz[:, 2 * P:3 * P]):
                    d(TT(z_, z_, cmask[:, :], AD))
                dve.tensor_reduce(mxs[:, 0:1], zz[:, 0:P], AX.X, ALU.max)
                d(dve.tensor_reduce(mxs[:, 1:2], zz[:, P:3 * P], AX.X, ALU.max))
                TS(nm, mxs, -1.0, None, M).then_inc(S("fx_max"), 1)

            def fox_b(h):
                dve.wait_ge(S("fx_exp"), h + 1)
                d(dve.reciprocal(rs, ls))
                TS(pp[:, 0:P], pp[:, 0:P], rs[:, 0:1], None, M)
                TS(pp[:, P:3 * P], pp[:, P:3 * P], rs[:, 1:2], None, M).then_inc(S("fx_p"), 1)

            def gates():
                dve.wait_ge(S("act_stage"), AT["hf_sig"])
                for h in range(HH):
                    last = TS(PT[:, HF + h, :], PT[:, HF + h, :], oml[:, h:h + 1], lb[:, h:h + 1], M, AD)
                last.then_inc(S("dve_stage"), once("dve_stage", "f_ok"))
                dve.wait_ge(S("dve_stage"), AT["f_ok"])
                d(TS(knew, PT[:, HF:HF + HH, T:NT], -1.0, 1.0, M, AD))
                dve.wait_ge(S("silu_sig"), 1)
                TT(PT[:, HQ:HQ + 4, :], PT[:, HQ:HQ + 4, :], tmp4, M).then_inc(S("silu"), 1)

            def hi_nat():
                natural(6, (hin,), (0, 1))
                dve.wait_ge(S("silu_sig"), 2)
                TT(PT[:, HG:HG + 4, :], PT[:, HG:HG + 4, :], tmp4, M).then_inc(S("silu"), 1)
                dve.wait_ge(S("silu"), 2)

            def hgd_a():
                dve.wait_ge(S("st_in"), 16)
                dve.wait_ge(S("fx_o"), FH)
                for b in range(B):
                    dve.wait_ge(S("vb_mm"), b + 1)
                    kb = knew[:, :, b:b + 1].broadcast_to([P, HH, DK])
                    fb = PT[:, HF:HF + HH, T + b:T + b + 1].broadcast_to([P, HH, DK])
                    t = av(512 + 512 * (b % 2), 512).rearrange("p (h v) -> p h v", h=HH)
                    TT(t, PS[b % 2][:, :].rearrange("p (h v) -> p h v", h=HH), kb, M).then_inc(S("vb_used"), 1)
                    d(TT(stt[:, b, :, :], stt[:, b, :, :], fb, M))
                    dve.wait_ge(S("vb_used"), b + 1)
                    TT(stt[:, b, :, :], stt[:, b, :, :], t, SU).then_inc(S("st_new"), 1)
                dve.wait_ge(S("st_new"), B)

            def chunks(t):
                return t.rearrange("p (c r) -> p c r", r=CH)

            def hg_a(h):
                if h == 0:
                    d(dve.memset(St[:, 0, :], 0.0))
                dve.wait_ge(S("hg_ln"), h + 1)
                d(dve.tensor_tensor_scan(bb, reset[:, :], qe, 0.0, M, AD))
                mid = chunks(bb)[:, :, CH // 2 - 1:CH // 2].broadcast_to([P, NCH, CH])
                end = chunks(bb)[:, :, CH - 1:CH].broadcast_to([P, NCH, CH])
                d(TT(chunks(qe), chunks(bb), mid, SU))
                if h:
                    dve.wait_ge(S("hg_koT"), h)
                TT(chunks(ko), end, chunks(bb), SU)
                d(TS(qe, qe, 80.0, -80.0, ALU.min, ALU.max))
                TS(kh, PT[:, HF + h, 0:T], -1.0, 1.0, M, AD).then_inc(S("hg_d"), 1)
                dve.wait_ge(S("hg_exp"), h + 1)
                dve.wait_ge(S("hg_d"), h + 1)
                if h:
                    dve.wait_ge(S("hg_o"), h)
                qh = PT[:, HQ + h, 0:T]
                TT(qe, qh, qe, M)
                TT(kd, kh, kd, M)
                TT(qi, qh, bb, M)
                TT(ko, kh, ko, M).then_inc(S("hg_qk"), 1)

            def hg_b(h):
                dve.wait_ge(S("hg_A"), h + 1)
                for i in range(NTILE):
                    last = TT(ats[:, i * P:(i + 1) * P], PS[6][:, i * P:(i + 1) * P], hmask[:, :], M)
                last.then_inc(S("hg_ats"), 1)

            def hg_c(h):
                dve.wait_ge(S("hg_U"), h + 1)
                for c in range(NCH):
                    U = PS[(0, 1, 5, 6)[c % 4]][:, (c // 4) * P:(c // 4 + 1) * P]
                    dst = St[:, c + 1, :] if c < NCH - 1 else sfin[:, h, :]
                    last = STT(dst, St[:, c, :], bb[:, c * CH + CH - 1:c * CH + CH], U, M, AD)
                    if c < NCH - 1:
                        d(last)
                last.then_inc(S("hg_S"), 1)
                dve.wait_ge(S("hg_S"), h + 1)
                dve.nop().then_inc(S("sfin_ok"), 1)

            run({"seq_k": seq_k, "seq_max": seq_max, "seq_exp": seq_exp, "seq_pv": seq_pv, "seq_out": seq_out,
                 "fox_a": fox_a, "fox_b": fox_b, "gates": gates, "hi_nat": hi_nat, "hgd_a": hgd_a,
                 "hg_a": hg_a, "hg_b": hg_b, "hg_c": hg_c})

            dve.wait_ge(S("fo_ev"), B)
            for c in range(KC):
                mc = PT[:, mixc(c), :]
                if c >= 2:
                    dve.wait_ge(S("hs_mm"), c - 1)
                TT(sq[:, c % 2, :], mc, mc, M).then_inc(S("hs_ready"), 1)
                if c:
                    head_scale(c - 1)
            head_scale(KC - 1)
            for m_ in range(KC):
                dve.wait_ge(S("h_mm"), m_ + 1)
                TT(xT[:, m_, :], xT[:, m_, :], PS[m_ % 2][:, 0:NT], AD).then_inc(S("h_ev"), 1)
            dve.wait_ge(S("h_ev"), KC)
            dve.wait_ge(S("hs_mm"), KC)
            rms(KC, GMLP)
            dve.wait_ge(S("pe_stage"), AT["lg_mm"])
            for i, (t0, n) in enumerate(TILES):
                L = lg[0:n, i, :]
                r0, r1, r2, r3 = (rt4[0:n, k, :] for k in range(4))
                d(CP(L, PS[3][0:n, i * E:(i + 1) * E]))
                d(dve.max(m8[0:n, i, :], L))
                TS(m8neg[0:n, i:i + 1], m8[0:n, i, 0:1], -1.0, None, M).then_inc(S("top_ok"), 1)
                d(TS(r0, L, m8[0:n, i, 3:4], None, ALU.is_gt))
                d(dve.tensor_reduce(cnt[0:n, 0:1], r0, AX.X, AD))
                TS(r1, L, m8[0:n, i, 3:4], None, ALU.is_equal)
                d(dve.memset(r3, 1.0))
                d(dve.tensor_tensor_scan(r2, r3, r1, 0.0, M, AD))
                d(TS(r2, r2, cnt[0:n, 0:1], float(TOPK), AD, ALU.is_le))
                d(TT(r1, r1, r2, M))
                TT(selm[0:n, i, :], r0, r1, AD).then_inc(S("sel_t"), 1)
                dve.wait_ge(S("sel_t"), i + 1)
                dve.wait_ge(S("g_exp"), i + 1)
                G = gate[0:n, i, :]
                d(TT(G, G, selm[0:n, i, :], M))
                d(dve.tensor_reduce(cnt[0:n, 1:2], G, AX.X, AD))
                d(dve.reciprocal(cnt[0:n, 2:3], cnt[0:n, 1:2]))
                TS(G, G, cnt[0:n, 2:3], None, M).then_inc(S("sel_ok"), 1)
            for q in range(6):
                i, half = q // 2, q % 2
                n = TILES[i][1]
                src = PS[q % 2][0:n, :]
                c0 = 512 * half
                dve.wait_ge(S("u_hi"), q + 1)
                hi_, mi_, lo_ = (UB[0:n, s, i, c0:c0 + 512] for s in range(3))
                TT(a1[0:n, :], src, hi_, SU).then_inc(S("un_ev"), 1)
                dve.wait_ge(S("un_ev"), q + 1)
                d(CP(mi_, a1[0:n, :]))
                d(TT(lo_, a1[0:n, :], mi_, SU))
            dve.wait_ge(S("pe_stage"), AT["rk_mm"])
            d(dve.memset(RG[:, :, :], -1.0))
            for i, (t0, n) in enumerate(TILES):
                d(STT(rk[0:n, i, :], PS[4][0:n, i * E:(i + 1) * E], 1.0, selm[0:n, i, :], AD, M))
                d(TS(RG[0:n, :, i], rk[0:n, i, :], -1.0, None, AD))
                d(CP(RG[0:n, :, 3 + i], gate[0:n, i, :]))
            for k in range(NBLK):
                TS(flag[:, E * k:E * k + E], PS[4][0:XMAX, 128:128 + E], float(SLOTS * (k + 1)), None, ALU.is_gt)
            d(dve.memset(hit, 1.0))
            d(dve.tensor_tensor_scan(pos, hit, flag, 0.0, M, AD))
            d(TS(hit, pos, order_no[0:XMAX, :], None, ALU.is_equal))
            d(TT(hit, hit, flag, M))
            dve.wait_ge(S("codes_ok"), 1)
            for w in range(2):
                d(TT(flag, hit, codes[:, w * E * NBLK:(w + 1) * E * NBLK], M))
                d(dve.tensor_reduce(found[:, w:w + 1], flag, AX.X, AD))
            d(CP(found[:, 2:3], pos[:, E * NBLK - 1:E * NBLK]))
            for w in range(2):
                d(TS(dgl[:, 1 + w * XMAX:1 + (w + 1) * XMAX], ident[0:XMAX, 0:XMAX], found[:, w:w + 1], None, M))
            TS(dgl[:, 0:1], ident[0:XMAX, 0:1], found[:, 2:3], None, M).then_inc(S("dve_stage"), once("dve_stage", "tot_ok"))
            dve.wait_ge(S("pe_stage"), AT["tot_mm"])
            d(CP(xlist, PS[7][:, 0:2 * XMAX + 1]))
            CP(xint, xlist[0:1, 0:XMAX + 1]).then_inc(S("dve_stage"), once("dve_stage", "list_ok"))
            for c in range(KC):
                dve.wait_ge(S("bd_mm"), c + 1)
                TT(xT[:, c, :], xT[:, c, :], PS[c % 2][:, 0:NT], AD).then_inc(S("bd_ev"), 1)
            dve.wait_ge(S("sfin_out"), 16)
            dve.memset(STz[:, :, :, :], 0.0).then_inc(S("dve_stage"), once("dve_stage", "stz_zero"))

            SEL_STEPS, ACT_STEPS = 1, 1

            def choose(n, e, u, first, after=None, start=None):
                if not first:
                    k = n - 1 if after is None else after
                    dve.wait_ge(S("xg_mm"), k)
                    dve.wait_ge(S("st_mm"), k)
                    dve.wait_ge(S("up_mm"), k)
                d(CP(cur[:, u, :], RG[:, ds(e, 1), :].rearrange("p a r -> p (a r)")))
                if start is not None:
                    d(CP(first_rank, start))
                    d(TS(cur[:, u, 0:3], cur[:, u, 0:3], first_rank, None, SU))
                CP(sel32[0:E, u, :], ident[0:E, ds(e, 1)].broadcast_to([E, 64]))
                for i, (t0, nn) in enumerate(TILES):
                    TS(SB[0:nn, u, i, :], slot_no[0:nn, 0:64], cur[0:nn, u, i:i + 1], None, ALU.is_equal)
                    last = TS(SG[0:nn, u, i, :], slot_no[0:nn, :], cur[0:nn, u, i:i + 1],
                              cur[0:nn, u, 3 + i:4 + i], ALU.is_equal, M)
                last.then_inc(S("sel_e"), 1)

            def swiglu(n):
                dve.wait_ge(S("up_mm"), n + 1)
                TS(a1, PS[0][:, :], LIMIT, None, ALU.min).then_inc(S("glu_ok"), 1)
                TS(a2, PS[1][:, :], LIMIT, -LIMIT, ALU.min, ALU.max).then_inc(S("h_read"), 1)
                dve.wait_ge(S("h_read"), n + 1)
                d(STT(a2, a2, 1.0, a1, AD, M))
                dve.wait_ge(S("sig_ok"), n + 1)
                TT(a3, a3, a2, M).then_inc(S("act_ok"), 1)

            def add_up(n):
                for c in range(KC):
                    dve.wait_ge(S("y_mm"), KC * n + c + 1)
                    TT(xT[:, c, :], xT[:, c, :], PS[6 + c % 2][:, 0:NT], AD).then_inc(S("y_add"), 1)

            def experts(base, i, first, last):
                for u in range(2):
                    n = base + 2 * i + u
                    if not (last and u == 1):
                        choose(n + 1, 2 * i + u + 1, 1 - u, isinstance(n, int) and n == 0)
                    swiglu(n)
                    if not (first and u == 0):
                        add_up(n - 1)

            def moe_pass(base):
                choose(base, 0, 0, isinstance(base, int))
                experts(base, 0, True, False)
                start, off = d.n, d.off
                with dve.Fori(1, PAIRS - 1) as i:
                    d.off = off + (i - 1) * 4
                    experts(base, i, False, False)
                assert d.n - start == 4
                d.n, d.off = start + 4 * (PAIRS - 2), off
                experts(base, PAIRS - 1, False, True)
                add_up(base + E - 1)

            moe_pass(0)
            start = d.n
            with further(dve) as x:
                d.off = x * 4
                n = E + x
                e = dve.value_load(xint[0:1, ds(x + 1, 1)], min_val=0, max_val=E - 1)
                choose(n, e, 0, False, after=n, start=xlist[:, ds(x + (1 + XMAX), 1)])
                swiglu(n)
                add_up(n)
            assert d.n - start == 4, d.n - start
            d.sem, d.n, d.off = S("dve_chain_tail"), 0, 0
            dve.memset(small[:, 110:111], 0.0).then_inc(S("dve_stage"), once("dve_stage", "moe_done"))
            for m_ in range(KC):
                dve.wait_ge(S("sg_ev"), m_ + 1)
                TT(sgT[:, m_, :], sgT[:, m_, :], pwT[:, m_, :], M).then_inc(S("sp_ok"), 1)
                dve.wait_ge(S("sp_ok"), m_ + 1)
                if m_ == KC - 1:
                    dve.wait_ge(S("sg_mm"), KC)
            for m_ in range(KC):
                last = TT(xT[:, m_, :], xT[:, m_, :], sgT[:, m_, :], AD)
            d(last)
            rms(2 * KC, GFIN)
            for q in range(0, 6, 2):
                i = q // 2
                n = TILES[i][1]
                dve.wait_ge(S("yo_mm"), q + 1)
                CP(yout[0:n, i, 0:512], PS[0][0:n, :]).then_inc(S("yo_lo"), 1)


_INS = ['x_prompt', 'x_sample', 'state_hgrn', 'cache_k', 'cache_v', 'cache_logf', 'page_table', 'p_prompt', 'p_sample',
        'g_mix', 'w_in', 'hg_lb_logits', 'g_hg_out', 'fox_f_bias', 'g_fox_out', 'w_out', 'g_mlp', 'w_router',
        'b_router', 'w_up', 'b_up', 'w_down', 'b_down', 'w_ple', 'w_ple_gate', 'g_final']
_OUTS = [(1, 256, 1024), (8, 1, 1024), (1, 1, 4, 128, 128), (1, 1, 256, 8, 64), (1, 1, 256, 8, 64), (1, 1, 256, 8),
         (1, 8, 4, 128, 128), (1, 8, 1, 8, 64), (1, 8, 1, 8, 64), (1, 8, 1, 8)]


def kernel(**inputs):
    import numpy as _np
    import concourse.bacc as _bacc
    from concourse import mybir as _mybir
    from concourse.bass_utils import run_bass_kernel_spmd as _run

    nc = _bacc.Bacc("TRN2", target_bir_lowering=False, num_devices=1)
    arrays, args = {}, []
    for name in _INS:
        a = _np.ascontiguousarray(inputs[name])
        arrays[f"in_{name}_dram"] = a
        args.append(nc.dram_tensor(f"in_{name}_dram", a.shape, _mybir.dt.from_np(a.dtype), kind="ExternalInput").ap())
    for i, shape in enumerate(_OUTS):
        args.append(nc.dram_tensor(f"out_{i}_dram", shape, _mybir.dt.float32, kind="ExternalOutput").ap())
    hybrid_layer_kernel(nc, *args)
    r = _run(nc, [arrays], core_ids=[0])
    return tuple(r.results[0][f"out_{i}_dram"] for i in range(len(_OUTS)))
```

```python
from contextlib import ExitStack, contextmanager

import concourse.bass as bass
from concourse import mybir

F32 = mybir.dt.float32
BF16 = mybir.dt.bfloat16
I32 = mybir.dt.int32
U32 = mybir.dt.uint32
ALU = mybir.AluOpType
ACT = mybir.ActivationFunctionType
AX = mybir.AxisListType
ds = bass.ds

P = 128
EPS = 1e-6
NEG = -1.0e30
TOPK = 4
LIMIT = 7.0


class Chain:

    def __init__(self, eng, sem):
        self.eng, self.sem, self.n, self.off = eng, sem, 0, 0

    def __call__(self, ins):
        self.n += 1
        ins.then_inc(self.sem, 1)
        self.eng.wait_ge(self.sem, self.off + self.n)


def hybrid_layer_kernel(nc, x_prompt, x_sample, state_hgrn, cache_k, cache_v, cache_logf, page_table,
                        p_prompt, p_sample, g_mix, w_in, hg_lb_logits, g_hg_out, fox_f_bias, g_fox_out,
                        w_out, g_mlp, w_router, b_router, w_up, b_up, w_down, b_down, w_ple, w_ple_gate,
                        g_final, y_p, y_s, st_p, k_p, v_p, lf_p, st_s, k_s, v_s, lf_s, SLOTS=64):
    D = x_prompt.shape[2]
    T = x_prompt.shape[1]
    B = x_sample.shape[0]
    NT = T + B
    KC = D // P
    NTILE = T // P
    TILES = [(i * P, P) for i in range(NTILE)] + [(T, B)]
    HH, DK = state_hgrn.shape[2], state_hgrn.shape[3]
    FH, DH = cache_k.shape[3], cache_k.shape[4]
    FW = FH * DH
    NPG = page_table.shape[1]
    NPAGE = B * NPG
    E = w_up.shape[1]
    PLE = w_ple.shape[1]
    SCALE = float(DH) ** -0.5
    CH = 32
    NCH = T // CH
    NB = w_in.shape[2] // 512
    FC = FW // P
    HQ, HF, HI, HG, FQ, FK, FV = (4 * j for j in range(7))
    ORDER = [4, 5, 6, 1, 0, 2, 3]
    BLOCK_SLOT = [0, 2, 4, 8, 10, 8, 10]
    RING = 12
    CK = 4
    CPG = NPG // CK
    assert D == 1024 and T == 256 and B == 8 and FW == 512 and DK == P and NB == 7 and NPAGE == P

    with ExitStack() as ctx:
        def sb(name, shape, dt=F32):
            return ctx.enter_context(nc.sbuf_tensor(name, shape, dt))

        def sem(name):
            return ctx.enter_context(nc.semaphore(name))

        bank = [ctx.enter_context(nc.psum_tensor(f"bank{i}", [P, 512], F32)) for i in range(8)]

        ring = sb("ring", [P, RING, 2048])
        xT = sb("xT", [P, KC, NT])
        uT = sb("uT", [P, KC, NT])
        proj = sb("proj", [P, 28, NT])
        rows = sb("rows", [P, 3, D])
        hi_rows = sb("hi_rows", [P, 3, 512])
        arena = sb("arena", [P, 8064])

        ident = sb("ident", [P, P])
        ones = sb("ones", [P, P])
        pair_ones = sb("pair_ones", [P, P])
        hmask = sb("hmask", [P, P])
        cmask = sb("cmask", [P, P])
        tri_after = sb("tri_after", [P, P])
        tri_before = sb("tri_before", [P, P])
        later = sb("later", [P, P])
        slot_no = sb("slot_no", [P, P])
        reset = sb("reset", [P, T])
        ofmask = arena[:, 7040:7552].rearrange("p (h d) -> p h d", h=FH)
        hsel = arena[:, 7552:8064].rearrange("p (c r h) -> p c r h", c=FC, h=FH)
        negsel = sb("negsel", [B, FH, P])
        gcols = sb("gcols", [P, 40])
        small = sb("small", [P, 256])
        sq = sb("sq", [P, 2, NT])
        rt = sb("rt", [P, 2, NT])
        rstd = sb("rstd", [P, NT])
        snew = sb("snew", [P, B])
        page_i = sb("page_i", [1, NPAGE], I32)
        page_c = sb("page_c", [P, 1], I32)
        c_rows = sb("c_rows", [P, 2, FH])

        GMIX, GMLP, GFIN, GHG, GFOX, LB0, LB1 = 0, 8, 16, 24, 28, 32, 36
        eps = small[:, 0:1]
        lb = small[:, 4:8]
        oml = small[:, 8:12]
        lbt = small[:, 12:24].rearrange("p (a b) -> p a b", b=4)
        ffb = small[0:FH, 24:25]
        rb = small[0:E, 25:26]
        lf_rows = small[:, 32:56].rearrange("p (i h) -> p i h", i=3)

        sems = {}

        def S(name):
            if name not in sems:
                sems[name] = sem(name)
            return sems[name]

        STAGES = {
            "pe_stage": ["g_ready", "ff_mm", "qnat_mm", "lfn_mm", "snew_mm", "st_o", "lgT_mm", "lg_mm", "rk_mm", "tot_mm"],
            "act_stage": ["lb_exp", "ff_exp", "ff_ln", "snew_ok", "hf_sig", "st_o_ev", "lgT_ok", "gT_ok"],
            "dve_stage": ["lb_in", "ff_na", "ff_w", "lf_one", "lfT_ok", "qk_new", "q_nat", "fkv_nat", "lf_nat",
                          "lnew_cp", "c8_ok", "f_ok", "stz_zero", "tot_ok", "list_ok", "moe_done"],
        }
        AT = {name: k + 1 for names in STAGES.values() for k, name in enumerate(names)}
        told = {stage: 0 for stage in STAGES}

        def once(stage, name):
            told[stage] += 1
            assert STAGES[stage][told[stage] - 1] == name, name
            return 1

        dchain, gchain = S("dve_chain"), S("pool_chain")

        def arena_at(a, n):
            return arena[:, a:a + n]

        qe, kd, bb, ko, qi, ats, kn, kh = (arena_at(256 * i, 256) for i in range(8))
        St = arena_at(2048, 1152).rearrange("p (c v) -> p c v", v=P)
        sfin = arena_at(3200, 512).rearrange("p (h v) -> p h v", h=HH)
        tmp4 = arena_at(2048, 1056).rearrange("p (h t) -> p h t", h=HH)
        logit_p, prob_p, prob_T = arena_at(0, 512), arena_at(512, 384), arena_at(896, 384)
        later_sums = arena_at(1280, 2048).rearrange("p (h two g) -> p h two g", h=FH, two=2)
        suffix_T = arena_at(3712, 1024).rearrange("p (h g) -> p h g", h=FH)
        sc, z = arena_at(4736, 128), arena_at(4864, 128)
        page_lf = arena_at(4992, 1024)
        probs = arena_at(4992, 512).rearrange("p (g r h) -> p g r h", g=NPG, r=4)
        of = arena_at(5504, 512)
        qb = arena_at(6016, 1024).rearrange("p (u n) -> p u n", u=2)
        of2 = arena_at(7552, 512)
        states = ring[:, 8:10, :].rearrange("p a (b h v) -> p (a b) h v", h=HH, v=P)
        k_rows, v_rows = rows[:, :, 0:512], rows[:, :, 512:1024]
        q_rows = sq[0:B, :, :].rearrange("p a b -> p (a b)")[:, 0:512]
        proj_flat = proj[:, :, :].rearrange("p a b -> p (a b)")
        k_new_T = small[:, 160:192].rearrange("p (h b) -> p h b", h=HH)
        mx_rep, l_rep = rstd[:, 0:128], rstd[:, 128:256]
        mx, dmx, lsum = small[:, 192:200], small[:, 200:208], small[:, 208:216]
        mcol, pnew, ltot, rl, nrl = (small[:, 216 + i:217 + i] for i in range(5))
        qk_new = small[:, 64:96].rearrange("p (c b) -> p c b", c=4)
        mcol_neg = small[:, 221:222]
        lf_T = rt[0:FH, 1, :]
        c_T = rt[0:FH, 0, 0:T]
        ff = arena[0:FH, 0:4 * NT].rearrange("p (i t) -> p i t", i=4)
        lf_new = arena[0:B, 0:FH * NPAGE].rearrange("p (h g) -> p h g", h=FH)

        def zrep(z):
            return z.rearrange("p (g h) -> p g h", h=FH).unsqueeze(2).broadcast_to([P, NPG, 4, FH])

        def square_of(k, c):
            return arena_at(NT * c, NT) if k == 0 else sq[:, (k + c) % 2, :]

        sq4, rs4 = (arena_at(4 * NT * i, 4 * NT).rearrange("p (c t) -> p c t", c=4) for i in range(2))
        NORM_BANKS = (0, 1, 5, 6)
        UN_BANKS = (0, 1, 5, 6, 7, 2)

        def heads(k):
            base = (HI, FQ)[k]
            return proj[:, base:base + 4, :]

        def w_block(n):
            return ring[:, BLOCK_SLOT[n]:BLOCK_SLOT[n] + 2, :].rearrange("p a (c n) -> p (a c) n", n=512)

        w_ff = hi_rows[:, 2, 0:KC * FH].rearrange("p (c n) -> p c n", n=FH)
        w_out_sb = ring[:, 8:12, :].rearrange("p a (c n) -> p (a c) n", n=D)

        u_parts = proj_flat[:, 0:4608].bitcast(BF16).rearrange("p (s i d) -> p s i d", s=3, i=3)
        x_slots = proj_flat[:, 4608:5632].rearrange("p (u n) -> p u n", u=2)
        ranks_gates = proj_flat[:, 5632:5824].rearrange("p (e r) -> p e r", r=6)
        logits = proj_flat[:, 5824:5920].rearrange("p (i e) -> p i e", i=3)
        gate = proj_flat[:, 5920:6016].rearrange("p (i e) -> p i e", i=3)
        chosen = proj_flat[:, 6016:6112].rearrange("p (i e) -> p i e", i=3)
        rank = proj_flat[:, 6112:6208].rearrange("p (i e) -> p i e", i=3)
        top8 = proj_flat[:, 6208:6232].rearrange("p (i e) -> p i e", i=3)
        above = proj_flat[:, 6240:6336].rearrange("p (i e) -> p i e", i=3)
        equal, nth, restart = (proj_flat[:, 7072 + 96 * i:7168 + 96 * i].rearrange("p (i e) -> p i e", i=3) for i in range(3))
        per_token = proj_flat[:, 6368:6384]
        logits_T = proj_flat[:, 6400:6664]
        gates_rows = proj_flat[:, 6664:6928]
        cur_rank_gate = proj_flat[:, 6928:6940].rearrange("p (u r) -> p u r", u=2)
        first_rank = proj_flat[:, 6940:6941]
        slot_expert = proj_flat[:, 6944:7072].rearrange("p (u r) -> p u r", u=2)
        XMAX = NT * TOPK // SLOTS
        NBLK = (NT - 1) // SLOTS
        has_block, block_no, this_block = (hi_rows[0:XMAX, k, 0:E * NBLK] for k in range(3))
        codes = sq[0:XMAX, :, :].rearrange("p a b -> p (a b)")[:, 0:2 * E * NBLK]
        found = rstd[0:XMAX, 0:3]
        found_diag = rstd[0:XMAX, 8:8 + 2 * XMAX + 1]
        block_list = rstd[:, 128:128 + 2 * XMAX + 1]
        block_ints = small[0:1, 128:128 + XMAX + 1].bitcast(I32)
        order_no = small[:, 112:113]
        glu, lin, hidden, hidden_T, y_slots = (arena_at(512 * i, 512) for i in range(5))
        rest = (glu, lin, hidden, hidden_T, y_slots)
        gates_T = arena_at(2560, 4 * NT).rearrange("p (u d t) -> p u d t", u=2, d=2)
        slot_gate = arena_at(4672, 768).rearrange("p (u i s) -> p u i s", u=2, i=3)
        slot_token = arena_at(5440, 192).bitcast(BF16).rearrange("p (u i s) -> p u i s", u=2, i=3)
        b_up_sb = uT[:, :, :].rearrange("p a b -> p (a b)")[0:E, 0:2048]
        pw_T = rows[:, :, :].rearrange("p a b -> p (a b)")[:, 0:KC * NT].rearrange("p (c t) -> p c t", c=KC)
        w_rt = arena_at(7040, KC * E).rearrange("p (c e) -> p c e", e=E)
        b_down_sb = arena_at(6016, D)[0:E, :]
        w_ple_sb = ring[:, 3, :].rearrange("p (c n) -> p c n", n=D)
        p_rows = ring[:, 2, 0:3 * PLE].rearrange("p (i d) -> p i d", i=3)
        p_T = hi_rows[:, :, :].rearrange("p a b -> p (a b)")[:, 0:2 * NT].rearrange("p (c t) -> p c t", c=2)
        w_gate = ring[:, 0:4, :].rearrange("p a (c n) -> p (a c) n", n=D)
        sg_T = proj_flat[:, 0:KC * NT].rearrange("p (c t) -> p c t", c=KC)
        yout = proj_flat[:, 2112:2112 + 3 * D].rearrange("p (i d) -> p i d", i=3)

        w_in_c = w_in[0].rearrange("(c p) n -> p c n", p=P)
        wo_c = w_out[0].rearrange("(c p) n -> p c n", p=P)
        wg_c = w_ple_gate[0].rearrange("(c p) n -> p c n", p=P)
        PAIRS = E // 2

        HALVES = [[("block", n, m, k)] for n in range(3, NB) for m in range(4) for k in range(2)]
        HALVES[15].append(("gates",))
        HALVES[23].append(("hi_nat",))
        HALVES[31].append(("out_gate",))
        HEADS = [[(f"fox_{p}", h)] for h in range(FH) for p in "abc"]
        HEADS += [[(f"hgd_{p}", b)] for p, b in zip("aabababb", (0, 2, 0, 4, 2, 6, 4, 6))]
        HEADS[-1].append(("hg_l", 0))
        for h in range(HH):
            HEADS += [[(f"hg_{p}", h)] for p in "aebcd"]
            if h < HH - 1:
                HEADS[-2].append(("hg_l", h + 1))
        HEADS += [[("norm_a", 0)], [("norm_b", 0)], [("out_mm", 0)]]
        HEADS += [[("out_mm", m), ("out_add", m - 1)] for m in range(1, KC)] + [[("out_add", KC - 1)]]
        HEADS[HEADS.index([("hg_d", 1)])].append(("w_out",))
        TAIL = {(0, 0): "seq_max", (1, 0): "seq_exp", (2, 0): "seq_pv", (3, 0): "seq_out", (3, 1): "seq_sum"}
        STEPS = [("seq_q", 0)]
        for r_ in range(B + 1):
            for c_ in range(CK):
                if r_ < B:
                    STEPS.append(("seq_k", r_, c_))
                if c_ == 0 and r_ + 1 < B:
                    STEPS.append(("seq_q", r_ + 1))
                for k in range(2):
                    
                    if (c_, k) in TAIL and r_ and False:
                        STEPS.append((TAIL[c_, k], r_ - 1))
                    STEPS += HALVES.pop(0) if HALVES else []
                    if HEADS:
                        STEPS += HEADS.pop(0)
                    if (c_, k) in TAIL and r_ and not False:
                        STEPS.append((TAIL[c_, k], r_ - 1))
        assert not HEADS and not HALVES

        def run(parts):
            for name, *args in STEPS:
                if name in parts:
                    parts[name](*args)

        @contextmanager
        def further(eng):
            eng.wait_ge(S("dve_stage"), AT["list_ok"])
            count = eng.value_load(block_ints[0:1, 0:1], min_val=0, max_val=XMAX)
            with eng.If(count > 0):
                with eng.Fori(0, count) as x:
                    yield x

        block = ctx.enter_context(nc.Block())

        @block.sync
        def _(sp):
            def load(dst, src, s, k=16):
                sp.dma_start(dst, src).then_inc(S(s), k)

            load(rows[:, 0:2, :], x_prompt[0].rearrange("(i p) d -> p i d", p=P), "x_in")
            load(rows[0:B, 2, :], x_sample[:, 0, :], "x_in")
            for r, v in ((GMIX, g_mix[0]), (GMLP, g_mlp[0]), (GFIN, g_final), (GHG, g_hg_out[0]), (GFOX, g_fox_out[0]),
                         (LB0, hg_lb_logits[0]), (LB1, hg_lb_logits[1])):
                n = v.shape[0] // P
                load(hi_rows[r:r + n, 0, 0:P], v.rearrange("(c p) -> c p", p=P), "rows_in")
            load(ffb, fox_f_bias.rearrange("a h -> h a"), "rows_in")
            load(rb, b_router.rearrange("a h -> h a"), "rows_in")
            load(page_i[:, :], page_table.rearrange("b g -> (b g)").rearrange("(a n) -> a n", a=1), "page_in")
            load(page_c[:, :], page_table.rearrange("b g -> (b g)").rearrange("(n a) -> n a", a=1), "page_in")
            for n in range(5):
                load(w_block(n), w_in_c[:, :, 512 * ORDER[n]:512 * ORDER[n] + 512], f"w_in{n}")
                if n == 2:
                    load(w_ff, w_in_c[:, :, NB * 512:NB * 512 + FH], "wff_in")
            sp.wait_ge(S("page_in"), 32)

            def pages(cache, slot0, b, land, chunks=range(CK), first=False):
                for c in chunks:
                    _, numbers = nc.values_load_multi_w_load_instructions(
                        page_i[0:1, ds(b * NPG + c * CPG, CPG)], engines=(mybir.EngineType.SP,), min_val=0,
                        max_val=cache_k.shape[1] - 1,
                        skip_runtime_bounds_check_because="the page table holds numbers of the cache's pages")
                    for g, r in enumerate(numbers):
                        if g == 0 and first and c in (0, 2) and slot0 + c < 6:
                            sp.wait_ge(S("pt_mm"), 4 * ((slot0 + c) // 2) + 4)
                        if g == 0 and not first:
                            sp.wait_ge(S(land + "_used"), CK * b + c - CK + 1)
                        sp.dma_start(ring[:, slot0 + c, 512 * g:512 * g + 512],
                                     cache[0][ds(r, 1)].rearrange("a r h d -> r (a h d)")).then_inc(S(f"{land}{c}"), 16)

            pages(cache_k, 0, 0, "k_land", first=True)
            pages(cache_v, CK, 0, "v_land", first=True)
            sp.wait_ge(S("dve_stage"), AT["fkv_nat"])
            load(k_p[0, 0].rearrange("(i p) h d -> p i (h d)", p=P), k_rows[:, 0:2, :], "out")
            load(k_s[0, :, 0].rearrange("b h d -> b (h d)"), k_rows[0:B, 2, :], "out")
            load(v_p[0, 0].rearrange("(i p) h d -> p i (h d)", p=P), v_rows[:, 0:2, :], "out")
            load(v_s[0, :, 0].rearrange("b h d -> b (h d)"), v_rows[0:B, 2, :], "out")
            sp.wait_ge(S("dve_stage"), AT["lf_nat"])
            load(lf_p[0, 0].rearrange("(i p) h -> p i h", p=P), lf_rows[:, 0:2, :], "out")
            load(lf_s[0, :, 0], lf_rows[0:B, 2, :], "out")
            pages(cache_k, 0, 1, "k_land")
            with sp.Fori(1, B - 1) as b:
                pages(cache_k, 0, b + 1, "k_land", (0, 1, 2))
                pages(cache_v, CK, b, "v_land")
                pages(cache_k, 0, b + 1, "k_land", (3,))
            pages(cache_v, CK, B - 1, "v_land")
            def expert(src_e, n, first, s):
                if not first:
                    sp.wait_ge(S("w_used"), RING * (n - 1) + s + 1)
                if s < 8:
                    src = w_up[0][ds(src_e, 1)].rearrange("a (c p) n -> p (a c) n", p=P)[:, s, :]
                    sp.dma_start(ring[:, s, :], src).then_inc(S(f"w_land{s}"), 16)
                else:
                    j = s - 8
                    src = w_down[0][ds(src_e, 1)].rearrange("a (c p) n -> p (a c) n", p=P)[:, 2 * j:2 * j + 2, :]
                    sp.dma_start(ring[:, s, :].rearrange("p (c n) -> p c n", c=2), src)\
                      .then_inc(S(f"w_land{s}"), 16)

            sp.wait_ge(S("k_land_used"), CK * B)
            load(p_rows[:, 0:2, :], p_prompt[0, 0].rearrange("(i p) d -> p i d", p=P), "wple_in")
            load(p_rows[0:B, 2, :], p_sample[0, :, 0, :], "wple_in")
            load(w_ple_sb, w_ple[0].rearrange("(c p) n -> p c n", p=P), "wple_in")
            for s in (0, 1):
                expert(0, 0, True, s)
            sp.wait_ge(S("v_land_used"), CK * B)
            sp.wait_ge(S("fo_ev"), B)
            load(w_rt, w_router[0].rearrange("(c p) e -> p c e", p=P), "wr_in")
            load(b_down_sb, b_down[0], "wr_in")
            for s in range(4, 8):
                expert(0, 0, True, s)
            sp.wait_ge(S("pw_mm"), KC)
            for s in (2, 3):
                expert(0, 0, True, s)
            sp.wait_ge(S("h_mm"), 2 * KC)
            for s in range(8, RING):
                expert(0, 0, True, s)
            sp.wait_ge(S("un_mm"), 6)
            sp.wait_ge(S("pe_stage"), AT["lgT_mm"])
            load(b_up_sb, b_up[0], "bup_in")
            with sp.Fori(1, E) as e:
                for s in range(RING):
                    expert(e, e, False, s)
            with further(sp) as x:
                e = sp.value_load(block_ints[0:1, ds(x + 1, 1)], min_val=0, max_val=E - 1)
                for s in range(RING):
                    expert(e, E + x, False, s)
            blocks = sp.value_load(block_ints[0:1, 0:1], min_val=0, max_val=XMAX)
            sp.wait_ge(S("w_used"), (blocks + E) * RING - 4)
            load(w_gate[:, 0:4, :], wg_c[:, 0:4, :], "wg_in")
            load(w_gate[:, 4:8, :], wg_c[:, 4:8, :], "wg_in")
            for i, (t0, n) in enumerate(TILES):
                sp.wait_ge(S("yo_lo"), i + 1)
                sp.wait_ge(S("yo_hi"), i + 1)
                load(y_p[0, t0:t0 + n, :] if i < NTILE else y_s[:, 0, :], yout[0:n, i, :], "out")
            sp.wait_ge(S("out"), 16 * 9)
            sp.wait_ge(S("sfin_out"), 16)

        @block.gpsimd
        def _(gp):
            g = Chain(gp, gchain)

            def fill(t, v):
                g(gp.memset(t, v))

            def keep(t, base, cm, pattern, op=ALU.is_ge, fillv=0.0):
                g(gp.affine_select(out=t, in_=t, compare_op=op, fill=fillv, base=base, pattern=pattern,
                                   channel_multiplier=cm))

            fill(eps, EPS)
            fill(ident[:, :], 0.0)
            keep(ident[:, :], 0, 1, [[-1, P]], ALU.not_equal, 1.0)
            fill(ones[:, :], 1.0)
            gp.nop().then_inc(S("const_a"), 1)
            po = pair_ones[:, :].rearrange("p (a b) -> p a b", a=2)
            fill(po, 1.0)
            keep(po, 0, 1, [[-DH, 2], [0, DH]])
            keep(po, DH - 1, -1, [[DH, 2], [0, DH]])
            fill(hmask[:, :], 1.0)
            hm = hmask[:, :].rearrange("p (a b) -> p a b", b=CH)
            keep(hm, 0, 1, [[-CH, P // CH], [0, CH]])
            keep(hm, 0, -1, [[CH, P // CH], [1, CH]])
            fill(cmask[:, :], 0.0)
            keep(cmask[:, :], 0, 1, [[-1, P]], ALU.is_ge, NEG)
            fill(tri_after[:, :], 1.0)
            keep(tri_after[:, :], -1, 1, [[-1, P]])
            fill(tri_before[:, :], 1.0)
            keep(tri_before[:, :], -1, -1, [[1, P]])
            fill(later[:, :], 1.0)
            lt = later[:, :].rearrange("p (a b) -> p a b", b=NPG)
            keep(lt, -1, 1, [[-NPG, B], [-1, NPG]])
            keep(lt, NPG - 1, -1, [[NPG, B], [0, NPG]])
            fill(negsel[:, :, :], 0.0)
            keep(negsel[:, :, :], 0, 1, [[-1, FH], [0, P]], ALU.not_equal, -1.0)
            fill(reset[:, :], 1.0)
            fill(reset[:, :].rearrange("p (c r) -> p c r", r=CH)[:, :, 0:1], 0.0)
            g(gp.iota(slot_no[:, :], [[0, P // 64], [1, 64]], base=0, channel_multiplier=0,
                      allow_small_or_imprecise_dtypes=True))
            if SLOTS < 64:
                fill(slot_no[:, :].rearrange("p (a b) -> p a b", a=2)[:, :, SLOTS:64], -1.0e4)
            g(gp.iota(order_no, [[0, 1]], base=1, channel_multiplier=1, allow_small_or_imprecise_dtypes=True))
            gp.nop().then_inc(S("const_b"), 1)
            fill(ofmask, 0.0)
            for q in range(4):
                keep(ofmask, -CH * q, 1, [[-1, FH], [0, DH]], ALU.not_equal, 1.0)
            fill(hsel, 1.0)
            keep(hsel, 0, 1, [[P, FC], [0, 16], [-DH, FH]])
            keep(hsel, DH - 1, -1, [[-P, FC], [0, 16], [DH, FH]])
            gp.nop().then_inc(S("const_c"), 1)
            gp.wait_ge(S("page_in"), 32)
            gp.indirect_dma_start(
                page_lf, None, cache_logf[0].rearrange("n r h -> n (r h)"),
                bass.IndirectOffsetOnAxis(ap=page_c[:, :].bitcast(U32), axis=0)).then_inc(S("lf_past"), 16)
            gp.wait_ge(S("dve_stage"), AT["lnew_cp"])
            lv = lf_new.rearrange("p h (b g) -> p h b g", b=B)
            keep(lv, 0, 1, [[0, FH], [-1, B], [0, NPG]], ALU.is_equal, 0.0)
            gp.nop().then_inc(S("lnew_ok"), 1)

            def seq_k(b, c):
                if c == 0:
                    gp.wait_ge(S("qb_ok"), b + 1)
                gp.wait_ge(S(f"k_land{c}"), 16 * CPG * (b + 1))
                kv = ring[:, c, :].rearrange("p (g n) -> p g n", n=512)
                gp.tensor_tensor(kv, kv, qb[:, b % 2, :].unsqueeze(1).broadcast_to([P, CPG, 512]), ALU.mult)\
                    .then_inc(S("k_mul"), 1)

            run({"seq_k": seq_k})
            gp.wait_ge(S("u_ready"), 2 * KC)
            c4 = codes.rearrange("p (w b e) -> p w b e", w=2, e=E)
            g(gp.iota(c4[:, 0], [[0, NBLK], [1, E]], base=0, channel_multiplier=0,
                      allow_small_or_imprecise_dtypes=True))
            g(gp.iota(c4[:, 1], [[SLOTS, NBLK], [0, E]], base=SLOTS, channel_multiplier=0,
                      allow_small_or_imprecise_dtypes=True))
            gp.nop().then_inc(S("codes_ok"), 1)

        @block.tensor
        def _(pe):
            mm, tr = pe.matmul, pe.transpose

            def square_sum(k, c):
                pe.wait_ge(S("sq_ready"), k + c + 1)
                mm(bank[4][:, 0:NT], ones[:, :], square_of(k, c), start=c == 0, stop=c == KC - 1)\
                    .then_inc(S("sq_used"), 1)

            pe.wait_ge(S("const_a"), 1)
            pe.wait_ge(S("rows_in"), 16 * 9)
            tr(bank[7][:, 0:40], hi_rows[0:40, 0, 0:P], ident[0:40, 0:40]).then_inc(S("pe_stage"), once("pe_stage", "g_ready"))
            pe.wait_ge(S("x_in"), 32)
            for c in range(KC):
                if c >= 4:
                    pe.wait_ge(S("xt_ev"), c - 3)
                for i, (t0, n) in enumerate(TILES):
                    m = tr(bank[c % 4][:, t0:t0 + n], rows[0:n, i, c * P:(c + 1) * P], ident[0:n, 0:n])
                m.then_inc(S("xt_mm"), 1)
            for c in range(KC):
                square_sum(0, c)

            def block_quarter(n, m, half=None):
                q = 4 * n + m
                if half == 1:
                    parts = range(KC // 2, KC)
                else:
                    parts = range(KC // 2 if half == 0 else KC)
                if m == 0 and half != 1:
                    pe.wait_ge(S(f"w_in{n}"), 16)
                    if n == NB - 1:
                        pe.wait_ge(S("nat_ev"), 9)
                if q >= 2 and half != 1:
                    pe.wait_ge(S("pt_ev"), q - 1)
                for c in parts:
                    if q == 0:
                        pe.wait_ge(S("u_ready"), c + 1)
                    last = mm(bank[q % 2][:, 0:NT], w_block(n)[:, c, m * P:(m + 1) * P], uT[:, c, :],
                              start=c == 0, stop=c == KC - 1)
                if half != 0:
                    last.then_inc(S("pt_mm"), 1)

            for n in range(3):
                for m in range(4):
                    block_quarter(n, m)
                if n == 1:
                    pe.wait_ge(S("wff_in"), 16)
                    for c in range(KC):
                        last = mm(bank[5][0:FH, 0:NT], w_ff[:, c, :], uT[:, c, :], start=c == 0, stop=c == KC - 1)
                    last.then_inc(S("pe_stage"), once("pe_stage", "ff_mm"))

            def natural(q0, bases, banks):
                q = q0
                for base in bases:
                    for i, (t0, n) in enumerate(TILES):
                        if q - q0 >= 2:
                            pe.wait_ge(S("nat_ev"), q - 1)
                        for c in range(4):
                            m = tr(bank[banks[q % 2]][0:n, c * P:(c + 1) * P], proj[:, base + c, t0:t0 + n], ident[:, :])
                        m.then_inc(S("nat_mm"), 1)
                        q += 1

            pe.wait_ge(S("pt_ev"), 12)
            for c in range(4):
                m = tr(bank[2][0:B, c * P:(c + 1) * P], proj[:, FQ + c, T:NT], ident[:, :])
            m.then_inc(S("pe_stage"), once("pe_stage", "qnat_mm"))
            natural(0, (FK, FV), (6, 7))
            pe.wait_ge(S("dve_stage"), AT["lfT_ok"])
            for i, (t0, n) in enumerate(TILES):
                m = tr(bank[3][0:n, i * FH:(i + 1) * FH], lf_T[:, t0:t0 + n], ident[0:FH, 0:FH])
            for i in range(2):
                m = tr(bank[3][:, 32 + i * FH:32 + (i + 1) * FH], c_T[:, i * P:(i + 1) * P], ident[0:FH, 0:FH])
            m.then_inc(S("pe_stage"), once("pe_stage", "lfn_mm"))
            pe.wait_ge(S("const_b"), 1)
            pe.wait_ge(S("lf_past"), 16)
            pe.wait_ge(S("nat_ev"), 6)
            for h in range(FH):
                if h >= 2:
                    pe.wait_ge(S("lr_ev"), h - 1)
                lfh = page_lf.rearrange("p (r h) -> p h r", h=FH)[:, h, :]
                tr(bank[6 + h % 2][:, 0:P], lfh, ident[:, :])
                mm(bank[6 + h % 2][:, P:2 * P], lfh, later[:, :], start=True, stop=True).then_inc(S("lr_mm"), 1)
            pe.wait_ge(S("dve_stage"), AT["qk_new"])
            pe.wait_ge(S("const_c"), 1)
            for c in range(FC):
                m = mm(bank[4][:, 0:B], hsel[:, c, :, :].rearrange("p r h -> p (r h)"), qk_new[:, c, :],
                       start=c == 0, stop=c == FC - 1)
            m.then_inc(S("pe_stage"), once("pe_stage", "snew_mm"))
            pe.wait_ge(S("lr_ev"), FH)
            pe.wait_ge(S("lnew_ok"), 1)
            for q in range(2):
                hs = slice(4 * q, 4 * q + 4)
                O = bank[6 + q][:, :].rearrange("p (h g) -> p h g", h=4)
                mm(O, tri_after[:, :], later_sums[:, hs, 0, :], start=True, stop=False)
                mm(O, ones[:, :], later_sums[:, hs, 1, :], start=False, stop=False)
                mm(O, ones[0:B, :], lf_new[:, hs, :], start=False, stop=True).then_inc(S("sf_mm"), 1)
            pe.wait_ge(S("dve_stage"), AT["c8_ok"])
            pe.wait_ge(S("sf_ok"), 2)
            pe.wait_ge(S("act_stage"), AT["snew_ok"])

            def seq_q(b):
                if b:
                    pe.wait_ge(S("qb_ok"), b)
                mm(bank[2][:, :], negsel[:, b, :], q_rows, start=True, stop=True).then_inc(S("qb_mm"), 1)

            def seq_max(b):
                pe.wait_ge(S("mx_ok"), b + 1)
                if b:
                    pe.wait_ge(S("fo_ev"), b)
                tr(bank[3][:, 0:P], mx_rep, ident[:, :]).then_inc(S("mx_tr"), 1)

            def seq_exp(b):
                pe.wait_ge(S("dm_ok"), b + 1)
                mm(bank[3][:, 128:128 + FH], ones[0:FH, :], dmx[0:FH, :], start=True, stop=True)\
                    .then_inc(S("mb_mm"), 1)
                pe.wait_ge(S("qb_ok"), min(b + 3, B))
                mm(bank[2][:, :], negsel[:, b, :], v_rows[0:B, 2, :], start=True, stop=True).then_inc(S("vb2_mm"), 1)

            def seq_pv(b):
                pe.wait_ge(S("lp_ok"), b + 1)
                mm(bank[3][:, 136:137], l_rep, ones[:, 0:1], start=True, stop=True).then_inc(S("l_mm"), 1)
                for c in range(CK):
                    pe.wait_ge(S(f"v_land{c}"), 16 * CPG * (b + 1))
                    for g in range(CPG):
                        m = mm(bank[4][CH * g:CH * g + CH, :],
                               probs[:, c * CPG + g, :, :].rearrange("p r h -> p (r h)"),
                               ring[:, CK + c, 512 * g:512 * g + 512], start=c == 0, stop=c == CK - 1,
                               tile_position=(0, CH * g))
                    m.then_inc(S("v_land_used"), 1)

            def seq_sum(b):
                pe.wait_ge(S("of_ok"), b + 1)
                for c in range(FC):
                    m = mm(bank[3][:, 140 + c:141 + c], of[:, c * P:(c + 1) * P], ones[:, 0:1], start=True, stop=True)
                m.then_inc(S("fo_mm"), 1)

            def fox_a(h):
                c, o = h // 2, DH * (h % 2)
                if h:
                    pe.wait_ge(S("fx_z"), h)
                qh, kh_ = proj[o:o + DH, FQ + c, :], proj[o:o + DH, FK + c, :]
                for i, (a, n) in enumerate(((0, P), (P, 2 * P))):
                    mm(bank[6][:, a:a + n], qh[:, i * P:(i + 1) * P], kh_[:, 0:n], start=True, stop=False,
                       tile_position=(o, 0))
                    m = mm(bank[6][:, a:a + n], negsel[:, h, :], c_T[:, 0:n], start=False, stop=True)
                m.then_inc(S("fx_s"), 1)

            def fox_b(h):
                pe.wait_ge(S("fx_p"), h + 1)
                if h:
                    pe.wait_ge(S("fx_pt"), h)
                for k in range(3):
                    m = tr(bank[7][:, k * P:(k + 1) * P], prob_p[:, k * P:(k + 1) * P], ident[:, :])
                m.then_inc(S("fx_tr"), 1)

            def fox_c(h):
                c, o = h // 2, DH * (h % 2)
                pe.wait_ge(S("fx_pt"), h + 1)
                if h >= 2 and h % 2 == 0:
                    pe.wait_ge(S("fx_o_ev"), c)
                O = bank[5]
                v = v_rows[:, :, h * DH:(h + 1) * DH]
                mm(O[o:o + DH, 0:P], v[:, 0, :], prob_T[:, 0:P], start=True, stop=True, tile_position=(0, o))
                mm(O[o:o + DH, P:2 * P], v[:, 0, :], prob_T[:, P:2 * P], start=True, stop=False, tile_position=(0, o))
                mm(O[o:o + DH, P:2 * P], v[:, 1, :], prob_T[:, 2 * P:3 * P], start=False, stop=True,
                   tile_position=(0, o)).then_inc(S("fx_o"), 1)

            def hi_nat():
                pe.wait_ge(S("pt_ev"), 24)
                natural(6, (HI,), (0, 1))

            def hgd_a(b0):
                if b0 == 0:
                    pe.wait_ge(S("nat_ev"), 9)
                    pe.wait_ge(S("fx_z"), FH)
                    pe.wait_ge(S("fx_pt"), FH)
                for b in (b0, b0 + 1):
                    if b >= 2:
                        pe.wait_ge(S("vb_used"), b - 1)
                    mm(bank[6 + b % 2][:, :], negsel[:, b, :], hi_rows[0:B, 2, :], start=True, stop=True)\
                        .then_inc(S("vb_mm"), 1)

            def hgd_b(b0):
                if b0 == 0:
                    pe.wait_ge(S("fx_o_ev"), FC)
                for b in (b0, b0 + 1):
                    pe.wait_ge(S("st_new"), b + 1)
                    for h in range(HH):
                        m = mm(bank[5][:, h * B + b:h * B + b + 1], states[:, b, h, :], proj[:, HQ + h, T + b:T + b + 1],
                               start=True, stop=True)
                if b0 == B - 2:
                    m.then_inc(S("pe_stage"), once("pe_stage", "st_o"))

            U_BANKS = (0, 1, 5, 6)

            def hg_b(h):
                if h == 0:
                    pe.wait_ge(S("vb_used"), B)
                pe.wait_ge(S("hg_qk"), h + 1)
                if h:
                    pe.wait_ge(S("hg_S"), h)
                    pe.wait_ge(S("hg_o_ev"), h)
                for i in range(NTILE):
                    m = mm(bank[6][:, i * P:(i + 1) * P], kd[:, i * P:(i + 1) * P], qe[:, i * P:(i + 1) * P],
                           start=True, stop=True)
                m.then_inc(S("hg_A"), 1)
                for i in range(NTILE):
                    m = tr(bank[7][:, i * P:(i + 1) * P], ko[:, i * P:(i + 1) * P], ident[:, :])
                m.then_inc(S("hg_koT"), 1)

            def hg_c(h):
                if h == 0:
                    pe.wait_ge(S("act_stage"), AT["st_o_ev"])
                    pe.wait_ge(S("pt_ev"), 28)
                pe.wait_ge(S("hg_ats"), h + 1)
                pe.wait_ge(S("hg_kn"), h + 1)
                for c in range(NCH):
                    i, j = c // 4, c % 4
                    m = mm(bank[U_BANKS[j]][:, i * P:(i + 1) * P], kn[CH * j:CH * j + CH, i * P:(i + 1) * P],
                           hi_rows[CH * j:CH * j + CH, i, h * P:(h + 1) * P], start=True, stop=True,
                           tile_position=(CH * j, 0))
                m.then_inc(S("hg_U"), 1)

            def hg_d(h):
                pe.wait_ge(S("hg_S"), h + 1)
                for i in range(NTILE):
                    O = bank[7]
                    mm(O[:, i * P:(i + 1) * P], hi_rows[:, i, h * P:(h + 1) * P], ats[:, i * P:(i + 1) * P],
                       start=True, stop=False, skip_group_check=True)
                    for j in range(4):
                        c = 4 * i + j
                        if c:
                            m = mm(O[:, c * CH:(c + 1) * CH], St[:, c, :], qi[:, c * CH:(c + 1) * CH],
                                   start=False, stop=j == 3, skip_group_check=True)
                m.then_inc(S("hg_o"), 1)

            def norm_a(k):
                pe.wait_ge(S("hs_ready"), k + 1)
                for c in range(4):
                    mm(bank[NORM_BANKS[c]][:, 0:NT], pair_ones[:, :] if k else ones[:, :], sq4[:, c, :],
                       start=True, stop=True).then_inc(S("hs_mm"), 1)

            def out_mm(m_, k=0):
                q = KC * k + m_
                if m_ == 0:
                    pe.wait_ge(S("mix_ok"), 4 * k + 4)
                    pe.wait_ge(S("w_out"), 16)
                if q >= 2:
                    pe.wait_ge(S("h_ev"), q - 1)
                for c in range(4):
                    last = mm(bank[q % 2][:, 0:NT], w_out_sb[:, 4 * k + c, m_ * P:(m_ + 1) * P], heads(k)[:, c, :],
                              start=c == 0, stop=c == 3)
                last.then_inc(S("h_mm"), 1)

            def ple_t():
                pe.wait_ge(S("wple_in"), 48)
                for c in range(2):
                    for i, (t0, n) in enumerate(TILES):
                        last = tr(bank[5 + c][:, t0:t0 + n], p_rows[0:n, i, c * P:(c + 1) * P], ident[0:n, 0:n])
                    last.then_inc(S("pT_mm"), 1)

            run({"seq_q": seq_q, "seq_max": seq_max, "seq_exp": seq_exp, "seq_pv": seq_pv, "seq_sum": seq_sum,
                 "block": block_quarter, "fox_a": fox_a, "fox_b": fox_b, "fox_c": fox_c, "hi_nat": hi_nat,
                 "hgd_a": hgd_a, "hgd_b": hgd_b, "hg_b": hg_b, "hg_c": hg_c, "hg_d": hg_d, "norm_a": norm_a,
                 "out_mm": out_mm})
            pe.wait_ge(S("h_ev"), KC)
            pe.wait_ge(S("hs_ev"), 4)
            ple_t()
            pe.wait_ge(S("pT_ok"), 2)
            norm_a(1)
            for m_ in range(KC):
                if m_ >= 2:
                    pe.wait_ge(S("pw_ev"), m_ - 1)
                for c in range(2):
                    last = mm(bank[(7, 2)[m_ % 2]][:, 0:NT], w_ple_sb[:, c, m_ * P:(m_ + 1) * P], p_T[:, c, :],
                              start=c == 0, stop=c == 1)
                last.then_inc(S("pw_mm"), 1)

            pe.wait_ge(S("hs_ev"), 8)
            for m_ in range(KC):
                out_mm(m_, 1)
                if m_:
                    square_sum(KC, m_ - 1)
            square_sum(KC, KC - 1)
            pe.wait_ge(S("wr_in"), 32)
            pe.wait_ge(S("pw_ev"), KC)
            for c in range(KC):
                pe.wait_ge(S("u_ready"), KC + c + 1)
                last = mm(bank[2][0:E, 0:NT], w_rt[:, c, :], uT[:, c, :], start=c == 0, stop=c == KC - 1)
            last.then_inc(S("pe_stage"), once("pe_stage", "lgT_mm"))
            q = 0
            for i, (t0, n) in enumerate(TILES):
                for half in range(2):
                    if q == 5:
                        pe.wait_ge(S("act_stage"), AT["lgT_ok"])
                        for i_, (t0_, n_) in enumerate(TILES):
                            last = tr(bank[3][0:n_, i_ * E:(i_ + 1) * E], logits_T[0:E, t0_:t0_ + n_], ident[0:E, 0:E])
                        last.then_inc(S("pe_stage"), once("pe_stage", "lg_mm"))
                    for c in range(4):
                        last = tr(bank[UN_BANKS[q]][0:n, c * P:(c + 1) * P], uT[:, 4 * half + c, t0:t0 + n], ident[:, :])
                    last.then_inc(S("un_mm"), 1)
                    q += 1
            pe.wait_ge(S("sel_ok"), 1)
            for i, (t0, n) in enumerate(TILES):
                for j in range(i):
                    mm(bank[4][0:n, i * E:(i + 1) * E], ones[:, 0:n], chosen[:, j, :], start=j == 0, stop=False)
                last = mm(bank[4][0:n, i * E:(i + 1) * E], tri_before[0:n, 0:n], chosen[0:n, i, :],
                          start=i == 0, stop=True)
            for j, (t0, n) in enumerate(TILES):
                last = mm(bank[4][0:XMAX, 128:128 + E], ones[0:n, 0:XMAX], chosen[0:n, j, :], start=j == 0, stop=j == 2)
            for i, (t0, n) in enumerate(TILES):
                last = tr(bank[3][0:E, 128 + t0:128 + t0 + n], gate[0:n, i, :], ident[0:n, 0:n])
            last.then_inc(S("pe_stage"), once("pe_stage", "rk_mm"))

            def first_extras():
                pe.wait_ge(S("dve_stage"), AT["tot_ok"])
                mm(bank[7][:, 0:2 * XMAX + 1], ones[0:XMAX, :], found_diag, start=True, stop=True)\
                    .then_inc(S("pe_stage"), once("pe_stage", "tot_mm"))
                pe.wait_ge(S("act_stage"), AT["gT_ok"])
                for c in range(KC):
                    if c == 1:
                        pe.wait_ge(S("dve_stage"), AT["list_ok"])
                    if c >= 2:
                        pe.wait_ge(S("bd_ev"), c - 1)
                    mm(bank[6 + c % 2][:, 0:NT], b_down_sb[:, c * P:(c + 1) * P], gates_rows[0:E, :], start=True, stop=True)\
                        .then_inc(S("bd_mm"), 1)

            def gather(n, u):
                pe.wait_ge(S("sel_e"), n + 1)
                if isinstance(n, int) and n == 0:
                    pe.wait_ge(S("u_lo"), 6)
                    pe.wait_ge(S("act_stage"), AT["gT_ok"])
                else:
                    pe.wait_ge(S("xg_ev"), n)
                    pe.wait_ge(S("stz_ok"), n)
                for k in range(KC):
                    for i, (t0, nn) in enumerate(TILES):
                        for s in range(3):
                            last = mm(bank[2][:, k * 64:(k + 1) * 64], u_parts[0:nn, s, i, k * P:(k + 1) * P],
                                      slot_token[0:nn, u, i, :], start=(i == 0 and s == 0), stop=(i == 2 and s == 2))
                last.then_inc(S("xg_mm"), 1)
                for i, (t0, nn) in enumerate(TILES):
                    last = tr(bank[5][:, t0:t0 + nn], slot_gate[0:nn, u, i, :], ident[0:nn, 0:nn])
                last.then_inc(S("st_mm"), 1)

            def up(n, u, first):
                pe.wait_ge(S("xg_ev"), n + 1)
                if not first:
                    pe.wait_ge(S("h_read"), n)
                for k in range(KC):
                    pe.wait_ge(S(f"w_land{k}"), 16 * n + 16)
                    for q in range(2):
                        for hf in range(2):
                            last = mm(bank[q][64 * hf:64 * hf + 64, :], x_slots[:, u, k * 64:(k + 1) * 64],
                                      ring[:, k, q * 1024 + hf * 512:q * 1024 + hf * 512 + 512],
                                      start=k == 0, stop=False, tile_position=(0, 64 * hf))
                    last.then_inc(S("w_used"), 1)
                if first:
                    pe.wait_ge(S("bup_in"), 16)
                for q in range(2):
                    for hf in range(2):
                        last = mm(bank[q][64 * hf:64 * hf + 64, :], slot_expert[0:E, u, :],
                                  b_up_sb[:, q * 1024 + hf * 512:q * 1024 + hf * 512 + 512],
                                  start=False, stop=True)
                last.then_inc(S("up_mm"), 1)

            def down(n, u, first):
                pe.wait_ge(S("act_ok"), n + 1)
                for j in range(4):
                    last = tr(bank[3][:, j * P:(j + 1) * P], hidden[:, j * P:(j + 1) * P], ident[:, :])
                last.then_inc(S("at_mm"), 1)
                pe.wait_ge(S("at_ev"), n + 1)
                if not first:
                    pe.wait_ge(S("yg_ev"), n)
                for kk in range(KC):
                    if kk % 2 == 0:
                        pe.wait_ge(S(f"w_land{8 + kk // 2}"), 16 * n + 16)
                    for dh in range(2):
                        last = mm(bank[4][64 * dh:64 * dh + 64, :],
                                  hidden_T[:, (kk % 4) * P + (kk // 4) * 64:(kk % 4) * P + (kk // 4) * 64 + 64],
                                  ring[:, 8 + kk // 2, (kk % 2) * 1024 + dh * 512:(kk % 2) * 1024 + dh * 512 + 512],
                                  start=kk == 0, stop=kk == KC - 1, tile_position=(0, 64 * dh))
                    if kk % 2:
                        last.then_inc(S("w_used"), 1)

            def scatter(n, u, first):
                pe.wait_ge(S("yg_ev"), n + 1)
                pe.wait_ge(S("stz_ok"), n + 1)
                for c in range(KC):
                    if first and c == 0:
                        pe.wait_ge(S("bd_ev"), KC)
                    if not (first and c < 2):
                        pe.wait_ge(S("y_add"), KC * n + c - 1)
                    last = mm(bank[6 + c % 2][:, 0:NT], y_slots[:, (c % 4) * P:(c % 4) * P + P], gates_T[:, u, c // 4, :],
                              start=True, stop=True)
                    last.then_inc(S("y_mm"), 1)

            def experts(base, i, first, last):
                for u in range(2):
                    n = base + 2 * i + u
                    z0 = isinstance(n, int) and n == 0
                    up(n, u, z0)
                    if not (last and u == 1):
                        gather(n + 1, 1 - u)
                    if z0:
                        first_extras()
                    if not (first and u == 0):
                        scatter(n - 1, 1 - u, isinstance(n, int) and n == 1)
                    down(n, u, z0)

            def moe_pass(base):
                gather(base, 0)
                experts(base, 0, True, False)
                with pe.Fori(1, PAIRS - 1) as i:
                    experts(base, i, False, False)
                experts(base, PAIRS - 1, False, True)
                scatter(base + E - 1, 1, False)

            moe_pass(0)
            with further(pe) as x:
                gather(E + x, 0)
                up(E + x, 0, False)
                down(E + x, 0, False)
                scatter(E + x, 0, False)

            pe.wait_ge(S("dve_stage"), AT["moe_done"])
            for m_ in range(KC):
                if m_ >= 2:
                    pe.wait_ge(S("sg_ev"), m_ - 1)
                for c in range(KC):
                    if m_ == 0 and c % 4 == 0:
                        pe.wait_ge(S("wg_in"), 32)
                    last = mm(bank[m_ % 2][:, 0:NT], w_gate[:, c, m_ * P:(m_ + 1) * P], xT[:, c, :],
                              start=c == 0, stop=c == KC - 1)
                last.then_inc(S("sg_mm"), 1)
                if m_:
                    square_sum(2 * KC, m_ - 1)
            square_sum(2 * KC, KC - 1)
            for q in range(6):
                half, (t0, n) = q // 3, TILES[q % 3]
                pe.wait_ge(S("u_ready"), 2 * KC + 4 * half + 4)
                if q == 0:
                    pe.wait_ge(S("sg_ev"), KC)
                for c in range(4):
                    last = tr(bank[UN_BANKS[q]][0:n, c * P:(c + 1) * P], uT[:, 4 * half + c, t0:t0 + n], ident[:, :])
                last.then_inc(S("yo_mm"), 1)

        @block.scalar
        def _(act):
            A = act.activation

            def root(out, in_, width):
                return A(out, in_, ACT.Sqrt, bias=eps[0:out.shape[0]], scale=1.0 / width)

            act.wait_ge(S("const_a"), 1)
            act.wait_ge(S("dve_stage"), AT["lb_in"])
            A(lbt[:, 0:2, :], lbt[:, 0:2, :], ACT.Exp).then_inc(S("act_stage"), once("act_stage", "lb_exp"))
            for c in range(KC):
                act.wait_ge(S("xt_mm"), c + 1)
                A(xT[:, c, :], bank[c % 4][:, 0:NT], ACT.Copy).then_inc(S("xt_ev"), 1)
            act.wait_ge(S("sq_used"), KC)
            root(rt[:, 0, :], bank[4][:, 0:NT], D).then_inc(S("rt_ok"), 1)
            def block_quarter(n, m, half=1):
                q = 4 * n + m
                if half == 0:
                    return
                act.wait_ge(S("pt_mm"), q + 1)
                A(proj[:, 4 * ORDER[n] + m, :], bank[q % 2][:, 0:NT], ACT.Copy).then_inc(S("pt_ev"), 1)
                if n in (3, 4) and m == 3:
                    act.dma_start(w_block(n + 2), w_in_c[:, :, 512 * ORDER[n + 2]:512 * ORDER[n + 2] + 512])\
                       .then_inc(S(f"w_in{n + 2}"), 16)
                if n == 5 and m == 3:
                    act.dma_start(states, state_hgrn[0].rearrange("b h k v -> k b h v")).then_inc(S("st_in"), 16)

            for n in range(3):
                for m in range(4):
                    block_quarter(n, m)
                    if n == 2 and m == 0:
                        act.wait_ge(S("dve_stage"), AT["ff_na"])
                        A(ff[:, 1, :], ff[:, 1, :], ACT.Exp).then_inc(S("act_stage"), once("act_stage", "ff_exp"))
                        act.wait_ge(S("dve_stage"), AT["ff_w"])
                        A(ff[:, 3, :], ff[:, 2, :], ACT.Ln).then_inc(S("act_stage"), once("act_stage", "ff_ln"))
            for h in range(FH):
                act.wait_ge(S("lr_mm"), h + 1)
                A(later_sums[:, h, :, :], bank[6 + h % 2][:, 0:2 * P].rearrange("p (a b) -> p a b", a=2), ACT.Copy)\
                    .then_inc(S("lr_ev"), 1)
            act.wait_ge(S("pe_stage"), AT["snew_mm"])
            A(snew[:, :], bank[4][:, 0:B], ACT.Copy, scale=SCALE)\
                .then_inc(S("act_stage"), once("act_stage", "snew_ok"))
            for q in range(2):
                act.wait_ge(S("sf_mm"), q + 1)
                A(suffix_T[:, 4 * q:4 * q + 4, :], bank[6 + q][:, :].rearrange("p (h g) -> p h g", h=4), ACT.Copy)\
                    .then_inc(S("sf_ok"), 1)

            def seq_q(b):
                act.wait_ge(S("qb_mm"), b + 1)
                if b >= 2:
                    act.wait_ge(S("k_mul"), CK * (b - 1))
                A(qb[:, b % 2, :], bank[2][:, :], ACT.Copy).then_inc(S("qb_ok"), 1)

            def seq_exp(b):
                act.wait_ge(S("z_ok"), b + 1)
                if b:
                    act.wait_ge(S("v_land_used"), CK * b)
                A(probs[:, :, :, :], zrep(z), ACT.Exp).then_inc(S("p_ok"), 1)
                A(pnew, snew[:, b:b + 1], ACT.Exp, bias=mcol_neg).then_inc(S("pn_ok"), 1)

            def seq_sum(b):
                act.wait_ge(S("fo_mm"), b + 1)
                A(proj[:, FQ:FQ + FC, b + T:b + T + 1], bank[3][:, 140:140 + FC].rearrange("p (c a) -> p c a", a=1),
                  ACT.Copy).then_inc(S("fo_ev"), 1)

            def fox_a(h):
                act.wait_ge(S("fx_max"), h + 1)
                if h:
                    act.wait_ge(S("fx_tr"), h)
                A(prob_p[:, 0:P], logit_p[:, 0:P], ACT.Exp, bias=small[:, 100:101], accum_out=small[:, 102:103])
                A(prob_p[:, P:3 * P], logit_p[:, P:3 * P], ACT.Exp, bias=small[:, 101:102], accum_out=small[:, 103:104])\
                    .then_inc(S("fx_exp"), 1)

            def fox_b(h):
                act.wait_ge(S("fx_tr"), h + 1)
                if h:
                    act.wait_ge(S("fx_o"), h)
                A(prob_T, bank[7][:, 0:3 * P], ACT.Copy).then_inc(S("fx_pt"), 1)

            def fox_c(h):
                if h % 2:
                    c = h // 2
                    act.wait_ge(S("fx_o"), h + 1)
                    A(proj[:, FQ + c, 0:T], bank[5][:, 0:T], ACT.Copy).then_inc(S("fx_o_ev"), 1)

            def gates():
                act.wait_ge(S("pt_ev"), 20)
                A(proj[:, HF:HF + 4, :], proj[:, HF:HF + 4, :], ACT.Sigmoid)\
                    .then_inc(S("act_stage"), once("act_stage", "hf_sig"))
                act.wait_ge(S("sf_ok"), 2)
                A(tmp4, proj[:, HQ:HQ + 4, :], ACT.Sigmoid).then_inc(S("silu_sig"), 1)

            def out_gate():
                act.wait_ge(S("pt_ev"), 28)
                act.wait_ge(S("silu"), 1)
                A(tmp4, proj[:, HG:HG + 4, :], ACT.Sigmoid).then_inc(S("silu_sig"), 1)

            def hgd_b(b0):
                if b0 < B - 2:
                    return
                act.wait_ge(S("pe_stage"), AT["st_o"])
                A(proj[:, HI:HI + HH, T:NT], bank[5][:, 0:HH * B].rearrange("p (h b) -> p h b", h=HH), ACT.Copy)\
                    .then_inc(S("act_stage"), once("act_stage", "st_o_ev"))
                act.wait_ge(S("st_new"), B)
                act.dma_start(st_s[0].rearrange("b h k v -> k b h v"), states).then_inc(S("st_out"), 16)

            def load_w_out():
                act.wait_ge(S("st_out"), 16)
                act.dma_start(w_out_sb, wo_c).then_inc(S("w_out"), 16)

            def hg_l(h):
                if h == 0:
                    act.wait_ge(S("fx_o"), FH)
                    act.wait_ge(S("fx_tr"), FH)
                    act.wait_ge(S("dve_stage"), AT["f_ok"])
                else:
                    act.wait_ge(S("hg_A"), h)
                A(qe, proj[:, HF + h, 0:T], ACT.Ln).then_inc(S("hg_ln"), 1)

            def hg_e(h):
                act.wait_ge(S("hg_d"), h + 1)
                A(kd, qe, ACT.Exp, scale=-1.0).then_inc(S("act_chain"), 1)
                act.wait_ge(S("act_chain"), 3 * h + 1)
                A(qe, qe, ACT.Exp).then_inc(S("act_chain"), 1)
                A(bb, bb, ACT.Exp).then_inc(S("act_chain"), 1)
                A(ko, ko, ACT.Exp).then_inc(S("hg_exp"), 1)

            def hg_b(h):
                act.wait_ge(S("hg_koT"), h + 1)
                if h:
                    act.wait_ge(S("hg_U"), h)
                A(kn, bank[7][:, 0:T], ACT.Copy).then_inc(S("hg_kn"), 1)

            def hg_d(h):
                act.wait_ge(S("hg_o"), h + 1)
                A(proj[:, HI + h, 0:T], bank[7][:, 0:T], ACT.Copy).then_inc(S("hg_o_ev"), 1)
                if h == HH - 1:
                    act.wait_ge(S("sfin_ok"), HH)
                    act.dma_start(st_p[0, 0].rearrange("h k v -> k h v"), sfin).then_inc(S("sfin_out"), 16)

            def norm_a(k):
                for c in range(4):
                    act.wait_ge(S("hs_mm"), 4 * k + c + 1)
                    root(rs4[:, c, :], bank[NORM_BANKS[c]][:, 0:NT], DH if k else DK).then_inc(S("hs_ev"), 1)

            def ple_t():
                for c in range(2):
                    act.wait_ge(S("pT_mm"), c + 1)
                    A(p_T[:, c, :], bank[5 + c][:, 0:NT], ACT.Copy).then_inc(S("pT_ok"), 1)

            run({"seq_q": seq_q, "seq_exp": seq_exp, "seq_sum": seq_sum, "block": block_quarter, "fox_a": fox_a,
                 "fox_b": fox_b, "fox_c": fox_c, "gates": gates, "out_gate": out_gate, "hgd_b": hgd_b,
                 "w_out": load_w_out, "hg_l": hg_l, "hg_e": hg_e, "hg_b": hg_b, "hg_d": hg_d, "norm_a": norm_a})
            ple_t()
            norm_a(1)
            for m_ in range(KC):
                act.wait_ge(S("pw_mm"), m_ + 1)
                A(pw_T[:, m_, :], bank[(7, 2)[m_ % 2]][:, 0:NT], ACT.Copy).then_inc(S("pw_ev"), 1)
            act.wait_ge(S("sq_used"), 2 * KC)
            root(rt[:, 0, :], bank[4][:, 0:NT], D).then_inc(S("rt_ok"), 1)
            act.wait_ge(S("pe_stage"), AT["lgT_mm"])
            A(logits_T[0:E, :], bank[2][0:E, 0:NT], ACT.Identity, bias=rb).then_inc(S("act_stage"), once("act_stage", "lgT_ok"))
            def high(q):
                i, half = q // 2, q % 2
                n = TILES[i][1]
                act.wait_ge(S("un_mm"), q + 1)
                A(u_parts[0:n, 0, i, 512 * half:512 * half + 512], bank[UN_BANKS[q]][0:n, :], ACT.Copy).then_inc(S("u_hi"), 1)

            high(0)
            act.wait_ge(S("top_ok"), 1)
            A(gate, gate, ACT.Exp).then_inc(S("g_exp"), 1)
            for q in range(1, 6):
                high(q)
            for q in range(6):
                i, half = q // 2, q % 2
                n = TILES[i][1]
                act.wait_ge(S("un_ev"), q + 1)
                A(u_parts[0:n, 1, i, 512 * half:512 * half + 512], rest[q % 5][0:n, :], ACT.Copy).then_inc(S("u_mi"), 1)
            act.wait_ge(S("pe_stage"), AT["rk_mm"])
            A(gates_rows[0:E, :], bank[3][0:E, 128:128 + NT], ACT.Copy).then_inc(S("act_stage"), once("act_stage", "gT_ok"))
            act.wait_ge(S("dve_stage"), AT["stz_zero"])

            def gathered(n, u):
                act.wait_ge(S("xg_mm"), n + 1)
                A(x_slots[:, u, :], bank[2][:, :], ACT.Copy).then_inc(S("xg_ev"), 1)

            def turned(n, u, first, after=None):
                act.wait_ge(S("st_mm"), n + 1)
                if not first:
                    act.wait_ge(S("y_mm"), KC * (n - 1 if after is None else after))
                A(gates_T[0:64, u, 0, :], bank[5][0:64, 0:NT], ACT.Copy)
                A(gates_T[64:128, u, 1, :], bank[5][64:128, 0:NT], ACT.Copy).then_inc(S("stz_ok"), 1)

            def experts(base, i, first, last):
                for u in range(2):
                    n = base + 2 * i + u
                    z0 = isinstance(n, int) and n == 0
                    act.wait_ge(S("glu_ok"), n + 1)
                    A(hidden, glu, ACT.Sigmoid, scale=1.702).then_inc(S("sig_ok"), 1)
                    if not (last and u == 1):
                        gathered(n + 1, 1 - u)
                        turned(n + 1, 1 - u, z0)
                    act.wait_ge(S("at_mm"), n + 1)
                    A(hidden_T, bank[3][:, :], ACT.Copy).then_inc(S("at_ev"), 1)
                    act.wait_ge(S("w_used"), RING * n + RING)
                    if not z0:
                        act.wait_ge(S("y_mm"), KC * n)
                    A(y_slots, bank[4][:, :], ACT.Copy).then_inc(S("yg_ev"), 1)

            def moe_pass(base):
                gathered(base, 0)
                turned(base, 0, isinstance(base, int))
                experts(base, 0, True, False)
                with act.Fori(1, PAIRS - 1) as i:
                    experts(base, i, False, False)
                experts(base, PAIRS - 1, False, True)

            moe_pass(0)
            with further(act) as x:
                n = E + x
                gathered(n, 0)
                turned(n, 0, False, after=n)
                act.wait_ge(S("glu_ok"), n + 1)
                A(hidden, glu, ACT.Sigmoid, scale=1.702).then_inc(S("sig_ok"), 1)
                act.wait_ge(S("at_mm"), n + 1)
                A(hidden_T, bank[3][:, :], ACT.Copy).then_inc(S("at_ev"), 1)
                act.wait_ge(S("w_used"), RING * n + RING)
                act.wait_ge(S("y_mm"), KC * n)
                A(y_slots, bank[4][:, :], ACT.Copy).then_inc(S("yg_ev"), 1)
            act.wait_ge(S("dve_stage"), AT["moe_done"])
            for m_ in range(KC):
                act.wait_ge(S("sg_mm"), m_ + 1)
                A(sg_T[:, m_, :], bank[m_ % 2][:, 0:NT], ACT.Sigmoid).then_inc(S("sg_ev"), 1)
            act.wait_ge(S("sq_used"), 3 * KC)
            root(rt[:, 0, :], bank[4][:, 0:NT], D).then_inc(S("rt_ok"), 1)
            for i, (t0, n) in enumerate(TILES):
                act.wait_ge(S("yo_mm"), i + 1)
                A(yout[0:n, i, 0:512], bank[UN_BANKS[i]][0:n, :], ACT.Copy).then_inc(S("yo_lo"), 1)

        @block.vector
        def _(dve):
            d = Chain(dve, dchain)

            TT, TS, STT, CP = dve.tensor_tensor, dve.tensor_scalar, dve.scalar_tensor_tensor, dve.tensor_copy
            M, AD, SU = ALU.mult, ALU.add, ALU.subtract

            def bcast(ap, n):
                return ap.unsqueeze(len(ap.shape)).broadcast_to(list(ap.shape) + [n])

            def squares(k, src, c):
                if k:
                    dve.wait_ge(S("sq_used"), k + c - 1)
                TT(square_of(k, c), src, src, M).then_inc(S("sq_ready"), 1)

            def rms(k, g, src=xT):
                if k == 0:
                    for c in range(KC):
                        dve.wait_ge(S("xt_ev"), c + 1)
                        squares(k, xT[:, c, :], c)
                dve.wait_ge(S("rt_ok"), k // KC + 1)
                d(dve.reciprocal(rstd[:, :], rt[:, 0, :]))
                for c in range(KC):
                    STT(uT[:, c, :], src[:, c, :], gcols[:, g + c:g + c + 1], rstd[:, :], M, M)\
                        .then_inc(S("u_ready"), 1)

            dve.wait_ge(S("pe_stage"), AT["g_ready"])
            d(CP(gcols[:, :], bank[7][:, 0:40]))
            l0, l1 = gcols[:, LB0:LB0 + 4], gcols[:, LB1:LB1 + 4]
            d(TT(lbt[:, 2, :], l0, l1, ALU.max))
            TT(lbt[:, 0, :], l0, lbt[:, 2, :], SU)
            TT(lbt[:, 1, :], l1, lbt[:, 2, :], SU).then_inc(S("dve_stage"), once("dve_stage", "lb_in"))
            dve.wait_ge(S("act_stage"), AT["lb_exp"])
            d(TT(lbt[:, 2, :], lbt[:, 0, :], lbt[:, 1, :], AD))
            d(dve.reciprocal(oml, lbt[:, 2, :]))
            d(TT(lb, lbt[:, 0, :], oml, M))
            d(TS(oml, lb, -1.0, 1.0, M, AD))
            rms(0, GMIX)

            dve.wait_ge(S("pe_stage"), AT["ff_mm"])
            x, e, w, l = (ff[:, i, :] for i in range(4))
            d(TS(x, bank[5][0:FH, 0:NT], ffb, None, AD))
            d(TS(w, x, -1.0, None, M))
            TT(e, x, w, ALU.min).then_inc(S("dve_stage"), once("dve_stage", "ff_na"))
            dve.wait_ge(S("act_stage"), AT["ff_exp"])
            TS(w, e, 1.0, None, AD).then_inc(S("dve_stage"), once("dve_stage", "ff_w"))
            dve.wait_ge(S("dve_stage"), AT["ff_w"])
            t1, t2 = lf_T, sq[0:FH, 0, :]
            d(TS(t1, w, -1.0, None, AD))
            d(TS(t2, t1, 0.0, None, ALU.is_equal))
            d(TT(t1, t1, t2, AD))
            dve.wait_ge(S("act_stage"), AT["ff_ln"])
            d(dve.reciprocal(w, t1))
            d(TT(l, l, w, M))
            d(TT(l, l, t2, AD))
            d(TT(l, l, e, M))
            d(TS(x, x, 0.0, None, ALU.min))
            d(TT(lf_T, x, l, SU))
            dve.memset(ff[:, 1, 0:T], 1.0).then_inc(S("dve_stage"), once("dve_stage", "lf_one"))
            dve.wait_ge(S("dve_stage"), AT["lf_one"])
            dve.tensor_tensor_scan(c_T, ff[:, 1, 0:T], lf_T[:, 0:T], 0.0, M, AD).then_inc(S("dve_stage"), once("dve_stage", "lfT_ok"))
            TT(qk_new, proj[:, FQ:FQ + 4, T:NT], proj[:, FK:FK + 4, T:NT], M)\
                .then_inc(S("dve_stage"), once("dve_stage", "qk_new"))
            dve.wait_ge(S("pe_stage"), AT["qnat_mm"])
            CP(q_rows, bank[2][0:B, :]).then_inc(S("dve_stage"), once("dve_stage", "q_nat"))

            def natural(q0, dsts, banks):
                q = q0
                for dst in dsts:
                    for i, (t0, n) in enumerate(TILES):
                        dve.wait_ge(S("nat_mm"), q + 1)
                        CP(dst[0:n, i, :], bank[banks[q % 2]][0:n, :]).then_inc(S("nat_ev"), 1)
                        q += 1
                dve.wait_ge(S("nat_ev"), q)

            natural(0, (k_rows, v_rows), (6, 7))
            dve.nop().then_inc(S("dve_stage"), once("dve_stage", "fkv_nat"))
            dve.wait_ge(S("pe_stage"), AT["lfn_mm"])
            for i, (t0, n) in enumerate(TILES):
                CP(lf_rows[0:n, i, :], bank[3][0:n, i * FH:(i + 1) * FH])
            d(CP(c_rows[:, :, :], bank[3][:, 32:32 + 2 * FH].rearrange("p (i h) -> p i h", i=2)))
            dve.nop().then_inc(S("dve_stage"), once("dve_stage", "lf_nat"))
            CP(lf_new, bcast(lf_rows[0:B, 2, :], NPAGE)).then_inc(S("dve_stage"), once("dve_stage", "lnew_cp"))
            TS(c_T, c_T, 1.0 / SCALE, None, M).then_inc(S("dve_stage"), once("dve_stage", "c8_ok"))
            dve.wait_ge(S("sf_ok"), 2)
            dve.wait_ge(S("act_stage"), AT["snew_ok"])
            dve.wait_ge(S("const_b"), 1)
            dve.wait_ge(S("const_c"), 1)

            zv = z.rearrange("p (g h) -> p g h", h=FH)
            ofm = ofmask.rearrange("p h d -> p (h d)")

            def seq_k(b, c):
                dve.wait_ge(S("k_mul"), CK * b + c + 1)
                last = dve.tensor_reduce(sc[:, 32 * c:32 * c + 32], ring[:, c, :].rearrange("p (a b) -> p a b", b=DH),
                                         AX.X, AD)
                last.then_inc(S("k_land_used"), 1)
                if c < CK - 1:
                    return
                dve.wait_ge(S("k_land_used"), CK * (b + 1))
                if b:
                    dve.wait_ge(S("p_ok"), b)
                d(STT(zv, sc.rearrange("p (g h) -> p g h", h=FH), -SCALE,
                      suffix_T[:, :, b * NPG:(b + 1) * NPG].rearrange("p h g -> p g h"), M, AD))
                d(dve.tensor_reduce(mx, z.rearrange("p (g h) -> p h g", h=FH), AX.X, ALU.max))
                CP(mx_rep.rearrange("p (r h) -> p r h", h=FH), mx.unsqueeze(1).broadcast_to([P, 16, FH]))\
                    .then_inc(S("mx_ok"), 1)

            def seq_max(b):
                dve.wait_ge(S("mx_tr"), b + 1)
                if b:
                    dve.wait_ge(S("pn_ok"), b)
                d(dve.tensor_reduce(mcol, bank[3][:, 0:P], AX.X, ALU.max))
                d(TT(mcol, mcol, snew[:, b:b + 1], ALU.max))
                d(TS(mcol_neg, mcol, -1.0, None, M))
                TS(dmx[0:FH, :], ident[0:FH, 0:FH], mcol_neg[0:FH, :], None, M).then_inc(S("dm_ok"), 1)

            def seq_exp(b):
                dve.wait_ge(S("mb_mm"), b + 1)
                TT(zv, zv, bank[3][:, 128:128 + FH].unsqueeze(1).broadcast_to([P, NPG, FH]), AD)\
                    .then_inc(S("z_ok"), 1)

            def seq_pv(b):
                dve.wait_ge(S("p_ok"), b + 1)
                dve.wait_ge(S("vb2_mm"), b + 1)
                dve.wait_ge(S("pn_ok"), b + 1)
                STT(of2[0:FH, :], bank[2][0:FH, :], pnew[0:FH, :], ofm[0:FH, :], M, M)
                d(dve.tensor_reduce(lsum, probs[:, :, 0, :].rearrange("p g h -> p h g"), AX.X, AD))
                CP(l_rep.rearrange("p (r h) -> p r h", h=FH), lsum.unsqueeze(1).broadcast_to([P, 16, FH]))\
                    .then_inc(S("lp_ok"), 1)

            def seq_out(b):
                dve.wait_ge(S("l_mm"), b + 1)
                d(TT(ltot, bank[3][:, 136:137], pnew, AD))
                d(dve.reciprocal(rl, ltot))
                d(TS(nrl, rl, -1.0, None, M))
                dve.wait_ge(S("v_land_used"), CK * (b + 1))
                if b:
                    dve.wait_ge(S("fo_mm"), b)
                d(STT(of, bank[4][:, :], rl, ofm, M, M))
                STT(of[0:FH, :], of2[0:FH, :], nrl[0:FH, :], of[0:FH, :], M, AD).then_inc(S("of_ok"), 1)

            nm, ls, rs = small[:, 100:102], small[:, 102:104], small[:, 104:106]
            mxs = small[:, 106:108]

            def fox_a(h):
                dve.wait_ge(S("fx_s"), h + 1)
                if h:
                    dve.wait_ge(S("fx_exp"), h)
                TS(logit_p[:, 0:P], bank[6][:, 0:P], SCALE, c_rows[:, 0, h:h + 1], M, AD)
                TS(logit_p[:, P:3 * P], bank[6][:, P:3 * P], SCALE, c_rows[:, 1, h:h + 1], M, AD).then_inc(S("fx_z"), 1)
                dve.wait_ge(S("fx_z"), h + 1)
                for z_ in (logit_p[:, 0:P], logit_p[:, 2 * P:3 * P]):
                    d(TT(z_, z_, cmask[:, :], AD))
                dve.tensor_reduce(mxs[:, 0:1], logit_p[:, 0:P], AX.X, ALU.max)
                d(dve.tensor_reduce(mxs[:, 1:2], logit_p[:, P:3 * P], AX.X, ALU.max))
                TS(nm, mxs, -1.0, None, M).then_inc(S("fx_max"), 1)

            def fox_b(h):
                dve.wait_ge(S("fx_exp"), h + 1)
                d(dve.reciprocal(rs, ls))
                TS(prob_p[:, 0:P], prob_p[:, 0:P], rs[:, 0:1], None, M)
                TS(prob_p[:, P:3 * P], prob_p[:, P:3 * P], rs[:, 1:2], None, M).then_inc(S("fx_p"), 1)

            def gates():
                dve.wait_ge(S("act_stage"), AT["hf_sig"])
                for h in range(HH):
                    last = TS(proj[:, HF + h, :], proj[:, HF + h, :], oml[:, h:h + 1], lb[:, h:h + 1], M, AD)
                last.then_inc(S("dve_stage"), once("dve_stage", "f_ok"))
                dve.wait_ge(S("dve_stage"), AT["f_ok"])
                d(TS(k_new_T, proj[:, HF:HF + HH, T:NT], -1.0, 1.0, M, AD))
                dve.wait_ge(S("silu_sig"), 1)
                TT(proj[:, HQ:HQ + 4, :], proj[:, HQ:HQ + 4, :], tmp4, M).then_inc(S("silu"), 1)

            def hi_nat():
                natural(6, (hi_rows,), (0, 1))

            def out_gate():
                dve.wait_ge(S("silu_sig"), 2)
                TT(proj[:, HG:HG + 4, :], proj[:, HG:HG + 4, :], tmp4, M).then_inc(S("silu"), 1)
                dve.wait_ge(S("silu"), 2)

            def hgd_a(b0):
                if b0 == 0:
                    dve.wait_ge(S("st_in"), 16)
                    dve.wait_ge(S("fx_o"), FH)
                for b in (b0, b0 + 1):
                    dve.wait_ge(S("vb_mm"), b + 1)
                    kb = k_new_T[:, :, b:b + 1].broadcast_to([P, HH, DK])
                    fb = proj[:, HF:HF + HH, T + b:T + b + 1].broadcast_to([P, HH, DK])
                    t = arena_at(512 + 512 * (b % 2), 512).rearrange("p (h v) -> p h v", h=HH)
                    TT(t, bank[6 + b % 2][:, :].rearrange("p (h v) -> p h v", h=HH), kb, M).then_inc(S("vb_used"), 1)
                    d(TT(states[:, b, :, :], states[:, b, :, :], fb, M))
                    dve.wait_ge(S("vb_used"), b + 1)
                    TT(states[:, b, :, :], states[:, b, :, :], t, SU).then_inc(S("st_new"), 1)
                dve.wait_ge(S("st_new"), b0 + 2)

            def chunks(t):
                return t.rearrange("p (c r) -> p c r", r=CH)

            def hg_a(h):
                if h == 0:
                    d(dve.memset(St[:, 0, :], 0.0))
                dve.wait_ge(S("hg_ln"), h + 1)
                d(dve.tensor_tensor_scan(bb, reset[:, :], qe, 0.0, M, AD))
                mid = chunks(bb)[:, :, CH // 2 - 1:CH // 2].broadcast_to([P, NCH, CH])
                end = chunks(bb)[:, :, CH - 1:CH].broadcast_to([P, NCH, CH])
                d(TT(chunks(qe), chunks(bb), mid, SU))
                if h:
                    dve.wait_ge(S("hg_koT"), h)
                TT(chunks(ko), end, chunks(bb), SU)
                d(TS(qe, qe, 80.0, -80.0, ALU.min, ALU.max))
                TS(kh, proj[:, HF + h, 0:T], -1.0, 1.0, M, AD).then_inc(S("hg_d"), 1)

            def hg_e(h):
                dve.wait_ge(S("hg_exp"), h + 1)
                dve.wait_ge(S("hg_d"), h + 1)
                if h:
                    dve.wait_ge(S("hg_o"), h)
                qh = proj[:, HQ + h, 0:T]
                TT(qe, qh, qe, M)
                TT(kd, kh, kd, M)
                TT(qi, qh, bb, M)
                TT(ko, kh, ko, M).then_inc(S("hg_qk"), 1)

            def hg_b(h):
                dve.wait_ge(S("hg_A"), h + 1)
                for i in range(NTILE):
                    last = TT(ats[:, i * P:(i + 1) * P], bank[6][:, i * P:(i + 1) * P], hmask[:, :], M)
                last.then_inc(S("hg_ats"), 1)

            def hg_c(h):
                dve.wait_ge(S("hg_U"), h + 1)
                for c in range(NCH):
                    U = bank[(0, 1, 5, 6)[c % 4]][:, (c // 4) * P:(c // 4 + 1) * P]
                    dst = St[:, c + 1, :] if c < NCH - 1 else sfin[:, h, :]
                    last = STT(dst, St[:, c, :], bb[:, c * CH + CH - 1:c * CH + CH], U, M, AD)
                    if c < NCH - 1:
                        d(last)
                last.then_inc(S("hg_S"), 1)
                dve.wait_ge(S("hg_S"), h + 1)
                dve.nop().then_inc(S("sfin_ok"), 1)

            def norm_a(k):
                if k == 0:
                    dve.wait_ge(S("hg_o_ev"), HH)
                TT(sq4, heads(k), heads(k), M).then_inc(S("hs_ready"), 1)
                if k == 0:
                    TT(heads(0), heads(0), proj[:, HG:HG + 4, :], M).then_inc(S("mix_gated"), 1)

            def norm_b(k):
                for c in range(4):
                    dve.wait_ge(S("hs_ev"), 4 * k + c + 1)
                    dve.reciprocal(rs4[:, c, :], rs4[:, c, :]).then_inc(S("hs_rstd"), 1)
                if k == 0:
                    dve.wait_ge(S("mix_gated"), 1)
                for c in range(4):
                    g = (GHG, GFOX)[k] + c
                    dve.wait_ge(S("hs_rstd"), 4 * k + c + 1)
                    STT(heads(k)[:, c, :], heads(k)[:, c, :], gcols[:, g:g + 1], rs4[:, c, :], M, M)\
                        .then_inc(S("mix_ok"), 1)

            def out_add(m_, k=0):
                dve.wait_ge(S("h_mm"), KC * k + m_ + 1)
                TT(xT[:, m_, :], xT[:, m_, :], bank[m_ % 2][:, 0:NT], AD).then_inc(S("h_ev"), 1)

            run({"seq_k": seq_k, "seq_max": seq_max, "seq_exp": seq_exp, "seq_pv": seq_pv, "seq_out": seq_out,
                 "fox_a": fox_a, "fox_b": fox_b, "gates": gates, "hi_nat": hi_nat, "out_gate": out_gate, "hgd_a": hgd_a,
                 "hg_a": hg_a, "hg_e": hg_e, "hg_b": hg_b, "hg_c": hg_c, "norm_a": norm_a, "norm_b": norm_b,
                 "out_add": out_add})

            dve.wait_ge(S("fo_ev"), B)
            norm_a(1)
            norm_b(1)
            dve.wait_ge(S("sfin_out"), 16)
            dve.memset(gates_T[:, :, :, :], 0.0).then_inc(S("dve_stage"), once("dve_stage", "stz_zero"))
            logits_flat, equal_flat, nth_flat, restart_flat = (
                t.rearrange("p i e -> p (i e)") for t in (logits, equal, nth, restart))
            dve.memset(logits_flat, 0.0)
            d(dve.memset(restart_flat, 1.0))
            d(dve.memset(restart[:, :, 0:1], 0.0))
            dve.memset(ranks_gates[:, :, :], -1.0)
            for m_ in range(KC):
                out_add(m_, 1)
                dve.wait_ge(S("h_ev"), KC + m_ + 1)
                squares(KC, xT[:, m_, :], m_)
            rms(KC, GMLP)
            dve.wait_ge(S("pe_stage"), AT["lg_mm"])

            def each(col):
                return col.broadcast_to([P, 3, E])

            for i, (t0, n) in enumerate(TILES):
                last = CP(logits[0:n, i, :], bank[3][0:n, i * E:(i + 1) * E])
            d(last)
            for i in range(3):
                last = dve.max(top8[:, i, :], logits[:, i, :])
            d(last)
            TT(gate, logits, each(top8[:, :, 0:1]), SU).then_inc(S("top_ok"), 1)
            TT(above[:, :, :], logits, each(top8[:, :, 3:4]), ALU.is_gt)
            d(TT(equal, logits, each(top8[:, :, 3:4]), ALU.is_equal))
            dve.tensor_reduce(per_token[:, 0:3], above[:, :, :], AX.X, AD)
            d(dve.tensor_tensor_scan(nth_flat, restart_flat, equal_flat, 0.0, M, AD))
            d(TT(nth, nth, each(per_token[:, 0:3].unsqueeze(2)), AD))
            d(TS(nth, nth, float(TOPK), None, ALU.is_le))
            d(TT(equal, equal, nth, M))
            d(TT(chosen, above[:, :, :], equal, AD))
            dve.wait_ge(S("g_exp"), 1)
            d(TT(gate, gate, chosen, M))
            d(dve.tensor_reduce(per_token[:, 3:6], gate, AX.X, AD))
            d(dve.reciprocal(per_token[:, 6:9], per_token[:, 3:6]))
            TT(gate, gate, each(per_token[:, 6:9].unsqueeze(2)), M).then_inc(S("sel_ok"), 1)
            dve.wait_ge(S("sel_ok"), 1)
            def low(q):
                i, half = q // 2, q % 2
                n = TILES[i][1]
                dve.wait_ge(S("u_mi"), q + 1)
                mi_, lo_ = (u_parts[0:n, s, i, 512 * half:512 * half + 512] for s in (1, 2))
                TT(lo_, rest[q % 5][0:n, :], mi_, SU).then_inc(S("u_lo"), 1)

            for q in range(6):
                i, half = q // 2, q % 2
                n = TILES[i][1]
                dve.wait_ge(S("u_hi"), q + 1)
                if q == 5:
                    dve.wait_ge(S("u_lo"), 1)
                TT(rest[q % 5][0:n, :], bank[UN_BANKS[q]][0:n, :], u_parts[0:n, 0, i, 512 * half:512 * half + 512], SU)\
                    .then_inc(S("un_ev"), 1)
                if q:
                    low(q - 1)
            low(5)
            dve.wait_ge(S("pe_stage"), AT["rk_mm"])
            for i, (t0, n) in enumerate(TILES):
                last = STT(rank[0:n, i, :], bank[4][0:n, i * E:(i + 1) * E], 1.0, chosen[0:n, i, :], AD, M)
            d(last)
            for i, (t0, n) in enumerate(TILES):
                TS(ranks_gates[0:n, :, i], rank[0:n, i, :], -1.0, None, AD)
                last = CP(ranks_gates[0:n, :, 3 + i], gate[0:n, i, :])
            d(last)

            def list_blocks():
                for k in range(NBLK):
                    last = TS(has_block[:, E * k:E * k + E], bank[4][0:XMAX, 128:128 + E], float(SLOTS * (k + 1)), None, ALU.is_gt)
                d(last)
                d(dve.memset(this_block, 1.0))
                d(dve.tensor_tensor_scan(block_no, this_block, has_block, 0.0, M, AD))
                d(TS(this_block, block_no, order_no[0:XMAX, :], None, ALU.is_equal))
                d(TT(this_block, this_block, has_block, M))
                dve.wait_ge(S("codes_ok"), 1)
                for w in range(2):
                    d(TT(has_block, this_block, codes[:, w * E * NBLK:(w + 1) * E * NBLK], M))
                    d(dve.tensor_reduce(found[:, w:w + 1], has_block, AX.X, AD))
                d(CP(found[:, 2:3], block_no[:, E * NBLK - 1:E * NBLK]))
                for w in range(2):
                    d(TS(found_diag[:, 1 + w * XMAX:1 + (w + 1) * XMAX], ident[0:XMAX, 0:XMAX], found[:, w:w + 1], None, M))
                TS(found_diag[:, 0:1], ident[0:XMAX, 0:1], found[:, 2:3], None, M)\
                    .then_inc(S("dve_stage"), once("dve_stage", "tot_ok"))

            def first_extras():
                dve.wait_ge(S("pe_stage"), AT["tot_mm"])
                d(CP(block_list, bank[7][:, 0:2 * XMAX + 1]))
                CP(block_ints, block_list[0:1, 0:XMAX + 1]).then_inc(S("dve_stage"), once("dve_stage", "list_ok"))
                for c in range(KC):
                    dve.wait_ge(S("bd_mm"), c + 1)
                    TT(xT[:, c, :], xT[:, c, :], bank[6 + c % 2][:, 0:NT], AD).then_inc(S("bd_ev"), 1)
                dve.wait_ge(S("bd_ev"), KC)

            def choose(n, e, u, first, after=None, start=None):
                if not first:
                    k = n - 1 if after is None else after
                    dve.wait_ge(S("xg_mm"), k)
                    dve.wait_ge(S("st_mm"), k)
                    dve.wait_ge(S("up_mm"), k)
                d(CP(cur_rank_gate[:, u, :], ranks_gates[:, ds(e, 1), :].rearrange("p a r -> p (a r)")))
                if start is not None:
                    d(CP(first_rank, start))
                    d(TS(cur_rank_gate[:, u, 0:3], cur_rank_gate[:, u, 0:3], first_rank, None, SU))
                CP(slot_expert[0:E, u, :], ident[0:E, ds(e, 1)].broadcast_to([E, 64]))
                for i, (t0, nn) in enumerate(TILES):
                    TS(slot_token[0:nn, u, i, :], slot_no[0:nn, 0:64], cur_rank_gate[0:nn, u, i:i + 1], None, ALU.is_equal)
                    last = TS(slot_gate[0:nn, u, i, :], slot_no[0:nn, :], cur_rank_gate[0:nn, u, i:i + 1],
                              cur_rank_gate[0:nn, u, 3 + i:4 + i], ALU.is_equal, M)
                last.then_inc(S("sel_e"), 1)

            def swiglu(n):
                dve.wait_ge(S("up_mm"), n + 1)
                TS(glu, bank[0][:, :], LIMIT, None, ALU.min).then_inc(S("glu_ok"), 1)
                TS(lin, bank[1][:, :], LIMIT, -LIMIT, ALU.min, ALU.max).then_inc(S("h_read"), 1)
                dve.wait_ge(S("h_read"), n + 1)
                d(STT(lin, lin, 1.0, glu, AD, M))
                dve.wait_ge(S("sig_ok"), n + 1)
                TT(hidden, hidden, lin, M).then_inc(S("act_ok"), 1)

            def add_up(n):
                for c in range(KC):
                    dve.wait_ge(S("y_mm"), KC * n + c + 1)
                    TT(xT[:, c, :], xT[:, c, :], bank[6 + c % 2][:, 0:NT], AD).then_inc(S("y_add"), 1)

            def experts(base, i, first, last):
                for u in range(2):
                    n = base + 2 * i + u
                    if not (last and u == 1):
                        choose(n + 1, 2 * i + u + 1, 1 - u, isinstance(n, int) and n == 0)
                    swiglu(n)
                    if isinstance(n, int) and n == 0:
                        first_extras()
                    if not (first and u == 0):
                        add_up(n - 1)

            def moe_pass(base):
                choose(base, 0, 0, isinstance(base, int))
                list_blocks()
                experts(base, 0, True, False)
                start, off = d.n, d.off
                with dve.Fori(1, PAIRS - 1) as i:
                    d.off = off + (i - 1) * 4
                    experts(base, i, False, False)
                assert d.n - start == 4
                d.n, d.off = start + 4 * (PAIRS - 2), off
                experts(base, PAIRS - 1, False, True)
                add_up(base + E - 1)

            moe_pass(0)
            start = d.n
            with further(dve) as x:
                d.off = x * 4
                n = E + x
                e = dve.value_load(block_ints[0:1, ds(x + 1, 1)], min_val=0, max_val=E - 1)
                choose(n, e, 0, False, after=n, start=block_list[:, ds(x + (1 + XMAX), 1)])
                swiglu(n)
                add_up(n)
            assert d.n - start == 4, d.n - start
            d.sem, d.n, d.off = S("dve_chain_tail"), 0, 0
            dve.memset(small[:, 110:111], 0.0).then_inc(S("dve_stage"), once("dve_stage", "moe_done"))
            for m_ in range(KC):
                dve.wait_ge(S("sg_ev"), m_ + 1)
                d(TT(sg_T[:, m_, :], sg_T[:, m_, :], pw_T[:, m_, :], M))
                d(TT(uT[:, m_, :], xT[:, m_, :], sg_T[:, m_, :], AD))
                squares(2 * KC, uT[:, m_, :], m_)
            rms(2 * KC, GFIN, uT)
            for i, (t0, n) in enumerate(TILES):
                dve.wait_ge(S("yo_mm"), 4 + i)
                CP(yout[0:n, i, 512:1024], bank[UN_BANKS[3 + i]][0:n, :]).then_inc(S("yo_hi"), 1)


_INS = ['x_prompt', 'x_sample', 'state_hgrn', 'cache_k', 'cache_v', 'cache_logf', 'page_table', 'p_prompt', 'p_sample',
        'g_mix', 'w_in', 'hg_lb_logits', 'g_hg_out', 'fox_f_bias', 'g_fox_out', 'w_out', 'g_mlp', 'w_router',
        'b_router', 'w_up', 'b_up', 'w_down', 'b_down', 'w_ple', 'w_ple_gate', 'g_final']
_OUTS = [(1, 256, 1024), (8, 1, 1024), (1, 1, 4, 128, 128), (1, 1, 256, 8, 64), (1, 1, 256, 8, 64), (1, 1, 256, 8),
         (1, 8, 4, 128, 128), (1, 8, 1, 8, 64), (1, 8, 1, 8, 64), (1, 8, 1, 8)]


def kernel(**inputs):
    import numpy as _np
    import concourse.bacc as _bacc
    from concourse import mybir as _mybir
    from concourse.bass_utils import run_bass_kernel_spmd as _run

    nc = _bacc.Bacc("TRN2", target_bir_lowering=False, num_devices=1)
    arrays, args = {}, []
    for name in _INS:
        a = _np.ascontiguousarray(inputs[name])
        arrays[f"in_{name}_dram"] = a
        args.append(nc.dram_tensor(f"in_{name}_dram", a.shape, _mybir.dt.from_np(a.dtype), kind="ExternalInput").ap())
    for i, shape in enumerate(_OUTS):
        args.append(nc.dram_tensor(f"out_{i}_dram", shape, _mybir.dt.float32, kind="ExternalOutput").ap())
    hybrid_layer_kernel(nc, *args)
    r = _run(nc, [arrays], core_ids=[0])
    return tuple(r.results[0][f"out_{i}_dram"] for i in range(len(_OUTS)))
```
